# Optimizing a Trainium2 kernel written in Bass

```python
import math
import jax, jax.numpy as jnp
from jax import lax
import numpy as np

D_MODEL = 1024
BATCH = 1
SEQ = 256
DEPTH = 2

CHUNK = 64
Q_BLOCK = 128
ROPE_THETA = 500000.0
NORM_EPS = 1e-6
ROPE_FRACTION_DEN = 4

DSA_HEADS = 4
DSA_HEAD_DIM = 64
DSA_IDX_HEADS = 8
DSA_IDX_DIM = 64
DSA_TOPK_MAX = 256
DSA_IDX_SCALE = (DSA_IDX_HEADS * DSA_IDX_DIM) ** -0.5

DIFF_HEADS = 4
DIFF_QK_DIM = 32
DIFF_V_DIM = 2 * DIFF_QK_DIM

MLA_HEADS = 8
MLA_Q_LORA = 256
MLA_KV_LORA = 128
MLA_NOPE_DIM = 64
MLA_ROPE_DIM = 32
MLA_V_DIM = 64

D_MIX = DSA_HEADS * DSA_HEAD_DIM + DIFF_HEADS * DIFF_V_DIM + MLA_HEADS * MLA_V_DIM

IN_SPLITS = (
    DSA_HEADS * DSA_HEAD_DIM,
    DSA_HEAD_DIM,
    DSA_HEAD_DIM,
    DSA_IDX_HEADS * DSA_IDX_DIM,
    DSA_IDX_DIM,
    DSA_IDX_HEADS,
    DIFF_HEADS * 2 * DIFF_QK_DIM,
    DIFF_HEADS * 2 * DIFF_QK_DIM,
    DIFF_HEADS * DIFF_V_DIM,
    MLA_Q_LORA,
    MLA_KV_LORA,
    MLA_ROPE_DIM,
)
N_IN = sum(IN_SPLITS)

D_FF = 3584
MOE_EXPERTS = 8
MOE_TOP_K = 2
MOE_D_FF = 3584
N_DENSE = (DEPTH + 1) // 2
N_MOE = DEPTH // 2

kernel_name = 'hybrid_dsa_diff_mla_moe_block'

def rms_norm(x, g):
    xf = x.astype(jnp.float32)
    y = xf * lax.rsqrt(jnp.mean(xf * xf, axis=-1, keepdims=True) + NORM_EPS)
    return (y * g.astype(jnp.float32)).astype(x.dtype)

def rope(x, pos, rot_dim):
    half = rot_dim // 2
    inv_freq = ROPE_THETA ** (-(jnp.arange(half, dtype=jnp.float32) * 2.0 / rot_dim))
    ang = pos.astype(jnp.float32)[..., None] * inv_freq
    ang = ang.reshape(ang.shape[:2] + (1,) * (x.ndim - 3) + (half,))
    cos, sin = jnp.cos(ang), jnp.sin(ang)
    xr = x[..., :rot_dim].astype(jnp.float32)
    x1, x2 = xr[..., :half], xr[..., half:]
    rot = jnp.concatenate([x1 * cos - x2 * sin, x2 * cos + x1 * sin], axis=-1).astype(x.dtype)
    return jnp.concatenate([rot, x[..., rot_dim:]], axis=-1)

def chunk_mask(blk, s_len):
    t = blk * Q_BLOCK + jnp.arange(Q_BLOCK)
    s = jnp.arange(s_len)
    return (s[None, :] // CHUNK) <= (t[:, None] // CHUNK)

def masked_softmax(logits, mask):
    return jax.nn.softmax(jnp.where(mask, logits.astype(jnp.float32), -jnp.inf), axis=-1)

def sweep_query_blocks(fn, *q_arrays):
    b, s = q_arrays[0].shape[:2]
    nb = s // Q_BLOCK
    xs = tuple(jnp.swapaxes(a.reshape((b, nb, Q_BLOCK) + a.shape[2:]), 0, 1) for a in q_arrays)
    out = lax.map(lambda args: fn(args[0], *args[1]), (jnp.arange(nb), xs))
    return jnp.swapaxes(out, 0, 1).reshape((b, s) + out.shape[3:])

def dsa_attention(q, k, v, q_idx, k_idx, w_idx):
    s_len = k.shape[1]
    top_k = min(DSA_TOPK_MAX, s_len // 4)

    def block(blk, qb, qib, wb):
        mask = chunk_mask(blk, s_len)
        rel = jax.nn.relu(jnp.einsum('bqhd,bsd->bqhs', qib, k_idx).astype(jnp.float32))
        score = jnp.einsum('bqh,bqhs->bqs', wb.astype(jnp.float32), rel) * DSA_IDX_SCALE
        score = jnp.where(mask[None], score, -jnp.inf)
        _, idx = lax.top_k(score, top_k)
        t = blk * Q_BLOCK + jnp.arange(Q_BLOCK)
        valid = (idx // CHUNK) <= (t // CHUNK)[None, :, None]
        k_sel = jax.vmap(lambda kb, ib: kb[ib])(k, idx)
        v_sel = jax.vmap(lambda vb, ib: vb[ib])(v, idx)
        logits = jnp.einsum('bqhd,bqkd->bqhk', qb, k_sel) * DSA_HEAD_DIM ** -0.5
        p = masked_softmax(logits, valid[:, :, None, :])
        return jnp.einsum('bqhk,bqkd->bqhd', p.astype(v.dtype), v_sel)

    return sweep_query_blocks(block, q, q_idx, w_idx)

def diff_attention(q, k, v, lam, lam_init, subln):
    s_len = k.shape[1]

    def block(blk, qb):
        mask = chunk_mask(blk, s_len)
        logits = jnp.einsum('bqhcd,bshcd->bhcqs', qb, k) * DIFF_QK_DIM ** -0.5
        p = masked_softmax(logits, mask)
        a = p[:, :, 0] - lam * p[:, :, 1]
        return jnp.einsum('bhqs,bshd->bqhd', a.astype(v.dtype), v)

    o = sweep_query_blocks(block, q)
    return rms_norm(o, subln) * (1.0 - lam_init)

def mla_attention(q_nope, q_rope, k_nope, k_rope, v):
    s_len = k_nope.shape[1]
    scale = (MLA_NOPE_DIM + MLA_ROPE_DIM) ** -0.5

    def block(blk, qn, qr):
        mask = chunk_mask(blk, s_len)
        logits = (jnp.einsum('bqhd,bshd->bhqs', qn, k_nope)
                  + jnp.einsum('bqhd,bsd->bhqs', qr, k_rope)) * scale
        p = masked_softmax(logits, mask)
        return jnp.einsum('bhqs,bshd->bqhd', p.astype(v.dtype), v)

    return sweep_query_blocks(block, q_nope, q_rope)

def hybrid_mixer(h, pos, layer, w_in, q_norm, w_uq, kv_norm, w_ukv,
                 lam_q1, lam_k1, lam_q2, lam_k2, subln, w_out):
    b, s, _ = h.shape
    f32 = jnp.float32
    rf = ROPE_FRACTION_DEN
    splits = np.cumsum(IN_SPLITS)[:-1].tolist()
    (q_a, k_a, v_a, q_i, k_i, w_i, q_b, k_b, v_b, c_q, c_kv, k_r) = jnp.split(h @ w_in, splits, axis=-1)
    q_a = rope(q_a.reshape(b, s, DSA_HEADS, DSA_HEAD_DIM), pos, DSA_HEAD_DIM // rf)
    k_a = rope(k_a, pos, DSA_HEAD_DIM // rf)
    q_i = rope(q_i.reshape(b, s, DSA_IDX_HEADS, DSA_IDX_DIM), pos, DSA_IDX_DIM // rf)
    k_i = rope(k_i, pos, DSA_IDX_DIM // rf)
    o_a = dsa_attention(q_a, k_a, v_a, q_i, k_i, w_i)
    q_b = rope(q_b.reshape(b, s, DIFF_HEADS, 2, DIFF_QK_DIM), pos, DIFF_QK_DIM // rf)
    k_b = rope(k_b.reshape(b, s, DIFF_HEADS, 2, DIFF_QK_DIM), pos, DIFF_QK_DIM // rf)
    v_b = v_b.reshape(b, s, DIFF_HEADS, DIFF_V_DIM)
    lam_init = 0.8 - 0.6 * math.exp(-0.3 * layer)
    lam = (jnp.exp(jnp.sum(lam_q1.astype(f32) * lam_k1.astype(f32)))
           - jnp.exp(jnp.sum(lam_q2.astype(f32) * lam_k2.astype(f32))) + lam_init)
    o_b = diff_attention(q_b, k_b, v_b, lam, lam_init, subln)
    q_c = (rms_norm(c_q, q_norm) @ w_uq).reshape(b, s, MLA_HEADS, MLA_NOPE_DIM + MLA_ROPE_DIM)
    q_nope = q_c[..., :MLA_NOPE_DIM]
    q_rope = rope(q_c[..., MLA_NOPE_DIM:], pos, MLA_ROPE_DIM)
    kv = (rms_norm(c_kv, kv_norm) @ w_ukv).reshape(b, s, MLA_HEADS, MLA_NOPE_DIM + MLA_V_DIM)
    k_nope = kv[..., :MLA_NOPE_DIM]
    v_c = kv[..., MLA_NOPE_DIM:]
    k_rope = rope(k_r, pos, MLA_ROPE_DIM)
    o_c = mla_attention(q_nope, q_rope, k_nope, k_rope, v_c)
    o = jnp.concatenate([o_a.reshape(b, s, -1), o_b.reshape(b, s, -1), o_c.reshape(b, s, -1)], axis=-1)
    return o @ w_out

def swiglu(h, wg, wu, wd):
    return (jax.nn.silu(h @ wg) * (h @ wu)) @ wd

def moe_ffn(h, router, wg, wu, wd):
    b, s, d = h.shape
    hf = h.reshape(-1, d)
    logits = (hf @ router).astype(jnp.float32)
    top_val, top_idx = lax.top_k(logits, MOE_TOP_K)
    gates = jax.nn.softmax(top_val, axis=-1)
    combine = jnp.sum(jax.nn.one_hot(top_idx, MOE_EXPERTS, dtype=jnp.float32) * gates[..., None], axis=1)
    out = jnp.zeros_like(hf)
    for e in range(MOE_EXPERTS):
        out = out + combine[:, e:e + 1].astype(h.dtype) * swiglu(hf, wg[e], wu[e], wd[e])
    return out.reshape(b, s, d)

def setup_inputs(seed: int = 0) -> dict:
    key = jax.random.key(seed)
    ks = jax.random.split(key, 24)
    f32 = jnp.float32

    def w(k, shape, fan_in):
        return jax.random.normal(k, shape, f32) * fan_in ** -0.5

    def gain(k, shape):
        return 1.0 + 0.02 * jax.random.normal(k, shape, f32)

    x = jax.random.normal(ks[0], (BATCH, SEQ, D_MODEL), f32)
    offsets = jax.random.randint(ks[1], (BATCH,), 0, 64) * CHUNK
    positions = (offsets[:, None] + jnp.arange(SEQ)[None, :]).astype(jnp.int32)
    return {
        'x': x,
        'positions': positions,
        'attn_norm': gain(ks[2], (DEPTH, D_MODEL)),
        'w_in': w(ks[3], (DEPTH, D_MODEL, N_IN), D_MODEL),
        'mla_q_norm': gain(ks[4], (DEPTH, MLA_Q_LORA)),
        'w_uq': w(ks[5], (DEPTH, MLA_Q_LORA, MLA_HEADS * (MLA_NOPE_DIM + MLA_ROPE_DIM)), MLA_Q_LORA),
        'mla_kv_norm': gain(ks[6], (DEPTH, MLA_KV_LORA)),
        'w_ukv': w(ks[7], (DEPTH, MLA_KV_LORA, MLA_HEADS * (MLA_NOPE_DIM + MLA_V_DIM)), MLA_KV_LORA),
        'diff_lambda_q1': 0.1 * jax.random.normal(ks[8], (DEPTH, DIFF_QK_DIM), f32),
        'diff_lambda_k1': 0.1 * jax.random.normal(ks[9], (DEPTH, DIFF_QK_DIM), f32),
        'diff_lambda_q2': 0.1 * jax.random.normal(ks[10], (DEPTH, DIFF_QK_DIM), f32),
        'diff_lambda_k2': 0.1 * jax.random.normal(ks[11], (DEPTH, DIFF_QK_DIM), f32),
        'diff_subln': gain(ks[12], (DEPTH, DIFF_V_DIM)),
        'w_out': w(ks[13], (DEPTH, D_MIX, D_MODEL), D_MIX),
        'ffn_norm': gain(ks[14], (DEPTH, D_MODEL)),
        'dense_w_gate': w(ks[15], (N_DENSE, D_MODEL, D_FF), D_MODEL),
        'dense_w_up': w(ks[16], (N_DENSE, D_MODEL, D_FF), D_MODEL),
        'dense_w_down': w(ks[17], (N_DENSE, D_FF, D_MODEL), D_FF),
        'moe_router': w(ks[18], (N_MOE, D_MODEL, MOE_EXPERTS), D_MODEL),
        'moe_w_gate': w(ks[19], (N_MOE, MOE_EXPERTS, D_MODEL, MOE_D_FF), D_MODEL),
        'moe_w_up': w(ks[20], (N_MOE, MOE_EXPERTS, D_MODEL, MOE_D_FF), D_MODEL),
        'moe_w_down': w(ks[21], (N_MOE, MOE_EXPERTS, MOE_D_FF, D_MODEL), MOE_D_FF),
        'final_norm': gain(ks[22], (D_MODEL,)),
    }

def reference(x, positions, attn_norm, w_in, mla_q_norm, w_uq, mla_kv_norm, w_ukv,
              diff_lambda_q1, diff_lambda_k1, diff_lambda_q2, diff_lambda_k2, diff_subln,
              w_out, ffn_norm, dense_w_gate, dense_w_up, dense_w_down,
              moe_router, moe_w_gate, moe_w_up, moe_w_down, final_norm):
    h = x
    for layer in range(DEPTH):
        h = h + hybrid_mixer(rms_norm(h, attn_norm[layer]), positions, layer, w_in[layer],
                             mla_q_norm[layer], w_uq[layer], mla_kv_norm[layer], w_ukv[layer],
                             diff_lambda_q1[layer], diff_lambda_k1[layer],
                             diff_lambda_q2[layer], diff_lambda_k2[layer],
                             diff_subln[layer], w_out[layer])
        hn = rms_norm(h, ffn_norm[layer])
        j = layer // 2
        if layer % 2 == 0:
            h = h + swiglu(hn, dense_w_gate[j], dense_w_up[j], dense_w_down[j])
        else:
            h = h + moe_ffn(hn, moe_router[j], moe_w_gate[j], moe_w_up[j], moe_w_down[j])
    return rms_norm(h, final_norm)


_drawn_inputs = setup_inputs


def setup_inputs(seed=0):
    import zlib

    import numpy as np

    out = dict(_drawn_inputs(seed))
    spreads = {}
    factors = {'mla_q_norm': 3.957, 'final_norm': 2.826}
    for name, (base, spread) in spreads.items():
        noise = np.random.default_rng([zlib.crc32(name.encode()), seed]).standard_normal(out[name].shape)
        drawn = base * np.exp(spread * noise) if base else spread * noise
        out[name] = __import__('jax').numpy.asarray(drawn.astype(out[name].dtype))
    for name, factor in factors.items():
        out[name] = (out[name] * factor).astype(out[name].dtype)
    return out
```

```python
import math
from contextlib import ExitStack

import concourse.bass as bass
from concourse import mybir
from concourse.alu_op_type import AluOpType as ALU

F32 = mybir.dt.float32
BF16 = mybir.dt.bfloat16
I32 = mybir.dt.int32
U32 = mybir.dt.uint32
ACT = mybir.ActivationFunctionType
AX = mybir.AxisListType

P = 128
CHUNK = 64
THETA = 500000.0
EPS = 1e-6
TWO_PI = 2.0 * math.pi
PI_PARTS = (6.28125, 1.9340515136718750e-03, 1.2554228305816650e-06)
PI_PARTS = PI_PARTS + (TWO_PI - sum(PI_PARTS),)
ROUND = 1.5 * 2.0 ** 23
MASKED = -(2.0 ** 100)
TAKEN = -3.0e38

RING = 7
SLOT = 4096
ARENA = 15296
WBANKS = 4


def attention_order(n_tiles, idx_units, units):
    T = range(n_tiles)
    order = []
    for t in T:
        order += [("N1", t), ("N2", t), ("X", t, 0), ("X", t, 1), ("PC", t)]
    order += [(name, t) for name in ("PI", "PK") for t in T]
    order += [("C2", t) for t in T] + [("CT", t) for t in T] + [("PA", t) for t in T]
    order += [(name, t) for t in T for name in ("IT", "KIT")]
    order += [("U", 0), ("U", 1), ("PB", 0), ("U", 2), ("U", 3), ("PB", 1), ("U", 4), ("U", 5)]
    order += [("QC", 0, 0), ("QC", 0, 1), ("U", 6), ("U", 7), ("KV", 0, 0), ("KV", 0, 1)]
    order += [("BT", t) for t in T]
    n0, n1 = idx_units, idx_units + units
    fills = {
        n0 + 3: [(name, 0, i) for name in ("MQ", "MK") for i in range(2)],
        n0 + 4: [(name, 1, i) for name in ("QC", "KV") for i in range(2)],
        n0 + 7: [(name, 1, i) for name in ("MQ", "MK") for i in range(2)],
        n0 + 10: [("AT", t) for t in T] + [("D1", t) for t in T],
        n0 + 13: [("D2", t) for t in T],
    }
    for n in range(n0, n1 + 2):
        order += fills.get(n, [])
        if n < n1:
            order.append(("U", n))
        if n0 <= n - 1 < n1:
            order.append(("TP", n - 1))
        if n0 <= n - 2 < n1:
            order.append(("O", n - 2))
    order += [("OT", 0, 0), ("OT", 0, 1), ("WO", 0, 0), ("WO", 0, 1), ("NF1", 0), ("OT", 1, 0),
              ("OT", 1, 1), ("WO", 1, 0), ("NF2", 0), ("XF", 0, 0), ("XF", 0, 1), ("WO", 1, 1),
              ("NF1", 1), ("NF2", 1)]
    return order


def hybrid_block(nc, a, out):
    x, positions = a["x"], a["positions"]
    S, D = x.shape[1], x.shape[2]
    DEPTH, _, NIN = a["w_in"].shape
    T, KT = S // P, D // P
    HA, DA = 4, 64
    HI, DI = 8, 64
    TOPK = min(256, S // 4)
    LAM_INIT = [0.8 - 0.6 * math.exp(-0.3 * layer) for layer in range(DEPTH)]
    IDX_SCALE = (HI * DI) ** -0.5
    HB, DB = 4, 32
    HC, DN, DR, DV = 8, 64, 32, 64
    DC = DN + DR
    CQ, CKV = a["w_uq"].shape[1], a["w_ukv"].shape[1]
    NF = DR // 2
    FF = a["dense_w_gate"].shape[2]
    NCH = FF // 512
    E = a["moe_w_gate"].shape[1]
    CAP = S
    assert T == 2 and D == 1024 and FF % 512 == 0 and DEPTH == 2 and NCH * 3 % RING == 0

    widths = (HA * DA, DA, DA, HI * DI, DI, HI, HB * 2 * DB, HB * 2 * DB, HB * 2 * DB, CQ, CKV, DR)
    starts = [sum(widths[:i]) for i in range(len(widths) + 1)]
    q_a, k_a, v_a, q_i, k_i, w_i, q_b, k_b, v_b, c_q, c_kv, k_r, end = starts
    assert end == NIN
    PROJ = {"PC": (c_q, end), "PI": (q_i, k_i), "PK": (k_i, k_b), "PA": (q_a, q_i), "PB": (k_b, c_q)}

    IDXP = HI // 2
    index_units = [("idx", t, p) for t in (1, 0) for p in range(IDXP)]
    attention_units = [(kind, t, p) for kind, n in (("diff", HB), ("mla", HC // 2), ("dsa", HA // 2))
                       for t in range(T) for p in range(n)]
    UNITS = index_units + attention_units
    NU, NI = len(UNITS), len(index_units)
    ORDER = attention_order(T, NI, NU - NI)

    NOT_JOBS = ("U", "N1", "N2", "C2", "D1", "D2", "NF1", "NF2")
    JOB = {}
    for layer in range(DEPTH):
        for item in ORDER:
            if item[0] not in NOT_JOBS:
                JOB[(layer, *item)] = len(JOB)
        for half in range(2):
            JOB[(layer, "XF", 1, half)] = len(JOB)
    for t in range(T):
        JOB[("RT", t)] = len(JOB)
    JOB[("POS",)] = len(JOB)

    DENSE_STEPS = NCH * T
    USE = {}
    for layer in range(DEPTH):
        for c in PROJ:
            USE[(layer, c)] = len(USE)
        for name in ("UP", "WO0", "WO1"):
            USE[(layer, name)] = len(USE)
        if layer == 0:
            for j in range(NCH):
                for kind in "gud":
                    USE[("dense", kind, j)] = len(USE)
    MOE_USE = len(USE)
    PER_EXPERT = 3 * NCH

    ctx = ExitStack()
    with ctx:
        def sb(name, shape, dt=F32):
            return ctx.enter_context(nc.sbuf_tensor(name, shape, dt))

        def sem(name):
            return ctx.enter_context(nc.semaphore(name))

        xg = nc.dram_tensor("expert_rows", (E * CAP, D), F32, kind="Internal").ap()
        yg = nc.dram_tensor("expert_results", (E * CAP, D), F32, kind="Internal").ap()

        ring = sb("ring", [P, RING, SLOT])
        h = sb("h", [P, T, D])
        hn = sb("hn", [P, T, D])
        hnT = sb("hnT", [P, KT, S])
        gain = sb("gain", [P, D])
        arena = sb("arena", [P, ARENA])
        ident = sb("ident", [P, P])
        neg_chunk = sb("neg_chunk", [P, CHUNK])
        mask_q = sb("mask_q", [P, P], BF16)
        mask_k = sb("mask_k", [P, CHUNK], BF16)
        freq = sb("freq", [P, NF])
        cos = sb("cos", [P, T, NF])
        sin = sb("sin", [P, T, NF])
        cgain = sb("cgain", [P, CQ + CKV])
        sgain = sb("sgain", [P, 2 * DB])
        stat = sb("stat", [P, 2 * (2 * DEPTH + 1), 2])
        mhalf = sb("mhalf", [P, 4])
        cstat = sb("cstat", [P, T, 2, 2])
        dstat = sb("dstat", [P, T, 2, HB])
        lam = sb("lam", [P, DEPTH])
        nmax = sb("nmax", [P, NU, 2])
        lsum = sb("lsum", [P, NU, 2])
        rsum = sb("rsum", [P, NU, 2])
        top8 = sb("top8", [P, 8])
        wi = sb("wi", [P, T, HI])
        rope_c = sb("rope_c", [P, HC * DR])
        rope_s = sb("rope_s", [P, HC * DR])

        used = [0]

        def carve(n):
            at = used[0]
            used[0] += n
            assert used[0] <= ARENA, used[0]
            return arena[:, at:at + n]

        pa = carve(T * 448).rearrange("p (t n) -> p t n", t=T)
        both = carve(2 * HC * DC)
        pqi = both[:, 0:T * 640].rearrange("p (t n) -> p t n", t=T)
        qc = both[:, 0:HC * DC].rearrange("p (h d) -> p h d", h=HC)
        kc = both[:, HC * DC:2 * HC * DC].rearrange("p (h d) -> p h d", h=HC)
        pb = carve(T * 768).rearrange("p (t n) -> p t n", t=T)
        pc = carve(T * 416).rearrange("p (t n) -> p t n", t=T)
        vc = carve(T * HC * DV).rearrange("p (t n) -> p t n", t=T)
        cT = carve(3 * S).rearrange("p (k s) -> p k s", k=3)
        bT = carve(4 * S).rearrange("p (k s) -> p k s", k=4)
        aT = carve(3 * S).rearrange("p (k s) -> p k s", k=3)
        kiT = carve(S)
        qiT_or_pt = carve(4 * S)
        qiT = qiT_or_pt.rearrange("p (k s) -> p k s", k=4)
        pt = qiT_or_pt.rearrange("p (b k s) -> p b k s", b=2, k=4)
        qcT = carve(HC * S).rearrange("p (k s) -> p k s", k=HC)
        kcT = carve(HC * S).rearrange("p (k s) -> p k s", k=HC)
        prob = carve(2 * 2 * S).rearrange("p (b m s) -> p b m s", b=2, m=2)
        score = carve(T * S).rearrange("p (t s) -> p t s", t=T)
        lamv = qcT[:, 0, :].rearrange("p (l v d) -> p l v d", l=DEPTH, v=4)
        lamp = qcT[:, 1, 0:DEPTH * 2 * DB].rearrange("p (l v d) -> p l v d", l=DEPTH, v=2)
        lams = qcT[:, 2, 0:2 * DEPTH].rearrange("p (l v) -> p l v", l=DEPTH)
        lame = qcT[:, 2, 64:64 + 2 * DEPTH].rearrange("p (l v) -> p l v", l=DEPTH)
        pos_i = qcT[:, 3, 0:T].bitcast(I32)
        pos_f = qcT[:, 3, 64:64 + T]
        ang = qcT[:, 4, 0:T * NF].rearrange("p (t f) -> p t f", t=T)
        turns = qcT[:, 5, 0:T * NF].rearrange("p (t f) -> p t f", t=T)
        angc = qcT[:, 6, 0:T * NF].rearrange("p (t f) -> p t f", t=T)
        zeros = kcT.rearrange("p k s -> p (k s)")[:, 0:D]
        used[0] = 0
        sig = carve(512)
        rec = carve(512)
        sg = carve(512)
        hid = carve(512)
        hidT = carve(4 * P).rearrange("p (k s) -> p k s", k=4)
        xrow = carve(D)
        xT = carve(D).rearrange("p (k s) -> p k s", k=KT)
        yrow = carve(D)
        back = carve(4 * D).rearrange("p (n d) -> p n d", n=4)
        router = carve(KT * E).rearrange("p (k e) -> p k e", k=KT)
        before = carve(P)
        ones = carve(P)
        lg = carve(T * E).rearrange("p (t e) -> p t e", t=T)
        lg2 = carve(T * E).rearrange("p (t e) -> p t e", t=T)
        eq = carve(T * E).rearrange("p (t e) -> p t e", t=T)
        pick = [carve(T * E).rearrange("p (t e) -> p t e", t=T) for _ in range(2)]
        chosen = carve(T * E).rearrange("p (t e) -> p t e", t=T)
        rank = carve(3 * E).rearrange("p (t e) -> p t e", t=3)
        falling = carve(E)
        base = carve(E)
        best = carve(2 * T).rearrange("p (k t) -> p k t", k=2)
        first = carve(2 * T).rearrange("p (k t) -> p k t", k=2)
        gate = carve(2 * T).rearrange("p (k t) -> p k t", k=2)
        dest_f = carve(2 * T).rearrange("p (k t) -> p k t", k=2)
        dest = carve(2 * T).bitcast(U32).rearrange("p (k t) -> p k t", k=2)
        most = carve(1)
        flag = carve(1).bitcast(I32)

        pair = [ctx.enter_context(nc.psum_tensor(f"pair{i}", [P, 2, 512], F32)) for i in range(2)]
        work = [ctx.enter_context(nc.psum_tensor(f"work{i}", [P, 512], F32)) for i in range(WBANKS)]
        gate_bank, up_bank, tr_bank = pair[0][:, 0, :], pair[0][:, 1, :], pair[1][:, 0, :]
        free_late = (JOB[(1, "X", 0, 0)] + 3) % WBANKS
        down_bank = (pair[1][:, 1, :], work[free_late][:, :])
        x_bank = [work[(free_late + 1 + i) % WBANKS][:, :] for i in range(2)]

        loaded_x = [sem(f"loaded_x{t}") for t in range(T)]
        loaded_ukv = sem("loaded_ukv")
        loaded_small = sem("loaded_small")
        loaded_gain = sem("loaded_gain")
        loaded_cgain = sem("loaded_cgain")
        loaded_router = sem("loaded_router")
        slot_full = [sem(f"slot_full{i}") for i in range(RING)]
        consts_ready = sem("consts_ready")
        pool_chain = sem("pool_chain")
        dve_chain = sem("dve_chain")
        angles_ready = sem("angles_ready")
        trig_ready = sem("trig_ready")
        lam_sums = sem("lam_sums")
        lam_exp = sem("lam_exp")
        lam_ready = sem("lam_ready")
        residual_ready = sem("residual_ready")
        squares_ready = sem("squares_ready")
        mean_ready = sem("mean_ready")
        rms_ready = sem("rms_ready")
        normed = sem("normed")
        job_done = sem("job_done")
        evacuated = [sem(f"evacuated{i}") for i in range(WBANKS)]
        c_squares = sem("c_squares")
        c_mean = sem("c_mean")
        c_rms = sem("c_rms")
        c_normed = sem("c_normed")
        roped = sem("roped")
        logits_ready = sem("logits_ready")
        relu_done = sem("relu_done")
        index_added = sem("index_added")
        max_ready = sem("max_ready")
        exp_done = sem("exp_done")
        combined = sem("combined")
        d_mean = sem("d_mean")
        d_rms = sem("d_rms")
        d_normed = sem("d_normed")
        gate_done, up_done, tr_done, down_done, sig_ready, den_ready, rec_ready, sg_ready, hid_ready, \
            hidT_ready, xrow_full, xt_done, xT_ready, y_ready, y_stored = (
                [sem(f"{n}{half}") for half in range(2)] for n in (
                    "gate_done", "up_done", "tr_done", "down_done", "sig_ready", "den_ready",
                    "rec_ready", "sg_ready", "hid_ready", "hidT_ready", "xrow_full", "xt_done",
                    "xT_ready", "y_ready", "y_stored"))
        dense_added = sem("dense_added")
        zeroed = sem("zeroed")
        zeroed_more = sem("zeroed_more")
        routed = sem("routed")
        chosen_ready = sem("chosen_ready")
        scattered = sem("scattered")
        gathered = [sem(f"gathered{t}") for t in range(T)]
        gates_in = sem("gates_in")
        gates_exp = sem("gates_exp")
        more_zeroed = sem("more_zeroed")
        out_ready = sem("out_ready")
        stored = sem("stored")

        def job(eng, key):
            eng.wait_ge(job_done, JOB[key] + 1)
            return work[JOB[key] % WBANKS]

        def emptied(eng, key):
            eng.wait_ge(evacuated[JOB[key] % WBANKS], JOB[key] // WBANKS + 1)

        def out_of(key):
            return evacuated[JOB[key] % WBANKS]

        def slot(use):
            return ring[:, use % RING, :]

        def arrived(eng, use, rounds=0):
            eng.wait_ge(slot_full[use % RING], rounds + 16 * (use // RING + 1))

        def first_step(half):
            return DENSE_STEPS if half == 0 else 0

        def bc(ap, shape):
            for _ in range(len(shape) - len(ap.shape)):
                ap = ap.unsqueeze(1)
            return ap.to_broadcast(shape)

        def keys(t):
            return P * (t + 1)

        EXPS = {n: i + 1 for i, n in enumerate(range(NI, NU))}
        NE = NU - NI
        DIFFS = [n for n in range(NU) if UNITS[n][0] == "diff"]
        ROPES = [("kr", 0), ("kr", 1), ("i", 0), ("i", 1), ("a", 0), ("a", 1), ("b", 0), ("b", 1),
                 ("c", 0), ("c", 1)]

        def roped_by(eng, layer, key):
            eng.wait_ge(roped, layer * len(ROPES) + ROPES.index(key) + 1)

        NORMS = [("attn", 0), ("ffn", 0), ("attn", 1), ("ffn", 1), ("final", 1)]

        def norm_count(which, t):
            return NORMS.index(which) * T + t + 1

        FREE = {}
        for layer in range(DEPTH):
            for c in PROJ:
                FREE[USE[(layer, c)]] = (job_done, JOB[(layer, c, T - 1)] + 1)
            FREE[USE[(layer, "UP")]] = (job_done, JOB[(layer, "KV", 1, 1)] + 1)
            for half in range(2):
                FREE[USE[(layer, f"WO{half}")]] = (job_done, JOB[(layer, "WO", T - 1, half)] + 1)
        for j in range(NCH):
            FREE[USE[("dense", "g", j)]] = (gate_done[0], T * j + T)
            FREE[USE[("dense", "u", j)]] = (up_done[0], T * j + T)
            FREE[USE[("dense", "d", j)]] = (down_done[0], 2 * (T * j + T))

        block = ctx.enter_context(nc.Block())

        @block.sync
        def _(sp):
            wg, wu, wd = a["moe_w_gate"], a["moe_w_up"], a["moe_w_down"]

            def column_chunk(w, c0, c1):
                return w[:, c0:c1].rearrange("(k p) n -> p k n", p=P)

            def load(use, view, src, rounds=0):
                sp.dma_start(view, src).then_inc(slot_full[use % RING], 16)

            def freed(use):
                if use in FREE:
                    sp.wait_ge(*FREE[use])

            def wide(use, n, k=KT):
                return slot(use)[:, 0:k * n].rearrange("p (k n) -> p k n", k=k)

            for t in range(T):
                sp.dma_start(h[:, t, :], x[0, t * P:(t + 1) * P, :]).then_inc(loaded_x[t], 16)
            for layer in range(DEPTH):
                for c, (c0, c1) in PROJ.items():
                    use = USE[(layer, c)]
                    freed(use - RING)
                    load(use, wide(use, c1 - c0), column_chunk(a["w_in"][layer], c0, c1))
                use = USE[(layer, "UP")]
                freed(use - RING)
                nq, nkv = HC * DC, HC * (DN + DV)
                sp.dma_start(slot(use)[:, 0:2 * nq].rearrange("p (k n) -> p k n", k=2),
                             a["w_uq"][layer].rearrange("(k p) n -> p k n", p=P)) \
                    .then_inc(slot_full[use % RING], 16)
                sp.dma_start(slot(use)[:, 2 * nq:2 * nq + nkv], a["w_ukv"][layer]) \
                    .then_inc(loaded_ukv, 16)
                for half in range(2):
                    use = USE[(layer, f"WO{half}")]
                    freed(use - RING)
                    load(use, wide(use, 512), column_chunk(a["w_out"][layer], 512 * half, 512 * half + 512))
                if layer == 0:
                    for j in range(NCH):
                        for kind, w in (("g", a["dense_w_gate"][0]), ("u", a["dense_w_up"][0])):
                            use = USE[("dense", kind, j)]
                            freed(use - RING)
                            load(use, wide(use, 512), column_chunk(w, 512 * j, 512 * j + 512))
                        use = USE[("dense", "d", j)]
                        freed(use - RING)
                        load(use, wide(use, D, 4),
                             a["dense_w_down"][0][512 * j:512 * j + 512, :]
                             .rearrange("(k p) n -> p k n", p=P))

            def chunk_at(e, k):
                e, k = e + k // PER_EXPERT, k % PER_EXPERT
                j, kind = k // 3 + 1, k % 3
                if kind == 2:
                    return e, j - 1, 2
                return (e, j, kind) if j < NCH else (e + 1, 0, kind)

            def load_chunk(use, e, j, kind):
                w = (wg, wu, wd)[kind]
                w = w[0, e] if isinstance(e, int) else w[0][bass.ds(e, 1)].rearrange("a k n -> (a k) n")
                if kind < 2:
                    load(use, wide(use, 512), column_chunk(w, 512 * j, 512 * j + 512))
                else:
                    load(use, wide(use, D, 4),
                         w[512 * j:512 * j + 512, :].rearrange("(k p) n -> p k n", p=P))

            def chunk_freed(half, e, j, kind):
                step = first_step(half) + NCH * e + j
                if kind == 2:
                    sp.wait_ge(down_done[half], 2 * (step + 1))
                else:
                    sp.wait_ge((gate_done, up_done)[kind][half], step + 1)

            def expert_weights(half):
                first = MOE_USE + half * E * PER_EXPERT
                for i in range(RING + 2):
                    if i >= RING:
                        chunk_freed(half, 0, 0, i - RING)
                    elif half == 0:
                        freed(first + i - RING)
                    load_chunk(first + i, *((0, 0, i) if i < 2 else chunk_at(0, i - 2)))
                with sp.Fori(0, E - 1) as e:
                    for k in range(PER_EXPERT):
                        chunk_freed(half, *chunk_at(e, k))
                        load_chunk(first + 2 + k + RING, *chunk_at(e, k + RING))
                last = (E - 1) * PER_EXPERT
                for k in range(last + RING, last + PER_EXPERT - 2):
                    chunk_freed(half, *chunk_at(0, k - RING))
                    load_chunk(first + 2 + k, *((E - 1, NCH - 1, 2) if k % PER_EXPERT == 3 * NCH - 3
                                                else chunk_at(0, k)))

            expert_weights(0)
            sp.wait_ge(routed, 1)
            more = sp.value_load(flag[0:1, 0:1])
            with sp.If(more > 0):
                sp.wait_ge(down_done[0], 2 * (first_step(0) + NCH * E))
                expert_weights(1)
            for t in range(T):
                sp.wait_ge(out_ready, t + 1)
                sp.dma_start(out[0, t * P:(t + 1) * P, :], hn[:, t, :]).then_inc(stored, 16)
            sp.wait_ge(stored, 16 * T)

        @block.gpsimd
        def _(pool):
            chained = [0]

            def link(ins):
                chained[0] += 1
                ins.then_inc(pool_chain, 1)
                pool.wait_ge(pool_chain, chained[0])

            pool.memset(zeros, 0.0).then_inc(consts_ready, 1)
            link(pool.memset(ident[:, :], 0.0))
            link(pool.affine_select(out=ident[:, :], in_=ident[:, :], compare_op=ALU.not_equal, fill=1.0,
                                    base=0, pattern=[[-1, P]], channel_multiplier=1))
            pool.memset(mhalf[:, :], -0.5)
            pool.memset(mask_q[:, 0:CHUNK], 1.0)
            pool.memset(mask_q[:, CHUNK:P], 0.0)
            pool.memset(mask_k[:, :], MASKED)
            link(pool.memset(neg_chunk[:, :], 0.0))
            pool.memset(neg_chunk[0:CHUNK, :], MASKED).then_inc(consts_ready, 1)
            pool.wait_ge(consts_ready, 2)

            def inverse_root(outp, inp, n):
                return pool.tensor_tensor(outp, inp, mhalf[:, 0:n], ALU.pow)

            def norm_root(which, t):
                i = norm_count(which, t)
                pool.wait_ge(mean_ready, i)
                inverse_root(stat[:, i - 1, 0:1], stat[:, i - 1, 1:2], 1).then_inc(rms_ready, 1)

            def rope(v, t, n, half):
                shape = [P, n, 2, half]
                step = NF // half
                c, s = (bc(z[:, t, :].rearrange("p (f s) -> p f s", s=step)[:, :, 0], shape) for z in (cos, sin))
                rc = rope_c[:, 0:2 * n * half].rearrange("p (n a f) -> p n a f", n=n, a=2)
                rs = rope_s[:, 0:2 * n * half].rearrange("p (n a f) -> p n a f", n=n, a=2)
                link(pool.tensor_tensor(rc, v, c, ALU.mult))
                link(pool.tensor_tensor(rs, v, s, ALU.mult))
                link(pool.tensor_tensor(v[:, :, 0, :], rc[:, :, 0, :], rs[:, :, 1, :], ALU.subtract))
                return pool.tensor_tensor(v[:, :, 1, :], rc[:, :, 1, :], rs[:, :, 0, :], ALU.add)

            def halves(v, n, d, half):
                return v.rearrange("p (n d) -> p n d", n=n)[:, :, 0:2 * half] \
                        .rearrange("p n (a f) -> p n a f", a=2)

            rotations = [0]

            def rotated(ins):
                rotations[0] += 1
                ins.then_inc(roped, 1)
                pool.wait_ge(roped, rotations[0])

            for layer in range(DEPTH):
                for t in range(T):
                    norm_root(("attn", layer), t)
                for t in range(T):
                    pool.wait_ge(c_mean, layer * T + t + 1)
                    inverse_root(cstat[:, t, 0, :], cstat[:, t, 1, :], 2).then_inc(c_rms, 1)
                if layer == 0:
                    pool.wait_ge(trig_ready, 2)
                for t in range(T):
                    emptied(pool, (layer, "PC", t))
                    rotated(rope(halves(pc[:, t, CQ + CKV:], 1, DR, DR // 2), t, 1, DR // 2))
                for t in range(T):
                    emptied(pool, (layer, "PI", t))
                    emptied(pool, (layer, "PK", t))
                    link(rope(halves(pqi[:, t, 0:(HI + 1) * DI], HI + 1, DI, DI // 8), t, HI + 1, DI // 8))
                    rotated(pool.tensor_copy(pqi[:, t, (HI + 1) * DI:], pqi[:, t, HI * DI:(HI + 1) * DI]))
                for t in range(T):
                    emptied(pool, (layer, "PA", t))
                    link(rope(halves(pa[:, t, 0:(HA + 1) * DA], HA + 1, DA, DA // 8), t, HA + 1, DA // 8))
                    rotated(pool.tensor_copy(pa[:, t, (HA + 1) * DA:(HA + 2) * DA],
                                             pa[:, t, HA * DA:(HA + 1) * DA]))
                for t in range(T):
                    emptied(pool, (layer, "PK", t))
                    emptied(pool, (layer, "PB", t))
                    rotated(rope(halves(pb[:, t, 0:4 * HB * DB], 4 * HB, DB, DB // 8), t, 4 * HB, DB // 8))
                for t in range(T):
                    for i in range(2):
                        emptied(pool, (layer, "QC", t, i))
                    link(rope(qc[:, :, DN:].rearrange("p n (a f) -> p n a f", a=2), t, HC, DR // 2))
                    for i in range(2):
                        emptied(pool, (layer, "KV", t, i))
                    rotated(pool.tensor_copy(kc[:, :, DN:], bc(pc[:, t, CQ + CKV:], [P, HC, DR])))
                for t in range(T):
                    pool.wait_ge(d_mean, layer * T + t + 1)
                    inverse_root(dstat[:, t, 0, :], dstat[:, t, 1, :], HB).then_inc(d_rms, 1)
                for t in range(T):
                    norm_root(("ffn", layer), t)

            pool.wait_ge(normed, norm_count(("ffn", 1), 0))
            link(pool.memset(before[:, :], 1.0))
            link(pool.affine_select(out=before[:, :], in_=before[:, :], compare_op=ALU.is_gt, fill=0.0,
                               base=0, pattern=[[1, P]], channel_multiplier=-1))
            pool.memset(ones[:, :], 1.0)
            pool.iota(falling, [[-1, E]], base=E, channel_multiplier=0,
                      allow_small_or_imprecise_dtypes=True)
            pool.iota(base, [[P, E]], base=0, channel_multiplier=0,
                      allow_small_or_imprecise_dtypes=True).then_inc(consts_ready, 1)
            pool.wait_ge(routed, 1)
            more = pool.value_load(flag[0:1, 0:1])
            rows = xg.rearrange("(s e p) d -> s p e d", e=E, p=P)
            with pool.If(more > 0):
                pool.memset(back[:, 0, :], 0.0).then_inc(zeroed_more, 1)
                pool.wait_ge(zeroed_more, 1)
                for e in range(E):
                    pool.dma_start(rows[1, :, e, :], back[:, 0, :]).then_inc(more_zeroed, 16)
                pool.wait_ge(more_zeroed, 16 * E)
            pool.wait_ge(zeroed, 16)
            for k in range(2):
                for t in range(T):
                    pool.indirect_dma_start(
                        out=xg, out_offset=bass.IndirectOffsetOnAxis(ap=dest[:, k, t:t + 1], axis=0),
                        in_=hn[:, t, :], in_offset=None).then_inc(scattered, 16)
            def gather(table):
                for t in range(T):
                    for k in range(2):
                        pool.indirect_dma_start(
                            out=back[:, 2 * t + k, :], out_offset=None, in_=table,
                            in_offset=bass.IndirectOffsetOnAxis(ap=dest[:, k, t:t + 1], axis=0)) \
                            .then_inc(gathered[t], 16)

            pool.wait_ge(y_stored[0], 16 * E)
            with pool.If(more > 0):
                pool.wait_ge(y_stored[1], 16 * E)
                gather(yg)
            with pool.Else():
                gather(yg[0:E * P, :])
            for t in range(T):
                norm_root(("final", 1), t)

        @block.tensor
        def _(pe):
            def begin(key):
                n = JOB[key]
                if n >= WBANKS:
                    pe.wait_ge(evacuated[n % WBANKS], n // WBANKS)
                if n % WBANKS == free_late and JOB[(1, "X", 0, 0)] <= n < JOB[(1, "X", 0, 0)] + WBANKS:
                    pe.wait_ge(dense_added, 2 * DENSE_STEPS)
                return work[n % WBANKS]

            def transposes(b, blocks, n=P):
                for i, src in enumerate(blocks):
                    last = pe.transpose(b[0:n, i * P:(i + 1) * P], src, ident[:, :])
                return last

            def tile(t):
                return slice(t * P, (t + 1) * P)

            def cols(src, t, i0, n):
                return [src[:, t, (i0 + i) * P:(i0 + i + 1) * P] for i in range(n)]

            def product(b, n, lhs, rhs):
                for k in range(len(rhs)):
                    last = pe.matmul(b[:, 0:n], lhs[k], rhs[k], start=(k == 0), stop=(k == len(rhs) - 1))
                return last

            def wide(use, n):
                v = slot(use)[:, 0:KT * n].rearrange("p (k n) -> p k n", k=KT)
                return [v[:, k, :] for k in range(KT)]

            def transpose_rows(layer, item):
                name, t, i = item
                b = begin((layer, *item))
                if name == "OT":
                    last_o = max(n for n in range(NI, NU) if UNITS[n][1] == t)
                    emptied(pe, (layer, "O", last_o))
                    pe.wait_ge(d_normed, layer * T + t + 1)
                else:
                    pe.wait_ge(normed, norm_count(("attn" if name == "X" else "ffn", layer), t))
                transposes(b, cols(hn, t, 4 * i, 4)).then_inc(job_done, 1)

            def logits(layer, n):
                kind, t, p = UNITS[n]
                S2 = pair[n % 2]
                nk = keys(t)
                if n >= 2:
                    if n - 2 < NI:
                        pe.wait_ge(relu_done, layer * NI + n - 1)
                    else:
                        pe.wait_ge(exp_done, layer * NE + EXPS[n - 2])
                if (kind, p) in (("idx", 0), ("diff", 0), ("mla", 0), ("dsa", 0)):
                    for name in {"idx": ("IT", "KIT"), "diff": ("BT",), "dsa": ("AT",), "mla": ("MQ", "MK")}[kind]:
                        for tt in range(t + 1):
                            for i in (range(2) if kind == "mla" else (None,)):
                                emptied(pe, (layer, name, tt) if i is None else (layer, name, tt, i))
                for m in range(2):
                    if kind == "idx":
                        q, k, r = qiT[64 * m:64 * m + 64, p, tile(t)], kiT[64 * m:64 * m + 64, 0:nk], 0
                    elif kind == "diff":
                        blk, r = (2 * p + m) // 4, 32 * ((2 * p + m) % 4)
                        q, k = bT[r:r + DB, blk, tile(t)], bT[r:r + DB, 2 + blk, 0:nk]
                    elif kind == "mla":
                        q, k, r = qcT[0:DC, 2 * p + m, tile(t)], kcT[0:DC, 2 * p + m, 0:nk], 0
                    else:
                        q, k, r = aT[64 * m:64 * m + 64, p, tile(t)], aT[64 * m:64 * m + 64, 2, 0:nk], 0
                    plain = kind in ("idx", "dsa")
                    last = pe.matmul(S2[:, m, 0:nk], q, k, start=True, stop=plain)
                    if not plain:
                        last = pe.matmul(S2[:, m, nk - CHUNK:nk], mask_q[r:r + 1, :], mask_k[r:r + 1, :],
                                         start=False, stop=True)
                last.then_inc(logits_ready, 1)

            def attention(layer):
                for item in ORDER:
                    name, key = item[0], (layer, *item)
                    if name in ("X", "XF", "OT"):
                        transpose_rows(layer, item)
                    elif name in PROJ:
                        t, use = item[1], USE[(layer, name)]
                        b = begin(key)
                        n = PROJ[name][1] - PROJ[name][0]
                        arrived(pe, use)
                        for i in range(2):
                            emptied(pe, (layer, "X", t, i))
                        product(b, n, [hnT[:, k, tile(t)] for k in range(KT)], wide(use, n)) \
                            .then_inc(job_done, 1)
                    elif name == "CT":
                        b = begin(key)
                        pe.wait_ge(c_normed, layer * T + item[1] + 1)
                        transposes(b, cols(pc, item[1], 0, 3)).then_inc(job_done, 1)
                    elif name in ("IT", "KIT", "AT", "BT"):
                        t = item[1]
                        b = begin(key)
                        roped_by(pe, layer, ({"IT": "i", "KIT": "i", "AT": "a", "BT": "b"}[name], t))
                        src, i0, n = {"IT": (pqi, 0, 4), "KIT": (pqi, 4, 1), "AT": (pa, 0, 3), "BT": (pb, 0, 4)}[name]
                        transposes(b, cols(src, t, i0, n)).then_inc(job_done, 1)
                    elif name == "QC":
                        _, t, i = item
                        b, use, n = begin(key), USE[(layer, "UP")], HC * DC // 2
                        arrived(pe, use)
                        emptied(pe, (layer, "CT", t))
                        product(b, n, [cT[:, k, tile(t)] for k in range(2)],
                                [slot(use)[:, k * 2 * n + i * n:k * 2 * n + i * n + n] for k in range(2)]) \
                            .then_inc(job_done, 1)
                    elif name == "KV":
                        _, t, i = item
                        b, at = begin(key), 2 * HC * DC + 512 * i
                        pe.wait_ge(loaded_ukv, 16 * (layer + 1))
                        product(b, 512, [cT[:, 2, tile(t)]], [slot(USE[(layer, "UP")])[:, at:at + 512]]) \
                            .then_inc(job_done, 1)
                    elif name in ("MQ", "MK"):
                        _, t, i = item
                        b = begin(key)
                        roped_by(pe, layer, ("c", t))
                        src = qc if name == "MQ" else kc
                        transposes(b, [src[:, 4 * i + j, :] for j in range(4)], DC).then_inc(job_done, 1)
                    elif name == "U":
                        logits(layer, item[1])
                    elif name == "TP":
                        n = item[1]
                        kind, t, p = UNITS[n]
                        b = begin(key)
                        if kind == "diff":
                            pe.wait_ge(combined, layer * len(DIFFS) + DIFFS.index(n) + 1)
                        else:
                            pe.wait_ge(exp_done, layer * NE + EXPS[n])
                        transposes(b, [prob[:, n % 2, m, tile(kb)] for m in range(1 if kind == "diff" else 2)
                                       for kb in range(t + 1)]).then_inc(job_done, 1)
                    elif name == "O":
                        n = item[1]
                        kind, t, p = UNITS[n]
                        b = begin(key)
                        emptied(pe, (layer, "TP", n))
                        for m in range(1 if kind == "diff" else 2):
                            for kb in range(t + 1):
                                v = {"diff": pb[:, kb, 512 + 64 * p:576 + 64 * p],
                                     "mla": vc[:, kb, DV * (2 * p + m):DV * (2 * p + m + 1)],
                                     "dsa": pa[:, kb, 384:448]}[kind]
                                last = pe.matmul(b[:, 64 * m:64 * m + 64], pt[:, n % 2, m * (t + 1) + kb, :],
                                                 v, start=(kb == 0), stop=(kb == t))
                        last.then_inc(job_done, 1)
                    elif name == "WO":
                        _, t, half = item
                        b, use = begin(key), USE[(layer, f"WO{half}")]
                        arrived(pe, use)
                        for i in range(2):
                            emptied(pe, (layer, "OT", t, i))
                        product(b, 512, [hnT[:, k, tile(t)] for k in range(KT)], wide(use, 512)) \
                            .then_inc(job_done, 1)

            def columns(which, half, step, use, rounds, lhs):
                b, done, empty = ((gate_bank, gate_done, sg_ready), (up_bank, up_done, hid_ready))[which]
                if not (isinstance(step, int) and step == 0):
                    pe.wait_ge(empty[half], step)
                arrived(pe, use, rounds)
                product(b, 512, lhs, wide(use, 512)).then_inc(done[half], 1)

            def turn(half, step):
                pe.wait_ge(hid_ready[half], step + 1)
                transposes(tr_bank, [hid[:, k * P:(k + 1) * P] for k in range(4)]) \
                    .then_inc(tr_done[half], 1)

            def down(half, step, use, rounds, first, last, added=None):
                pe.wait_ge(hidT_ready[half], step + 1)
                arrived(pe, use, rounds)
                w = slot(use)[:, 0:4 * D].rearrange("p (k n) -> p k n", k=4)
                for c in range(2):
                    if added is not None and added > 0:
                        pe.wait_ge(dense_added, 2 * (added - 1) + c + 1)
                    for k in range(4):
                        mm = pe.matmul(down_bank[c], hidT[:, k, :], w[:, k, 512 * c:512 * c + 512],
                                       start=(first and k == 0), stop=(last and k == 3))
                    mm.then_inc(down_done[half], 1)

            def dense():
                lhs = [[hnT[:, k, tile(t)] for k in range(KT)] for t in range(T)]
                for s in range(DENSE_STEPS + 1):
                    j, t = s // T, s % T
                    if s < DENSE_STEPS:
                        if t < T and s < T:
                            for i in range(2):
                                emptied(pe, (0, "XF", t, i))
                        columns(0, 0, s, USE[("dense", "g", j)], 0, lhs[t])
                    if s:
                        turn(0, s - 1)
                    if s < DENSE_STEPS:
                        columns(1, 0, s, USE[("dense", "u", j)], 0, lhs[t])
                    if s == 0:
                        for i in range(2):
                            transpose_rows(0, ("XF", 1, i))
                    if s:
                        down(0, s - 1, USE[("dense", "d", (s - 1) // T)], 0, True, True, s - 1)

            def experts(half):
                s0, use0 = first_step(half), MOE_USE + half * E * PER_EXPERT
                lhs = [xT[:, k, :] for k in range(KT)]

                def rows_turned(n):
                    pe.wait_ge(xrow_full[half], 16 * n)
                    for i in range(2):
                        last = transposes(x_bank[i], [xrow[:, (4 * i + k) * P:(4 * i + k + 1) * P] for k in range(4)])
                    last.then_inc(xt_done[half], 1)

                def expert(e, last):
                    rounds = 0 if last else 16 * (PER_EXPERT // RING) * e
                    at = use0 + 2 + (e * PER_EXPERT if last else 0)
                    for j in range(1, NCH + 1):
                        step = e * NCH + (s0 + j)
                        ahead = j < NCH or not last
                        if j == NCH and not last:
                            pe.wait_ge(xT_ready[half], e * 2 + 4)
                        if ahead:
                            columns(0, half, step, at + 3 * j - 3, rounds, lhs)
                        turn(half, step - 1)
                        if ahead:
                            columns(1, half, step, at + 3 * j - 2, rounds, lhs)
                        if j == 3 and not last:
                            rows_turned(e + 2)
                        down(half, step - 1, at + 3 * j - (1 if ahead else 3), rounds, j == 1, j == NCH)

                rows_turned(1)
                pe.wait_ge(xT_ready[half], 2)
                columns(0, half, s0, use0, 0, lhs)
                columns(1, half, s0, use0 + 1, 0, lhs)
                with pe.Fori(0, E - 1) as e:
                    expert(e, False)
                expert(E - 1, True)

            pe.wait_ge(consts_ready, 2)
            attention(0)
            dense()
            attention(1)
            for i in range(2):
                transpose_rows(1, ("XF", 1, i))
            pe.wait_ge(loaded_router, 16)
            for t in range(T):
                b = begin(("RT", t))
                for i in range(2):
                    emptied(pe, (1, "XF", t, i))
                product(b, E, [hnT[:, k, tile(t)] for k in range(KT)], [router[:, k, :] for k in range(KT)]) \
                    .then_inc(job_done, 1)
            b = begin(("POS",))
            pe.wait_ge(consts_ready, 3)
            pe.wait_ge(chosen_ready, 1)
            pe.matmul(b[:, 0:E], before[:, :], chosen[:, 0, :], start=True, stop=True)
            pe.matmul(b[:, E:2 * E], ones[:, :], chosen[:, 0, :], start=True, stop=False)
            pe.matmul(b[:, E:2 * E], before[:, :], chosen[:, 1, :], start=False, stop=True)
            pe.matmul(b[:, 2 * E:3 * E], ones[:, :], chosen[:, 0, :], start=True, stop=False)
            pe.matmul(b[:, 2 * E:3 * E], ones[:, :], chosen[:, 1, :], start=False, stop=True) \
                .then_inc(job_done, 1)
            experts(0)
            more = pe.value_load(flag[0:1, 0:1])
            with pe.If(more > 0):
                experts(1)

        @block.scalar
        def _(act):
            def copy(o, i):
                return act.activation(o, i, ACT.Copy)

            def row(v, n):
                return v.rearrange("(a n) -> a n", a=1).to_broadcast([P, n])

            def load_gain(v):
                act.dma_start(gain[:, :], row(v, D)).then_inc(loaded_gain, 16)

            def load_layer_gains(layer):
                act.dma_start(cgain[:, 0:CQ], row(a["mla_q_norm"][layer], CQ)).then_inc(loaded_cgain, 16)
                act.dma_start(cgain[:, CQ:], row(a["mla_kv_norm"][layer], CKV)).then_inc(loaded_cgain, 16)
                act.dma_start(sgain[:, :], row(a["diff_subln"][layer], 2 * DB)).then_inc(loaded_cgain, 16)

            def squares(which, t):
                if which == ("attn", 0):
                    act.wait_ge(loaded_x[t], 16)
                else:
                    act.wait_ge(residual_ready, norm_count(which, t) - T)
                act.activation(hn[:, t, :], h[:, t, :], ACT.Square,
                               accum_out=stat[:, norm_count(which, t) - 1, 0:1]).then_inc(squares_ready, 1)

            def turn_evac(key, item):
                b = job(act, key)
                _, t, i = item
                copy(hnT[:, 4 * i:4 * i + 4, t * P:(t + 1) * P], b[:, :].rearrange("p (k s) -> p k s", k=4)) \
                    .then_inc(out_of(key), 1)

            load_gain(a["attn_norm"][0])
            with nc.allow_non_contiguous_dma(reason="the positions, one to a partition"):
                act.dma_start(pos_i, positions.rearrange("a (t p) -> p (a t)", p=P)).then_inc(loaded_small, 16)
            act.dma_start(freq[:, :], row(a["rope_freq"], NF)).then_inc(loaded_small, 16)
            for i, name in enumerate(("q1", "k1", "q2", "k2")):
                v = a[f"diff_lambda_{name}"]
                act.dma_start(lamv[:, :, i, :], v.unsqueeze(0).to_broadcast([P, DEPTH, DB])).then_inc(loaded_small, 16)
            load_layer_gains(0)
            act.wait_ge(consts_ready, 1)
            act.dma_start(xg[0:E * P, :].rearrange("(e p) d -> p e d", p=P),
                          zeros.unsqueeze(1).to_broadcast([P, E, D])).then_inc(zeroed, 16)
            act.wait_ge(angles_ready, 1)
            act.activation(sin[:, :, :], ang, ACT.Sin).then_inc(trig_ready, 1)
            act.activation(cos[:, :, :], angc, ACT.Sin).then_inc(trig_ready, 1)
            act.wait_ge(lam_sums, 1)
            act.activation(lame, lams, ACT.Exp).then_inc(lam_exp, 1)

            def attention(layer):
                for item in ORDER:
                    name, key = item[0], (layer, *item)
                    if name == "N1":
                        squares(("attn", layer), item[1])
                    elif name == "NF1":
                        squares(("ffn", layer), item[1])
                    elif name in ("X", "OT", "XF"):
                        if item[2] == 0:
                            turn_evac(key, item)
                    elif name == "PC":
                        t = item[1]
                        b = job(act, key)
                        copy(pc[:, t, :], b[:, 0:416])
                        act.activation(qcT[:, 0, 0:CQ], b[:, 0:CQ], ACT.Square, accum_out=cstat[:, t, 0, 0:1])
                        act.activation(qcT[:, 1, 0:CKV], b[:, CQ:CQ + CKV], ACT.Square,
                                       accum_out=cstat[:, t, 0, 1:2]).then_inc(out_of(key), 1)
                        if t == T - 1:
                            act.wait_ge(normed, norm_count(("attn", layer), t))
                            load_gain(a["ffn_norm"][layer])
                    elif name == "PI":
                        b = job(act, key)
                        copy(pqi[:, item[1], 0:HI * DI], b[:, :]).then_inc(out_of(key), 1)
                    elif name == "PA":
                        b = job(act, key)
                        n = (HA + 1) * DA
                        copy(pa[:, item[1], 0:n], b[:, 0:n])
                        copy(pa[:, item[1], n + DA:n + 2 * DA], b[:, n:n + DA]).then_inc(out_of(key), 1)
                    elif name == "IT":
                        b = job(act, key)
                        t = item[1]
                        copy(qiT[:, :, t * P:(t + 1) * P], b[:, :].rearrange("p (k s) -> p k s", k=4)) \
                            .then_inc(out_of(key), 1)
                    elif name in ("BT", "AT"):
                        t = item[1]
                        b = job(act, key)
                        dst, n, scale = (bT, 4, DB ** -0.5) if name == "BT" else (aT, 3, DA ** -0.5)
                        v = b[:, 0:n * P].rearrange("p (k s) -> p k s", k=n)
                        act.mul(dst[:, 0:2, t * P:(t + 1) * P], v[:, 0:2, :], scale)
                        copy(dst[:, 2:n, t * P:(t + 1) * P], v[:, 2:n, :]).then_inc(out_of(key), 1)
                    elif name == "QC":
                        i = item[2]
                        b = job(act, key)
                        act.mul(qc[:, 4 * i:4 * i + 4, :], b[:, 0:4 * DC].rearrange("p (h d) -> p h d", h=4),
                                DC ** -0.5).then_inc(out_of(key), 1)
                    elif name == "MQ":
                        _, t, i = item
                        b = job(act, key)
                        copy(qcT[0:DC, 4 * i:4 * i + 4, t * P:(t + 1) * P],
                             b[0:DC, :].rearrange("p (k s) -> p k s", k=4)).then_inc(out_of(key), 1)
                    elif name == "U":
                        n = item[1]
                        kind, t, p = UNITS[n]
                        nk = keys(t)
                        if kind == "idx":
                            act.wait_ge(logits_ready, layer * NU + n + 1)
                            if n >= 2:
                                act.wait_ge(index_added, layer * NI + n - 1)
                            act.activation(prob[:, n % 2, :, 0:nk], pair[n % 2][:, :, 0:nk], ACT.Relu) \
                                .then_inc(relu_done, 1)
                        else:
                            act.wait_ge(max_ready, layer * NE + EXPS[n])
                            for m in range(2):
                                src = prob[:, n % 2, m, 0:nk] if kind == "dsa" else pair[n % 2][:, m, 0:nk]
                                last = act.activation(prob[:, n % 2, m, 0:nk], src, ACT.Exp,
                                                      bias=nmax[:, n, m:m + 1], accum_out=lsum[:, n, m:m + 1])
                            last.then_inc(exp_done, 1)
                    elif name == "TP" and UNITS[item[1]][0] != "mla":
                        n = item[1]
                        blocks = (UNITS[n][1] + 1) * (1 if UNITS[n][0] == "diff" else 2)
                        b = job(act, key)
                        copy(pt[:, n % 2, 0:blocks, :], b[:, 0:blocks * P].rearrange("p (k s) -> p k s", k=blocks)) \
                            .then_inc(out_of(key), 1)

            def silu_exp(half, step):
                act.wait_ge(gate_done[half], step + 1)
                act.activation(sig, gate_bank, ACT.Exp, scale=-1.0).then_inc(sig_ready[half], 1)

            def hidden_turned(half, step):
                act.wait_ge(tr_done[half], step + 1)
                copy(hidT, tr_bank.rearrange("p (k s) -> p k s", k=4)).then_inc(hidT_ready[half], 1)

            def dense():
                turn_evac((0, "XF", 1, 0), ("XF", 1, 0))
                for s in range(DENSE_STEPS):
                    silu_exp(0, s)
                    if s:
                        hidden_turned(0, s - 1)
                    if s == 1:
                        act.wait_ge(normed, norm_count(("ffn", 0), 1))
                        load_gain(a["attn_norm"][1])
                        act.wait_ge(d_normed, T)
                        load_layer_gains(1)
                hidden_turned(0, DENSE_STEPS - 1)

            def experts(half):
                s0 = first_step(half)
                rows = [v.rearrange("(s e p) d -> s p e d", e=E, p=P)[half] for v in (xg, yg)]

                def expert_rows(v, e):
                    return v[:, e, :] if isinstance(e, int) else v[:, bass.ds(e, 1), :].rearrange("p a d -> p (a d)")

                def turned(n):
                    act.wait_ge(xt_done[half], n)
                    copy(xT[:, 0:4, :], x_bank[0].rearrange("p (k s) -> p k s", k=4)).then_inc(xT_ready[half], 1)

                def expert(e, last):
                    if not last:
                        act.wait_ge(xt_done[half], e + 1)
                        act.dma_start(xrow, expert_rows(rows[0], e + 1)).then_inc(xrow_full[half], 16)
                    for j in range(1, NCH + 1):
                        step = e * NCH + (s0 + j)
                        if j < NCH or not last:
                            silu_exp(half, step)
                        hidden_turned(half, step - 1)
                        if j == NCH - 1 and not last:
                            act.wait_ge(up_done[half], step + 1)
                            turned(e + 2)
                    act.wait_ge(down_done[half], e * (2 * NCH) + 2 * (s0 + NCH))
                    for c in range(2):
                        copy(yrow[:, 512 * c:512 * c + 512], down_bank[c]).then_inc(y_ready[half], 1)
                    act.wait_ge(y_ready[half], e * 2 + 2)
                    act.dma_start(expert_rows(rows[1], e), yrow).then_inc(y_stored[half], 16)
                    act.wait_ge(y_stored[half], e * 16 + 16)

                act.wait_ge(scattered, 16 * 2 * T)
                act.dma_start(xrow, expert_rows(rows[0], 0)).then_inc(xrow_full[half], 16)
                turned(1)
                silu_exp(half, s0)
                with act.Fori(0, E - 1) as e:
                    expert(e, False)
                expert(E - 1, True)

            attention(0)
            dense()
            attention(1)
            act.wait_ge(normed, norm_count(("ffn", 1), 1))
            load_gain(a["final_norm"])
            act.dma_start(router, a["moe_router"][0].rearrange("(k p) e -> p k e", p=P)).then_inc(loaded_router, 16)
            turn_evac((1, "XF", 1, 0), ("XF", 1, 0))
            act.wait_ge(gates_in, 1)
            act.activation(gate[:, 1, :], gate[:, 0, :], ACT.Exp).then_inc(gates_exp, 1)
            experts(0)
            more = act.value_load(flag[0:1, 0:1])
            with act.If(more > 0):
                experts(1)
            for t in range(T):
                squares(("final", 1), t)

        @block.vector
        def _(dve):
            chained = [0]

            def link(ins):
                chained[0] += 1
                ins.then_inc(dve_chain, 1)
                dve.wait_ge(dve_chain, chained[0])

            def scalar2(o, i, s1, s2, op0, op1):
                return dve.tensor_scalar(o, i, s1, s2, op0, op1)

            def mean(which, t):
                i = norm_count(which, t)
                dve.wait_ge(squares_ready, i)
                scalar2(stat[:, i - 1, 1:2], stat[:, i - 1, 0:1], 1.0 / D, EPS, ALU.mult, ALU.add) \
                    .then_inc(mean_ready, 1)

            def norm(which, t):
                i = norm_count(which, t)
                dve.wait_ge(rms_ready, i)
                if t == 0:
                    dve.wait_ge(loaded_gain, 16 * (NORMS.index(which) + 1))
                return dve.scalar_tensor_tensor(out=hn[:, t, :], in0=h[:, t, :], scalar=stat[:, i - 1, 0:1],
                                                in1=gain[:, :], op0=ALU.mult, op1=ALU.mult)

            def turn_evac(key, item):
                b = job(dve, key)
                _, t, i = item
                dve.tensor_copy(hnT[:, 4 * i:4 * i + 4, t * P:(t + 1) * P],
                                b[:, :].rearrange("p (k s) -> p k s", k=4)).then_inc(out_of(key), 1)

            dve.wait_ge(loaded_small, 16 * 6)
            link(dve.tensor_copy(pos_f, pos_i))
            for t in range(T):
                last = dve.tensor_scalar(ang[:, t, :], freq[:, :], pos_f[:, t:t + 1], None, ALU.mult)
            link(last)
            link(scalar2(turns, ang, 1.0 / TWO_PI, ROUND, ALU.mult, ALU.add))
            link(dve.tensor_scalar(turns, turns, ROUND, None, ALU.subtract))
            for part in PI_PARTS:
                link(dve.scalar_tensor_tensor(out=ang, in0=turns, scalar=-part, in1=ang,
                                              op0=ALU.mult, op1=ALU.add))
            link(dve.tensor_scalar(angc, ang, math.pi / 2, None, ALU.add))
            link(scalar2(turns, angc, math.pi, -TWO_PI, ALU.is_gt, ALU.mult))
            link(dve.tensor_tensor(angc, angc, turns, ALU.add))
            link(scalar2(angc, angc, 3.1415925, -3.1415925, ALU.min, ALU.max))
            scalar2(ang, ang, 3.1415925, -3.1415925, ALU.min, ALU.max).then_inc(angles_ready, 1)
            link(dve.tensor_tensor(lamp, lamv[:, :, 0:4:2, :], lamv[:, :, 1:4:2, :], ALU.mult))
            dve.tensor_reduce(lams, lamp, AX.X, ALU.add).then_inc(lam_sums, 1)
            dve.wait_ge(lam_exp, 1)
            for layer in range(DEPTH):
                link(dve.tensor_tensor(lam[:, layer:layer + 1], lame[:, layer, 0:1], lame[:, layer, 1:2],
                                       ALU.subtract))
                link(dve.tensor_scalar(lam[:, layer:layer + 1], lam[:, layer:layer + 1],
                                       LAM_INIT[layer], None, ALU.add))

            def index_unit(layer, n):
                _, t, p = UNITS[n]
                nk = keys(t)
                dve.wait_ge(relu_done, layer * NI + n + 1)
                acc = score[:, t, 0:nk]
                for m in range(2):
                    i = 2 * p + m
                    rel = prob[:, n % 2, m, 0:nk]
                    if i == 0:
                        ins = dve.tensor_scalar(acc, rel, wi[:, t, 0:1], None, ALU.mult)
                    else:
                        ins = dve.scalar_tensor_tensor(out=acc, in0=rel, scalar=wi[:, t, i:i + 1], in1=acc,
                                                       op0=ALU.mult, op1=ALU.add)
                    if m == 0:
                        link(ins)
                ins.then_inc(index_added, 1)
                dve.wait_ge(index_added, layer * NI + n + 1)
                if p == IDXP - 1:
                    dve.tensor_scalar(score[:, t, 0:nk - CHUNK], score[:, t, 0:nk - CHUNK], IDX_SCALE, None,
                                      ALU.mult)
                    link(dve.scalar_tensor_tensor(out=score[:, t, nk - CHUNK:nk], in0=score[:, t, nk - CHUNK:nk],
                                                  scalar=IDX_SCALE, in1=neg_chunk[:, :], op0=ALU.mult,
                                                  op1=ALU.add))

            def select_round(t, r):
                v = score[:, t, 0:keys(t)]
                link(dve.max(top8[:, :], v))
                link(dve.match_replace(out=v, in_to_replace=top8[:, :], in_values=v, imm_value=TAKEN))
                if r == TOPK // 8 - 1:
                    link(scalar2(v, v, 0.5 * TAKEN, MASKED, ALU.is_gt, ALU.mult))

            def unit_max(layer, n):
                kind, t, p = UNITS[n]
                nk = keys(t)
                dve.wait_ge(logits_ready, layer * NU + n + 1)
                src = pair[n % 2][:, :, 0:nk]
                if kind == "dsa":
                    dst = prob[:, n % 2, :, 0:nk]
                    link(dve.tensor_tensor(dst, src, bc(score[:, t, 0:nk], [P, 2, nk]), ALU.add))
                    src = dst
                dve.tensor_reduce(nmax[:, n, :], src, AX.X, ALU.max, negate=True).then_inc(max_ready, 1)

            def attention(layer):
                rounds = []
                for item in ORDER:
                    name, key = item[0], (layer, *item)
                    if name == "N1":
                        mean(("attn", layer), item[1])
                    elif name == "N2":
                        norm(("attn", layer), item[1]).then_inc(normed, 1)
                    elif name == "NF1":
                        mean(("ffn", layer), item[1])
                    elif name == "NF2":
                        norm(("ffn", layer), item[1]).then_inc(normed, 1)
                    elif name in ("X", "OT", "XF"):
                        if item[2] == 1:
                            turn_evac(key, item)
                    elif name == "PI":
                        t = item[1]
                        emptied(dve, (layer, "PC", t))
                        scalar2(cstat[:, t, 1, 0:1], cstat[:, t, 0, 0:1], 1.0 / CQ, EPS, ALU.mult, ALU.add)
                        scalar2(cstat[:, t, 1, 1:2], cstat[:, t, 0, 1:2], 1.0 / CKV, EPS, ALU.mult, ALU.add) \
                            .then_inc(c_mean, 1)
                    elif name == "PK":
                        t = item[1]
                        b = job(dve, key)
                        dve.tensor_copy(pqi[:, t, HI * DI:(HI + 1) * DI], b[:, 0:DI])
                        dve.tensor_copy(wi[:, t, :], b[:, DI:DI + HI])
                        dve.tensor_copy(pb[:, t, 0:256], b[:, DI + HI:DI + HI + 256]).then_inc(out_of(key), 1)
                    elif name == "C2":
                        t = item[1]
                        dve.wait_ge(c_rms, layer * T + t + 1)
                        dve.wait_ge(loaded_cgain, 48 * (layer + 1))
                        for i, (c0, c1) in enumerate(((0, CQ), (CQ, CQ + CKV))):
                            last = dve.scalar_tensor_tensor(out=pc[:, t, c0:c1], in0=pc[:, t, c0:c1],
                                                            scalar=cstat[:, t, 0, i:i + 1], in1=cgain[:, c0:c1],
                                                            op0=ALU.mult, op1=ALU.mult)
                        last.then_inc(c_normed, 1)
                        if t == 0:
                            link(dve.tensor_scalar(sgain[:, :], sgain[:, :], 1.0 - LAM_INIT[layer], None, ALU.mult))
                    elif name == "CT":
                        b = job(dve, key)
                        t = item[1]
                        dve.tensor_copy(cT[:, :, t * P:(t + 1) * P], b[:, 0:3 * P].rearrange("p (k s) -> p k s", k=3)) \
                            .then_inc(out_of(key), 1)
                    elif name == "KIT":
                        b = job(dve, key)
                        t = item[1]
                        dve.tensor_copy(kiT[:, t * P:(t + 1) * P], b[:, 0:P]).then_inc(out_of(key), 1)
                    elif name == "PB":
                        b = job(dve, key)
                        dve.tensor_copy(pb[:, item[1], 256:768], b[:, :]).then_inc(out_of(key), 1)
                    elif name == "KV":
                        _, t, i = item
                        b = job(dve, key)
                        v = b[:, :].rearrange("p (h d) -> p h d", h=4)
                        dve.tensor_copy(kc[:, 4 * i:4 * i + 4, 0:DN], v[:, :, 0:DN])
                        dve.tensor_copy(vc[:, t, 4 * i * DV:4 * (i + 1) * DV].rearrange("p (h d) -> p h d", h=4),
                                        v[:, :, DN:]).then_inc(out_of(key), 1)
                    elif name == "MK":
                        _, t, i = item
                        b = job(dve, key)
                        if layer == 0 and t == 0 and i == 0:
                            dve.wait_ge(zeroed, 16)
                        dve.tensor_copy(kcT[0:DC, 4 * i:4 * i + 4, t * P:(t + 1) * P],
                                        b[0:DC, :].rearrange("p (k s) -> p k s", k=4)).then_inc(out_of(key), 1)
                    elif name == "U":
                        n = item[1]
                        if UNITS[n][0] == "idx":
                            index_unit(layer, n)
                            if UNITS[n][2] == IDXP - 1:
                                rounds += [(UNITS[n][1], r) for r in range(TOPK // 8)]
                        else:
                            unit_max(layer, n)
                    elif name == "TP":
                        n = item[1]
                        kind, t, p = UNITS[n]
                        nk = keys(t)
                        dve.wait_ge(exp_done, layer * NE + EXPS[n])
                        link(dve.reciprocal(rsum[:, n, :], lsum[:, n, :]))
                        if kind == "diff":
                            p0, p1 = prob[:, n % 2, 0, 0:nk], prob[:, n % 2, 1, 0:nk]
                            link(scalar2(p1, p1, rsum[:, n, 1:2], lam[:, layer:layer + 1], ALU.mult, ALU.mult))
                            dve.scalar_tensor_tensor(out=p0, in0=p0, scalar=rsum[:, n, 0:1], in1=p1,
                                                     op0=ALU.mult, op1=ALU.subtract).then_inc(combined, 1)
                        elif kind == "mla":
                            b = job(dve, key)
                            blocks = 2 * (t + 1)
                            dve.tensor_copy(pt[:, n % 2, 0:blocks, :],
                                            b[:, 0:blocks * P].rearrange("p (k s) -> p k s", k=blocks)) \
                                .then_inc(out_of(key), 1)
                    elif name == "O":
                        n = item[1]
                        kind, t, p = UNITS[n]
                        b = job(dve, key)
                        if kind == "diff":
                            dve.tensor_copy(hn[:, t, 256 + 64 * p:320 + 64 * p], b[:, 0:64]).then_inc(out_of(key), 1)
                        else:
                            at = (512 if kind == "mla" else 0) + 128 * p
                            dve.tensor_tensor(hn[:, t, at:at + 128].rearrange("p (m d) -> p m d", m=2),
                                              b[:, 0:128].rearrange("p (m d) -> p m d", m=2),
                                              rsum[:, n, :].unsqueeze(2).to_broadcast([P, 2, 64]), ALU.mult) \
                                .then_inc(out_of(key), 1)
                    elif name == "D1":
                        t = item[1]
                        o = hn[:, t, 256:512]
                        last_o = max(n for n in DIFFS if UNITS[n][1] == t)
                        emptied(dve, (layer, "O", last_o))
                        link(dve.tensor_tensor(kiT, o, o, ALU.mult))
                        link(dve.tensor_reduce(dstat[:, t, 0, :], kiT.rearrange("p (h d) -> p h d", h=HB), AX.X, ALU.add))
                        scalar2(dstat[:, t, 1, :], dstat[:, t, 0, :], 1.0 / (2 * DB), EPS, ALU.mult, ALU.add) \
                            .then_inc(d_mean, 1)
                    elif name == "D2":
                        t = item[1]
                        o = hn[:, t, 256:512].rearrange("p (h d) -> p h d", h=HB)
                        dve.wait_ge(d_rms, layer * T + t + 1)
                        link(dve.tensor_tensor(o, o, dstat[:, t, 0, :].unsqueeze(2).to_broadcast([P, HB, 2 * DB]),
                                               ALU.mult))
                        dve.tensor_tensor(o, o, bc(sgain[:, :], [P, HB, 2 * DB]), ALU.mult).then_inc(d_normed, 1)
                    elif name == "WO":
                        _, t, half = item
                        b = job(dve, key)
                        v = h[:, t, 512 * half:512 * half + 512]
                        dve.tensor_tensor(v, v, b[:, :], ALU.add).then_inc(out_of(key), 1)
                        if half == 1:
                            emptied(dve, key)
                            dve.sem_inc(residual_ready, 1)
                    if rounds and name in ("U", "TP", "O", "QC", "KV", "BT"):
                        select_round(*rounds.pop(0))
                assert not rounds

            def silu_up(half, step):
                dve.wait_ge(sig_ready[half], step + 1)
                dve.tensor_scalar(sig, sig, 1.0, None, ALU.add).then_inc(den_ready[half], 1)
                dve.wait_ge(den_ready[half], step + 1)
                dve.reciprocal(rec, sig).then_inc(rec_ready[half], 1)
                dve.wait_ge(rec_ready[half], step + 1)
                dve.tensor_tensor(sg, gate_bank, rec, ALU.mult).then_inc(sg_ready[half], 1)
                dve.wait_ge(sg_ready[half], step + 1)
                dve.wait_ge(up_done[half], step + 1)
                dve.tensor_tensor(hid, up_bank, sg, ALU.mult).then_inc(hid_ready[half], 1)

            def add_down(s):
                t = s % T
                for c in range(2):
                    dve.wait_ge(down_done[0], 2 * s + c + 1)
                    v = h[:, t, 512 * c:512 * c + 512]
                    dve.tensor_tensor(v, v, down_bank[c], ALU.add).then_inc(dense_added, 1)

            def dense():
                turn_evac((0, "XF", 1, 1), ("XF", 1, 1))
                for s in range(DENSE_STEPS + 1):
                    if s < DENSE_STEPS:
                        silu_up(0, s)
                    if s:
                        add_down(s - 1)
                    if s >= DENSE_STEPS - 1:
                        dve.wait_ge(dense_added, 2 * s)
                        dve.sem_inc(residual_ready, 1)

            def experts(half):
                s0 = first_step(half)

                def turned(n):
                    dve.wait_ge(xt_done[half], n)
                    dve.tensor_copy(xT[:, 4:8, :], x_bank[1].rearrange("p (k s) -> p k s", k=4)) \
                        .then_inc(xT_ready[half], 1)

                def expert(e, last):
                    for j in range(1, NCH + 1):
                        if j < NCH or not last:
                            silu_up(half, e * NCH + (s0 + j))
                        if j == NCH - 1 and not last:
                            turned(e + 2)

                turned(1)
                silu_up(half, s0)
                with dve.Fori(0, E - 1) as e:
                    expert(e, False)
                expert(E - 1, True)

            def route():
                for t in range(T):
                    b = job(dve, ("RT", t))
                    dve.tensor_copy(lg[:, t, :], b[:, 0:E]).then_inc(out_of(("RT", t)), 1)
                emptied(dve, ("RT", 0))
                emptied(dve, ("RT", 1))
                dve.wait_ge(consts_ready, 3)
                shape = [P, T, E]
                left = lg
                for k in range(2):
                    link(dve.tensor_reduce(best[:, k, :], left, AX.X, ALU.max))
                    link(dve.tensor_tensor(eq, left, best[:, k, :].unsqueeze(2).to_broadcast(shape), ALU.is_equal))
                    link(dve.tensor_tensor(eq, eq, bc(falling, shape), ALU.mult))
                    link(dve.tensor_reduce(first[:, k, :], eq, AX.X, ALU.max))
                    link(dve.tensor_tensor(pick[k], bc(falling, shape),
                                           first[:, k, :].unsqueeze(2).to_broadcast(shape), ALU.is_equal))
                    if k == 0:
                        link(dve.scalar_tensor_tensor(out=lg2, in0=pick[0], scalar=TAKEN, in1=lg,
                                                      op0=ALU.mult, op1=ALU.add))
                        left = lg2
                link(dve.tensor_tensor(chosen, pick[0], pick[1], ALU.add))
                dve.tensor_tensor(gate[:, 0, :], best[:, 1, :], best[:, 0, :], ALU.subtract).then_inc(gates_in, 1)
                dve.sem_inc(chosen_ready, 1)
                dve.wait_ge(gates_exp, 1)
                link(dve.tensor_scalar(gate[:, 0, :], gate[:, 1, :], 1.0, None, ALU.add))
                link(dve.reciprocal(gate[:, 0, :], gate[:, 0, :]))
                link(dve.tensor_tensor(gate[:, 1, :], gate[:, 1, :], gate[:, 0, :], ALU.mult))
                b = job(dve, ("POS",))
                dve.tensor_copy(rank, b[:, 0:3 * E].rearrange("p (t e) -> p t e", t=3)).then_inc(out_of(("POS",)), 1)
                emptied(dve, ("POS",))
                link(dve.tensor_reduce(most, rank[:, 2, :], AX.X, ALU.max))
                place = rank[:, 0:T, :]
                link(scalar2(eq, place, P - 0.5, (E - 1) * P, ALU.is_gt, ALU.mult))
                link(dve.tensor_tensor(place, place, bc(base, shape), ALU.add))
                link(dve.tensor_tensor(place, place, eq, ALU.add))
                for k in range(2):
                    link(dve.tensor_tensor(eq, place, pick[k], ALU.mult))
                    link(dve.tensor_reduce(dest_f[:, k, :], eq, AX.X, ALU.add))
                dve.tensor_copy(dest, dest_f)
                link(dve.tensor_scalar(flag, most, P + 0.5, None, ALU.is_gt))
                dve.sem_inc(routed, 1)

            attention(0)
            dense()
            attention(1)
            turn_evac((1, "XF", 1, 1), ("XF", 1, 1))
            route()
            experts(0)
            more = dve.value_load(flag[0:1, 0:1])
            with dve.If(more > 0):
                experts(1)
            for t in range(T):
                dve.wait_ge(gathered[t], 32)
                for k in range(2):
                    ins = dve.scalar_tensor_tensor(out=h[:, t, :], in0=back[:, 2 * t + k, :],
                                                   scalar=gate[:, k, t:t + 1], in1=h[:, t, :],
                                                   op0=ALU.mult, op1=ALU.add)
                    if k == 0:
                        link(ins)
                ins.then_inc(residual_ready, 1)
            for t in range(T):
                mean(("final", 1), t)
            for t in range(T):
                norm(("final", 1), t).then_inc(out_ready, 1)


_INS = ("x", "positions", "attn_norm", "w_in", "mla_q_norm", "w_uq", "mla_kv_norm", "w_ukv",
        "diff_lambda_q1", "diff_lambda_k1", "diff_lambda_q2", "diff_lambda_k2", "diff_subln", "w_out",
        "ffn_norm", "dense_w_gate", "dense_w_up", "dense_w_down", "moe_router", "moe_w_gate",
        "moe_w_up", "moe_w_down", "final_norm")


def kernel(**inputs):
    import numpy as np
    import concourse.bacc as bacc
    from concourse.bass_utils import run_bass_kernel_spmd

    nc = bacc.Bacc("TRN2", target_bir_lowering=False, num_devices=1)
    arrays = {n: np.ascontiguousarray(inputs[n]) for n in _INS}
    arrays["rope_freq"] = (THETA ** (-np.arange(16) / 16.0)).astype(np.float32)
    args = {n: nc.dram_tensor(f"in_{n}", v.shape, mybir.dt.from_np(v.dtype), kind="ExternalInput").ap()
            for n, v in arrays.items()}
    out = nc.dram_tensor("out_0", arrays["x"].shape, F32, kind="ExternalOutput").ap()
    hybrid_block(nc, args, out)
    r = run_bass_kernel_spmd(nc, [{f"in_{n}": v for n, v in arrays.items()}], core_ids=[0])
    return r.results[0]["out_0"]
```

```python
import math
from contextlib import ExitStack

import concourse.bass as bass
from concourse import mybir
from concourse.alu_op_type import AluOpType as ALU

F32 = mybir.dt.float32
F32R = mybir.dt.float32r
BF16 = mybir.dt.bfloat16
I32 = mybir.dt.int32
U32 = mybir.dt.uint32
ACT = mybir.ActivationFunctionType
AX = mybir.AxisListType

P = 128
CHUNK = 64
THETA = 500000.0
EPS = 1e-6
TWO_PI = 2.0 * math.pi
PI_PARTS = (6.28125, 1.9340515136718750e-03, 1.2554228305816650e-06)
PI_PARTS = PI_PARTS + (TWO_PI - sum(PI_PARTS),)
ROUND = 1.5 * 2.0 ** 23
MASKED = -(2.0 ** 100)
TAKEN = -3.0e38

RING = 3
SLOT = 4096
ARENA = 15296
FFN_ARENA = 5120
PARTS = 7
WBANKS = 4


def attention_order(n_tiles, idx_units, units):
    T = range(n_tiles)
    order = []
    for t in T:
        order += [("N1", t), ("N2", t), ("X", t, 0), ("X", t, 1), ("PC", t)]
    order += [(name, t) for name in ("PI", "PK") for t in T]
    order += [("C2", t) for t in T] + [("CT", t) for t in T] + [("PA", t) for t in T]
    order += [(name, t) for t in T for name in ("IT", "KIT")]
    order += [("U", 0), ("U", 1), ("PB", 0), ("U", 2), ("U", 3), ("PB", 1), ("U", 4), ("U", 5)]
    order += [("QC", 0, 0), ("QC", 0, 1), ("U", 6), ("U", 7), ("KV", 0, 0), ("KV", 0, 1)]
    order += [("BT", t) for t in T]
    n0, n1 = idx_units, idx_units + units
    fills = {
        n0 + 3: [(name, 0, i) for name in ("MQ", "MK") for i in range(2)],
        n0 + 4: [(name, 1, i) for name in ("QC", "KV") for i in range(2)],
        n0 + 7: [(name, 1, i) for name in ("MQ", "MK") for i in range(2)],
        n0 + 10: [("AT", t) for t in T] + [("D1", t) for t in T],
        n0 + 13: [("D2", t) for t in T],
    }
    for n in range(n0, n1 + 2):
        order += fills.get(n, [])
        if n < n1:
            order.append(("U", n))
        if n0 <= n - 1 < n1:
            order.append(("TP", n - 1))
        if n0 <= n - 2 < n1:
            order.append(("O", n - 2))
    order += [("OT", 0, 0), ("OT", 0, 1), ("WO", 0, 0), ("WO", 0, 1), ("NF1", 0), ("OT", 1, 0),
              ("OT", 1, 1), ("WO", 1, 0), ("NF2", 0), ("XF", 0, 0), ("XF", 0, 1), ("WO", 1, 1),
              ("NF1", 1), ("NF2", 1)]
    return order


def hybrid_block(nc, a, out):
    x, positions = a["x"], a["positions"]
    S, D = x.shape[1], x.shape[2]
    DEPTH, _, NIN = a["w_in"].shape
    T, KT = S // P, D // P
    HA, DA = 4, 64
    HI, DI = 8, 64
    TOPK = min(256, S // 4)
    LAM_INIT = [0.8 - 0.6 * math.exp(-0.3 * layer) for layer in range(DEPTH)]
    IDX_SCALE = (HI * DI) ** -0.5
    HB, DB = 4, 32
    HC, DN, DR, DV = 8, 64, 32, 64
    DC = DN + DR
    CQ, CKV = a["w_uq"].shape[1], a["w_ukv"].shape[1]
    NF = DR // 2
    FF = a["dense_w_gate"].shape[2]
    NCH = FF // 512
    E = a["moe_w_gate"].shape[1]
    assert T == 2 and D == 1024 and FF % 512 == 0 and DEPTH == 2
    assert 3 * NCH % RING == 0 and 12 * NCH % PARTS == 0

    widths = (HA * DA, DA, DA, HI * DI, DI, HI, HB * 2 * DB, HB * 2 * DB, HB * 2 * DB, CQ, CKV, DR)
    starts = [sum(widths[:i]) for i in range(len(widths) + 1)]
    q_a, k_a, v_a, q_i, k_i, w_i, q_b, k_b, v_b, c_q, c_kv, k_r, end = starts
    assert end == NIN
    PROJ = {"PC": (c_q, end), "PI": (q_i, k_i), "PK": (k_i, k_b), "PA": (q_a, q_i), "PB": (k_b, c_q)}

    IDXP = HI // 2
    index_units = [("idx", t, p) for t in (1, 0) for p in range(IDXP)]
    attention_units = [(kind, t, p) for kind, n in (("diff", HB), ("mla", HC // 2), ("dsa", HA // 2))
                       for t in range(T) for p in range(n)]
    UNITS = index_units + attention_units
    NU, NI = len(UNITS), len(index_units)
    ORDER = attention_order(T, NI, NU - NI)

    NOT_JOBS = ("U", "N1", "N2", "C2", "D1", "D2", "NF1", "NF2")
    JOB = {}
    for layer in range(DEPTH):
        for item in ORDER:
            if item[0] not in NOT_JOBS:
                JOB[(layer, *item)] = len(JOB)
        for half in range(2):
            JOB[(layer, "XF", 1, half)] = len(JOB)
    for t in range(T):
        JOB[("RT", t)] = len(JOB)
    JOB[("POS",)] = len(JOB)

    DENSE_STEPS = NCH * T
    USE = {}
    for layer in range(DEPTH):
        for c in PROJ:
            USE[(layer, c)] = len(USE)
        for name in ("UP", "WO0", "WO1"):
            USE[(layer, name)] = len(USE)
        if layer == 0:
            for j in range(NCH + 1):
                for kind, jj in (("g", j), ("u", j), ("d", j - 1)):
                    if 0 <= jj < NCH:
                        USE[("dense", kind, jj)] = len(USE)
    MOE_USE = len(USE)
    PER_EXPERT = 3 * NCH
    FFN_PARTS = 4 * PER_EXPERT

    ctx = ExitStack()
    with ctx:
        def sb(name, shape, dt=F32):
            return ctx.enter_context(nc.sbuf_tensor(name, shape, dt))

        with nc.sbuf_tensor("arena", [P, ARENA], F32) as arena:
            pass
        with nc.sbuf_tensor("ffn_arena", [P, FFN_ARENA], F32) as ffn_arena:
            split = [nc.sbuf_tensor(name, shape, F32R) for name, shape in (
                ("hnT_hi", [P, KT, S]), ("hnT_lo", [P, KT, S]),
                ("hidT_hi", [P, T, 4, P]), ("hidT_lo", [P, T, 4, P]))]
            with split[0] as hnT_hi, split[1] as hnT_lo, split[2] as hidT_hi, split[3] as hidT_lo:
                pass
        arena_room = sb("arena_room", [P, ARENA])

        def sem(name):
            return ctx.enter_context(nc.semaphore(name))

        ring = sb("ring", [P, RING, SLOT])
        h = sb("h", [P, T, D])
        hn = sb("hn", [P, T, D])
        hnT = sb("hnT", [P, KT, S])
        gain = sb("gain", [P, D])
        ident = sb("ident", [P, P])
        neg_chunk = sb("neg_chunk", [P, CHUNK])
        mask_q = sb("mask_q", [P, P], BF16)
        mask_k = sb("mask_k", [P, CHUNK], BF16)
        freq = sb("freq", [P, NF])
        cos = sb("cos", [P, T, NF])
        sin = sb("sin", [P, T, NF])
        cgain = sb("cgain", [P, CQ + CKV])
        sgain = sb("sgain", [P, 2 * DB])
        stat = sb("stat", [P, 2 * (2 * DEPTH + 1), 2])
        mhalf = sb("mhalf", [P, 4])
        cstat = sb("cstat", [P, T, 2, 2])
        dstat = sb("dstat", [P, T, 2, HB])
        lam = sb("lam", [P, DEPTH])
        nmax = sb("nmax", [P, NU, 2])
        lsum = sb("lsum", [P, NU, 2])
        rsum = sb("rsum", [P, NU, 2])
        top8 = sb("top8", [P, 8])
        wi = sb("wi", [P, T, HI])
        rope_c = sb("rope_c", [P, HC * DR])
        rope_s = sb("rope_s", [P, HC * DR])

        w_hi = sb("w_hi", [P, PARTS, 1024], F32R)
        w_lo = sb("w_lo", [P, PARTS, 1024], F32R)
        used = [0]

        def carve(n):
            at = used[0]
            used[0] += n
            assert used[0] <= ARENA, used[0]
            return arena[:, at:at + n]

        pa = carve(T * 448).rearrange("p (t n) -> p t n", t=T)
        both = carve(2 * HC * DC)
        pqi = both[:, 0:T * 640].rearrange("p (t n) -> p t n", t=T)
        qc = both[:, 0:HC * DC].rearrange("p (h d) -> p h d", h=HC)
        kc = both[:, HC * DC:2 * HC * DC].rearrange("p (h d) -> p h d", h=HC)
        pb = carve(T * 768).rearrange("p (t n) -> p t n", t=T)
        pc = carve(T * 416).rearrange("p (t n) -> p t n", t=T)
        vc = carve(T * HC * DV).rearrange("p (t n) -> p t n", t=T)
        cT = carve(3 * S).rearrange("p (k s) -> p k s", k=3)
        bT = carve(4 * S).rearrange("p (k s) -> p k s", k=4)
        aT = carve(3 * S).rearrange("p (k s) -> p k s", k=3)
        kiT = carve(S)
        qiT_or_pt = carve(4 * S)
        qiT = qiT_or_pt.rearrange("p (k s) -> p k s", k=4)
        pt = qiT_or_pt.rearrange("p (b k s) -> p b k s", b=2, k=4)
        qcT = carve(HC * S).rearrange("p (k s) -> p k s", k=HC)
        kcT = carve(HC * S).rearrange("p (k s) -> p k s", k=HC)
        prob = carve(2 * 2 * S).rearrange("p (b m s) -> p b m s", b=2, m=2)
        score = carve(T * S).rearrange("p (t s) -> p t s", t=T)
        lamv = qcT[:, 0, :].rearrange("p (l v d) -> p l v d", l=DEPTH, v=4)
        lamp = qcT[:, 1, 0:DEPTH * 2 * DB].rearrange("p (l v d) -> p l v d", l=DEPTH, v=2)
        lams = qcT[:, 2, 0:2 * DEPTH].rearrange("p (l v) -> p l v", l=DEPTH)
        lame = qcT[:, 2, 64:64 + 2 * DEPTH].rearrange("p (l v) -> p l v", l=DEPTH)
        pos_i = qcT[:, 3, 0:T].bitcast(I32)
        pos_f = qcT[:, 3, 64:64 + T]
        ang = qcT[:, 4, 0:T * NF].rearrange("p (t f) -> p t f", t=T)
        turns = qcT[:, 5, 0:T * NF].rearrange("p (t f) -> p t f", t=T)
        angc = qcT[:, 6, 0:T * NF].rearrange("p (t f) -> p t f", t=T)
        used[0] = 0
        sg = carve(T * 512).rearrange("p (t n) -> p t n", t=T)
        hid = carve(T * 512).rearrange("p (t n) -> p t n", t=T)
        yrow = carve(D)
        router = carve(KT * E).rearrange("p (k e) -> p k e", k=KT)
        before = carve(P)
        ones = carve(P)
        lg = carve(T * E).rearrange("p (t e) -> p t e", t=T)
        lg2 = carve(T * E).rearrange("p (t e) -> p t e", t=T)
        eq = carve(T * E).rearrange("p (t e) -> p t e", t=T)
        pick = [carve(T * E).rearrange("p (t e) -> p t e", t=T) for _ in range(2)]
        chosen = carve(T * E).rearrange("p (t e) -> p t e", t=T)
        spread = carve(T * E).rearrange("p (t e) -> p t e", t=T)
        rank = carve(3 * E).rearrange("p (t e) -> p t e", t=3)
        falling = carve(E)
        best = carve(2 * T).rearrange("p (k t) -> p k t", k=2)
        first = carve(2 * T).rearrange("p (k t) -> p k t", k=2)
        gate = carve(2 * T).rearrange("p (k t) -> p k t", k=2)
        slots = carve(2 * P).rearrange("p (s n) -> p s n", s=2)
        place = carve(T * E).rearrange("p (e t) -> p e t", e=E)
        share = carve(T * E).rearrange("p (e t) -> p e t", e=E)
        sel = carve(T * P).rearrange("p (t n) -> p t n", t=T)
        gsel = carve(T * P).rearrange("p (t n) -> p t n", t=T)
        gselT = carve(T * P).rearrange("p (t n) -> p t n", t=T)
        most = carve(1)
        flag = carve(1).bitcast(I32)
        assert used[0] <= FFN_ARENA and FFN_ARENA + 2 * KT * S + 2 * T * 4 * P <= ARENA
        xT_hi, xT_lo = hnT_hi[:, :, 0:P], hnT_lo[:, :, 0:P]

        pair = [ctx.enter_context(nc.psum_tensor(f"pair{i}", [P, 2, 512], F32)) for i in range(2)]
        work = [ctx.enter_context(nc.psum_tensor(f"work{i}", [P, 512], F32)) for i in range(WBANKS)]
        gate_bank = [pair[0][:, t, :] for t in range(T)]
        up_bank = [pair[1][:, t, :] for t in range(T)]
        dense_down = [[work[2 * c + t][:, :] for t in range(T)] for c in range(2)]
        dense_turn = dense_down[1]
        x_bank, down_bank = [work[0][:, :], work[1][:, :]], [work[2][:, :], work[3][:, :]]
        tr_bank, sel_bank = gate_bank[1], up_bank[1]

        loaded_x = [sem(f"loaded_x{t}") for t in range(T)]
        loaded_ukv = sem("loaded_ukv")
        loaded_small = sem("loaded_small")
        loaded_gain = sem("loaded_gain")
        loaded_cgain = sem("loaded_cgain")
        loaded_router = sem("loaded_router")
        slot_full = [sem(f"slot_full{i}") for i in range(RING)]
        consts_ready = sem("consts_ready")
        pool_chain = sem("pool_chain")
        dve_chain = sem("dve_chain")
        angles_ready = sem("angles_ready")
        trig_ready = sem("trig_ready")
        lam_sums = sem("lam_sums")
        lam_exp = sem("lam_exp")
        lam_ready = sem("lam_ready")
        residual_ready = sem("residual_ready")
        squares_ready = sem("squares_ready")
        mean_ready = sem("mean_ready")
        rms_ready = sem("rms_ready")
        normed = sem("normed")
        job_done = sem("job_done")
        evacuated = [sem(f"evacuated{i}") for i in range(WBANKS)]
        c_squares = sem("c_squares")
        c_mean = sem("c_mean")
        c_rms = sem("c_rms")
        c_normed = sem("c_normed")
        roped = sem("roped")
        logits_ready = sem("logits_ready")
        relu_done = sem("relu_done")
        index_added = sem("index_added")
        max_ready = sem("max_ready")
        exp_done = sem("exp_done")
        combined = sem("combined")
        d_mean = sem("d_mean")
        d_rms = sem("d_rms")
        d_normed = sem("d_normed")
        tr_done, silu_ready, hid_ready, hidT_hi_ready, hidT_ready, sel_ready, xt_done, xT_hi_ready, \
            xT_ready, gsel_ready, gsel_turned, gselT_ready, y_ready, spread_done, added = (
                [sem(f"{n}{half}") for half in range(2)] for n in (
                    "tr_done", "silu_ready", "hid_ready", "hidT_hi_ready", "hidT_ready",
                    "sel_ready", "xt_done", "xT_hi_ready", "xT_ready", "gsel_ready", "gsel_turned",
                    "gselT_ready", "y_ready", "spread_done", "added"))
        hi_done = sem("hi_done")
        lo_done = sem("lo_done")
        part_used = sem("part_used")
        gsel_found = [sem(f"gsel_found{half}") for half in range(2)]
        hnT_hi_ready = sem("hnT_hi_ready")
        dense_added = sem("dense_added")
        routed = sem("routed")
        chosen_ready = sem("chosen_ready")
        gates_in = sem("gates_in")
        gates_exp = sem("gates_exp")
        out_ready = sem("out_ready")
        stored = sem("stored")

        def job(eng, key):
            eng.wait_ge(job_done, JOB[key] + 1)
            return work[JOB[key] % WBANKS]

        def emptied(eng, key):
            eng.wait_ge(evacuated[JOB[key] % WBANKS], JOB[key] // WBANKS + 1)

        def out_of(key):
            return evacuated[JOB[key] % WBANKS]

        def slot(use):
            return ring[:, use % RING, :]

        def arrived(eng, use, rounds=0):
            eng.wait_ge(slot_full[use % RING], rounds + 16 * (use // RING + 1))

        def first_part(half):
            return FFN_PARTS * (1 + E * half)

        def part_view(n, kind, use):
            if kind < 2:
                return slot(use).rearrange("p (k n) -> p k n", k=KT)[:, 2 * n:2 * n + 2, :]
            c, k = n // 2, 2 * (n % 2)
            return slot(use).rearrange("p (k n) -> p k n", k=4)[:, k:k + 2, 512 * c:512 * c + 512]

        def part_buffers(part):
            return [w[:, part % PARTS, :].rearrange("p (k n) -> p k n", k=2) for w in (w_hi, w_lo)]

        def part_source(part, half, final):
            if half is None:
                first, use0 = 0, USE[("dense", "g", 0)]
            else:
                first, use0 = first_part(half), MOE_USE + half * E * PER_EXPERT
            n = (part - first) // 4
            kind = n if n < 2 else (n - 2) % 3
            if final and n == E * PER_EXPERT - 1 or half is None and n == PER_EXPERT - 1:
                kind = 2
            return (part - first) % 4, kind, use0 + n

        ROWS_AT, GATES_AT = 3, 5

        def opening(half):
            return [(j, 1, first_step(half) + j, first_part(half) + 12 * j - 4, 0, True, True) for j in (1, 2)]

        def places(half, e, last):
            found = []
            for i, j in enumerate([*range(3, NCH + 1), 1, 2]):
                if last and j < 3:
                    break
                step = e * NCH + (first_step(half) + 3 + i)
                part = first_part(half) + 32 + 12 * i + (FFN_PARTS * e if last else 0)
                found.append((j, e + (1 if j > 2 else 2), step, part, 0 if last else e * FFN_PARTS,
                              not (last and j == NCH), not last))
            return found

        def first_step(half):
            return DENSE_STEPS if half == 0 else 0

        def bc(ap, shape):
            for _ in range(len(shape) - len(ap.shape)):
                ap = ap.unsqueeze(1)
            return ap.to_broadcast(shape)

        def keys(t):
            return P * (t + 1)

        EXPS = {n: i + 1 for i, n in enumerate(range(NI, NU))}
        NE = NU - NI
        DIFFS = [n for n in range(NU) if UNITS[n][0] == "diff"]
        ROPES = [("kr", 0), ("kr", 1), ("i", 0), ("i", 1), ("a", 0), ("a", 1), ("b", 0), ("b", 1),
                 ("c", 0), ("c", 1)]

        def roped_by(eng, layer, key):
            eng.wait_ge(roped, layer * len(ROPES) + ROPES.index(key) + 1)

        NORMS = [("attn", 0), ("ffn", 0), ("attn", 1), ("ffn", 1), ("final", 1)]

        def norm_count(which, t):
            return NORMS.index(which) * T + t + 1

        FREE = {}
        for layer in range(DEPTH):
            for c in PROJ:
                FREE[USE[(layer, c)]] = (job_done, JOB[(layer, c, T - 1)] + 1)
            FREE[USE[(layer, "UP")]] = (job_done, JOB[(layer, "KV", 1, 1)] + 1)
            for half in range(2):
                FREE[USE[(layer, f"WO{half}")]] = (job_done, JOB[(layer, "WO", T - 1, half)] + 1)
        for n in range(PER_EXPERT):
            FREE[USE[("dense", "g", 0)] + n] = (lo_done, 4 * n + 4)

        block = ctx.enter_context(nc.Block())

        @block.sync
        def _(sp):
            wg, wu, wd = a["moe_w_gate"], a["moe_w_up"], a["moe_w_down"]

            def column_chunk(w, c0, c1):
                return w[:, c0:c1].rearrange("(k p) n -> p k n", p=P)

            def load(use, view, src, rounds=0):
                sp.dma_start(view, src).then_inc(slot_full[use % RING], 16)

            def freed(use):
                if use in FREE:
                    sp.wait_ge(*FREE[use])

            def wide(use, n, k=KT):
                return slot(use)[:, 0:k * n].rearrange("p (k n) -> p k n", k=k)

            for t in range(T):
                sp.dma_start(h[:, t, :], x[0, t * P:(t + 1) * P, :]).then_inc(loaded_x[t], 16)
            for layer in range(DEPTH):
                for c, (c0, c1) in PROJ.items():
                    use = USE[(layer, c)]
                    freed(use - RING)
                    load(use, wide(use, c1 - c0), column_chunk(a["w_in"][layer], c0, c1))
                use = USE[(layer, "UP")]
                freed(use - RING)
                nq, nkv = HC * DC, HC * (DN + DV)
                sp.dma_start(slot(use)[:, 0:2 * nq].rearrange("p (k n) -> p k n", k=2),
                             a["w_uq"][layer].rearrange("(k p) n -> p k n", p=P)) \
                    .then_inc(slot_full[use % RING], 16)
                sp.dma_start(slot(use)[:, 2 * nq:2 * nq + nkv], a["w_ukv"][layer]) \
                    .then_inc(loaded_ukv, 16)
                for half in range(2):
                    use = USE[(layer, f"WO{half}")]
                    freed(use - RING)
                    load(use, wide(use, 512), column_chunk(a["w_out"][layer], 512 * half, 512 * half + 512))
                if layer == 0:
                    for j in range(NCH + 1):
                        for kind, w in (("g", a["dense_w_gate"][0]), ("u", a["dense_w_up"][0])):
                            if j < NCH:
                                use = USE[("dense", kind, j)]
                                freed(use - RING)
                                load(use, wide(use, 512), column_chunk(w, 512 * j, 512 * j + 512))
                        if j:
                            use = USE[("dense", "d", j - 1)]
                            freed(use - RING)
                            load(use, wide(use, D, 4),
                                 a["dense_w_down"][0][512 * (j - 1):512 * j, :]
                                 .rearrange("(k p) n -> p k n", p=P))

            def chunk_at(e, k):
                e, k = e + k // PER_EXPERT, k % PER_EXPERT
                j, kind = k // 3 + 1, k % 3
                if kind == 2:
                    return e, j - 1, 2
                return (e, j, kind) if j < NCH else (e + 1, 0, kind)

            def load_chunk(use, e, j, kind):
                w = (wg, wu, wd)[kind]
                w = w[0, e] if isinstance(e, int) else w[0][bass.ds(e, 1)].rearrange("a k n -> (a k) n")
                if kind < 2:
                    load(use, wide(use, 512), column_chunk(w, 512 * j, 512 * j + 512))
                else:
                    load(use, wide(use, D, 4),
                         w[512 * j:512 * j + 512, :].rearrange("(k p) n -> p k n", p=P))

            def chunk_split(half, n):
                sp.wait_ge(lo_done, n * 4 + (first_part(half) + 4))

            def expert_weights(half):
                first = MOE_USE + half * E * PER_EXPERT
                for i in range(RING + 2):
                    if i >= RING:
                        chunk_split(half, i - RING)
                    elif half == 0:
                        freed(first + i - RING)
                    load_chunk(first + i, *((0, 0, i) if i < 2 else chunk_at(0, i - 2)))
                with sp.Fori(0, E - 1) as e:
                    for k in range(PER_EXPERT):
                        chunk_split(half, e * PER_EXPERT + (2 + k))
                        load_chunk(first + 2 + k + RING, *chunk_at(e, k + RING))
                last = (E - 1) * PER_EXPERT
                for k in range(last + RING, last + PER_EXPERT - 2):
                    chunk_split(half, 2 + k - RING)
                    load_chunk(first + 2 + k, *((E - 1, NCH - 1, 2) if k % PER_EXPERT == 3 * NCH - 3
                                                else chunk_at(0, k)))

            expert_weights(0)
            sp.wait_ge(routed, 1)
            more = sp.value_load(flag[0:1, 0:1])
            with sp.If(more > 0):
                sp.wait_ge(lo_done, first_part(1))
                expert_weights(1)
            for t in range(T):
                sp.wait_ge(out_ready, t + 1)
                sp.dma_start(out[0, t * P:(t + 1) * P, :], hn[:, t, :]).then_inc(stored, 16)
            sp.wait_ge(stored, 16 * T)

        @block.gpsimd
        def _(pool):
            chained = [0]

            def link(ins):
                chained[0] += 1
                ins.then_inc(pool_chain, 1)
                pool.wait_ge(pool_chain, chained[0])

            link(pool.memset(ident[:, :], 0.0))
            link(pool.affine_select(out=ident[:, :], in_=ident[:, :], compare_op=ALU.not_equal, fill=1.0,
                                    base=0, pattern=[[-1, P]], channel_multiplier=1))
            pool.memset(mhalf[:, :], -0.5)
            pool.memset(mask_q[:, 0:CHUNK], 1.0)
            pool.memset(mask_q[:, CHUNK:P], 0.0)
            pool.memset(mask_k[:, :], MASKED)
            link(pool.memset(neg_chunk[:, :], 0.0))
            pool.memset(neg_chunk[0:CHUNK, :], MASKED).then_inc(consts_ready, 1)
            pool.wait_ge(consts_ready, 1)

            def inverse_root(outp, inp, n):
                return pool.tensor_tensor(outp, inp, mhalf[:, 0:n], ALU.pow)

            def norm_root(which, t):
                i = norm_count(which, t)
                pool.wait_ge(mean_ready, i)
                inverse_root(stat[:, i - 1, 0:1], stat[:, i - 1, 1:2], 1).then_inc(rms_ready, 1)

            def rope(v, t, n, half):
                shape = [P, n, 2, half]
                step = NF // half
                c, s = (bc(z[:, t, :].rearrange("p (f s) -> p f s", s=step)[:, :, 0], shape) for z in (cos, sin))
                rc = rope_c[:, 0:2 * n * half].rearrange("p (n a f) -> p n a f", n=n, a=2)
                rs = rope_s[:, 0:2 * n * half].rearrange("p (n a f) -> p n a f", n=n, a=2)
                link(pool.tensor_tensor(rc, v, c, ALU.mult))
                link(pool.tensor_tensor(rs, v, s, ALU.mult))
                link(pool.tensor_tensor(v[:, :, 0, :], rc[:, :, 0, :], rs[:, :, 1, :], ALU.subtract))
                return pool.tensor_tensor(v[:, :, 1, :], rc[:, :, 1, :], rs[:, :, 0, :], ALU.add)

            def halves(v, n, d, half):
                return v.rearrange("p (n d) -> p n d", n=n)[:, :, 0:2 * half] \
                        .rearrange("p n (a f) -> p n a f", a=2)

            rotations = [0]

            def rotated(ins):
                rotations[0] += 1
                ins.then_inc(roped, 1)
                pool.wait_ge(roped, rotations[0])

            for layer in range(DEPTH):
                for t in range(T):
                    norm_root(("attn", layer), t)
                for t in range(T):
                    pool.wait_ge(c_mean, layer * T + t + 1)
                    inverse_root(cstat[:, t, 0, :], cstat[:, t, 1, :], 2).then_inc(c_rms, 1)
                if layer == 0:
                    pool.wait_ge(trig_ready, 2)
                for t in range(T):
                    emptied(pool, (layer, "PC", t))
                    rotated(rope(halves(pc[:, t, CQ + CKV:], 1, DR, DR // 2), t, 1, DR // 2))
                for t in range(T):
                    emptied(pool, (layer, "PI", t))
                    emptied(pool, (layer, "PK", t))
                    link(rope(halves(pqi[:, t, 0:(HI + 1) * DI], HI + 1, DI, DI // 8), t, HI + 1, DI // 8))
                    rotated(pool.tensor_copy(pqi[:, t, (HI + 1) * DI:], pqi[:, t, HI * DI:(HI + 1) * DI]))
                for t in range(T):
                    emptied(pool, (layer, "PA", t))
                    link(rope(halves(pa[:, t, 0:(HA + 1) * DA], HA + 1, DA, DA // 8), t, HA + 1, DA // 8))
                    rotated(pool.tensor_copy(pa[:, t, (HA + 1) * DA:(HA + 2) * DA],
                                             pa[:, t, HA * DA:(HA + 1) * DA]))
                for t in range(T):
                    emptied(pool, (layer, "PK", t))
                    emptied(pool, (layer, "PB", t))
                    rotated(rope(halves(pb[:, t, 0:4 * HB * DB], 4 * HB, DB, DB // 8), t, 4 * HB, DB // 8))
                for t in range(T):
                    for i in range(2):
                        emptied(pool, (layer, "QC", t, i))
                    link(rope(qc[:, :, DN:].rearrange("p n (a f) -> p n a f", a=2), t, HC, DR // 2))
                    for i in range(2):
                        emptied(pool, (layer, "KV", t, i))
                    rotated(pool.tensor_copy(kc[:, :, DN:], bc(pc[:, t, CQ + CKV:], [P, HC, DR])))
                for t in range(T):
                    pool.wait_ge(d_mean, layer * T + t + 1)
                    inverse_root(dstat[:, t, 0, :], dstat[:, t, 1, :], HB).then_inc(d_rms, 1)
                for t in range(T):
                    norm_root(("ffn", layer), t)

            pool.wait_ge(normed, norm_count(("ffn", 1), 0))
            link(pool.memset(before[:, :], 1.0))
            link(pool.affine_select(out=before[:, :], in_=before[:, :], compare_op=ALU.is_gt, fill=0.0,
                               base=0, pattern=[[1, P]], channel_multiplier=-1))
            pool.memset(ones[:, :], 1.0)
            pool.iota(falling, [[-1, E]], base=E, channel_multiplier=0,
                      allow_small_or_imprecise_dtypes=True)
            pool.iota(slots, [[P, 2], [1, P]], base=0, channel_multiplier=0,
                      allow_small_or_imprecise_dtypes=True).then_inc(consts_ready, 1)
            for t in range(T):
                norm_root(("final", 1), t)

        @block.tensor
        def _(pe):
            def begin(key):
                n = JOB[key]
                if n >= WBANKS:
                    pe.wait_ge(evacuated[n % WBANKS], n // WBANKS)
                if JOB[(1, "X", 0, 0)] <= n < JOB[(1, "X", 0, 0)] + WBANKS:
                    pe.wait_ge(dense_added, 2 * DENSE_STEPS)
                return work[n % WBANKS]

            def transposes(b, blocks, n=P):
                for i, src in enumerate(blocks):
                    last = pe.transpose(b[0:n, i * P:(i + 1) * P], src, ident[:, :])
                return last

            def tile(t):
                return slice(t * P, (t + 1) * P)

            def cols(src, t, i0, n):
                return [src[:, t, (i0 + i) * P:(i0 + i + 1) * P] for i in range(n)]

            def product(b, n, lhs, rhs):
                for k in range(len(rhs)):
                    last = pe.matmul(b[:, 0:n], lhs[k], rhs[k], start=(k == 0), stop=(k == len(rhs) - 1))
                return last

            def wide(use, n):
                v = slot(use)[:, 0:KT * n].rearrange("p (k n) -> p k n", k=KT)
                return [v[:, k, :] for k in range(KT)]

            def transpose_rows(layer, item):
                name, t, i = item
                b = begin((layer, *item))
                if name == "OT":
                    last_o = max(n for n in range(NI, NU) if UNITS[n][1] == t)
                    emptied(pe, (layer, "O", last_o))
                    pe.wait_ge(d_normed, layer * T + t + 1)
                else:
                    pe.wait_ge(normed, norm_count(("attn" if name == "X" else "ffn", layer), t))
                transposes(b, cols(hn, t, 4 * i, 4)).then_inc(job_done, 1)

            def logits(layer, n):
                kind, t, p = UNITS[n]
                S2 = pair[n % 2]
                nk = keys(t)
                if n >= 2:
                    if n - 2 < NI:
                        pe.wait_ge(relu_done, layer * NI + n - 1)
                    else:
                        pe.wait_ge(exp_done, layer * NE + EXPS[n - 2])
                if (kind, p) in (("idx", 0), ("diff", 0), ("mla", 0), ("dsa", 0)):
                    for name in {"idx": ("IT", "KIT"), "diff": ("BT",), "dsa": ("AT",), "mla": ("MQ", "MK")}[kind]:
                        for tt in range(t + 1):
                            for i in (range(2) if kind == "mla" else (None,)):
                                emptied(pe, (layer, name, tt) if i is None else (layer, name, tt, i))
                for m in range(2):
                    if kind == "idx":
                        q, k, r = qiT[64 * m:64 * m + 64, p, tile(t)], kiT[64 * m:64 * m + 64, 0:nk], 0
                    elif kind == "diff":
                        blk, r = (2 * p + m) // 4, 32 * ((2 * p + m) % 4)
                        q, k = bT[r:r + DB, blk, tile(t)], bT[r:r + DB, 2 + blk, 0:nk]
                    elif kind == "mla":
                        q, k, r = qcT[0:DC, 2 * p + m, tile(t)], kcT[0:DC, 2 * p + m, 0:nk], 0
                    else:
                        q, k, r = aT[64 * m:64 * m + 64, p, tile(t)], aT[64 * m:64 * m + 64, 2, 0:nk], 0
                    plain = kind in ("idx", "dsa")
                    last = pe.matmul(S2[:, m, 0:nk], q, k, start=True, stop=plain)
                    if not plain:
                        last = pe.matmul(S2[:, m, nk - CHUNK:nk], mask_q[r:r + 1, :], mask_k[r:r + 1, :],
                                         start=False, stop=True)
                last.then_inc(logits_ready, 1)

            def attention(layer):
                for item in ORDER:
                    name, key = item[0], (layer, *item)
                    if name in ("X", "XF", "OT"):
                        transpose_rows(layer, item)
                    elif name in PROJ:
                        t, use = item[1], USE[(layer, name)]
                        b = begin(key)
                        n = PROJ[name][1] - PROJ[name][0]
                        arrived(pe, use)
                        for i in range(2):
                            emptied(pe, (layer, "X", t, i))
                        product(b, n, [hnT[:, k, tile(t)] for k in range(KT)], wide(use, n)) \
                            .then_inc(job_done, 1)
                    elif name == "CT":
                        b = begin(key)
                        pe.wait_ge(c_normed, layer * T + item[1] + 1)
                        transposes(b, cols(pc, item[1], 0, 3)).then_inc(job_done, 1)
                    elif name in ("IT", "KIT", "AT", "BT"):
                        t = item[1]
                        b = begin(key)
                        roped_by(pe, layer, ({"IT": "i", "KIT": "i", "AT": "a", "BT": "b"}[name], t))
                        src, i0, n = {"IT": (pqi, 0, 4), "KIT": (pqi, 4, 1), "AT": (pa, 0, 3), "BT": (pb, 0, 4)}[name]
                        transposes(b, cols(src, t, i0, n)).then_inc(job_done, 1)
                    elif name == "QC":
                        _, t, i = item
                        b, use, n = begin(key), USE[(layer, "UP")], HC * DC // 2
                        arrived(pe, use)
                        emptied(pe, (layer, "CT", t))
                        product(b, n, [cT[:, k, tile(t)] for k in range(2)],
                                [slot(use)[:, k * 2 * n + i * n:k * 2 * n + i * n + n] for k in range(2)]) \
                            .then_inc(job_done, 1)
                    elif name == "KV":
                        _, t, i = item
                        b, at = begin(key), 2 * HC * DC + 512 * i
                        pe.wait_ge(loaded_ukv, 16 * (layer + 1))
                        product(b, 512, [cT[:, 2, tile(t)]], [slot(USE[(layer, "UP")])[:, at:at + 512]]) \
                            .then_inc(job_done, 1)
                    elif name in ("MQ", "MK"):
                        _, t, i = item
                        b = begin(key)
                        roped_by(pe, layer, ("c", t))
                        src = qc if name == "MQ" else kc
                        transposes(b, [src[:, 4 * i + j, :] for j in range(4)], DC).then_inc(job_done, 1)
                    elif name == "U":
                        logits(layer, item[1])
                    elif name == "TP":
                        n = item[1]
                        kind, t, p = UNITS[n]
                        b = begin(key)
                        if kind == "diff":
                            pe.wait_ge(combined, layer * len(DIFFS) + DIFFS.index(n) + 1)
                        else:
                            pe.wait_ge(exp_done, layer * NE + EXPS[n])
                        transposes(b, [prob[:, n % 2, m, tile(kb)] for m in range(1 if kind == "diff" else 2)
                                       for kb in range(t + 1)]).then_inc(job_done, 1)
                    elif name == "O":
                        n = item[1]
                        kind, t, p = UNITS[n]
                        b = begin(key)
                        emptied(pe, (layer, "TP", n))
                        for m in range(1 if kind == "diff" else 2):
                            for kb in range(t + 1):
                                v = {"diff": pb[:, kb, 512 + 64 * p:576 + 64 * p],
                                     "mla": vc[:, kb, DV * (2 * p + m):DV * (2 * p + m + 1)],
                                     "dsa": pa[:, kb, 384:448]}[kind]
                                last = pe.matmul(b[:, 64 * m:64 * m + 64], pt[:, n % 2, m * (t + 1) + kb, :],
                                                 v, start=(kb == 0), stop=(kb == t))
                        last.then_inc(job_done, 1)
                    elif name == "WO":
                        _, t, half = item
                        b, use = begin(key), USE[(layer, f"WO{half}")]
                        arrived(pe, use)
                        for i in range(2):
                            emptied(pe, (layer, "OT", t, i))
                        product(b, 512, [hnT[:, k, tile(t)] for k in range(KT)], wide(use, 512)) \
                            .then_inc(job_done, 1)

            def part_product(part, shift, k, lhs, b, first, last):
                w = part_buffers(part)
                for kk in range(2):
                    for i, (x_part, w_part) in enumerate(((0, 0), (0, 1), (1, 0))):
                        mm = pe.matmul(b, lhs[x_part][k + kk], w[w_part][:, kk, :],
                                       start=(first and kk == 0 and i == 0), stop=(last and kk == 1 and i == 2))
                return mm

            def part_ready(part, shift):
                pe.wait_ge(lo_done, shift + (part + 1))

            def columns(part, shift, operands, banks):
                for i in range(4):
                    part_ready(part + i, shift)
                    for lhs, b in zip(operands, banks):
                        mm = part_product(part + i, shift, 2 * i, lhs, b, i == 0, i == 3)
                    mm.then_inc(part_used, 1)

            def turn(half, step, t, b):
                pe.wait_ge(hid_ready[half], step + 1)
                transposes(b, [hid[:, t, k * P:(k + 1) * P] for k in range(4)]).then_inc(tr_done[half], 1)

            hidT_parts = [[[v[:, t, k, :] for k in range(4)] for v in (hidT_hi, hidT_lo)] for t in range(T)]

            def dense():
                lhs = [[[v[:, k, tile(t)] for k in range(KT)] for v in (hnT_hi, hnT_lo)] for t in range(T)]
                part = 0
                for j in range(NCH + 1):
                    if j == 0:
                        for t in range(T):
                            for i in range(2):
                                emptied(pe, (0, "XF", t, i))
                            for i in range(4):
                                part_ready(i, 0)
                                mm = part_product(i, 0, 2 * i, lhs[t], gate_bank[t], i == 0, i == 3)
                                if t == T - 1:
                                    mm.then_inc(part_used, 1)
                            if t == 0:
                                for i in range(2):
                                    transpose_rows(0, ("XF", 1, i))
                        part += 4
                    elif j < NCH:
                        pe.wait_ge(silu_ready[0], T * j)
                        columns(part, 0, lhs, gate_bank)
                        part += 4
                    if j:
                        if j > 1:
                            pe.wait_ge(dense_added, 4 * (j - 1))
                        for t in range(T):
                            turn(0, T * (j - 1) + t, t, dense_turn[t])
                    if j < NCH:
                        if j:
                            pe.wait_ge(hid_ready[0], T * j)
                        columns(part, 0, lhs, up_bank)
                        part += 4
                    if j:
                        pe.wait_ge(hidT_ready[0], T * j)
                        for i in range(4):
                            part_ready(part, 0)
                            for t in range(T):
                                mm = part_product(part, 0, 2 * (i % 2), hidT_parts[t], dense_down[i // 2][t],
                                                  i % 2 == 0, i % 2 == 1)
                            mm.then_inc(part_used, 1)
                            part += 1

            def experts(half):
                s0, part0 = first_step(half), first_part(half)
                lhs = [[v[:, k, :] for k in range(KT)] for v in (xT_hi, xT_lo)]

                def expert_rows(n):
                    pe.wait_ge(sel_ready[half], n)
                    for i in range(2):
                        for k in range(4):
                            for t in range(T):
                                c = (4 * i + k) * P
                                last = pe.matmul(x_bank[i][:, k * P:(k + 1) * P], hn[:, t, c:c + P], sel[:, t, :],
                                                 start=(t == 0), stop=(t == T - 1))
                    last.then_inc(xt_done[half], 1)

                def spread_result(n, t):
                    if t == 0:
                        pe.wait_ge(y_ready[half], n * 2)
                        pe.wait_ge(gselT_ready[half], n)
                    else:
                        pe.wait_ge(added[half], n * 4 - 2)
                    for c in range(2):
                        pe.matmul(x_bank[c], gselT[:, t, :], yrow[:, 512 * c:512 * c + 512], start=True,
                                  stop=True).then_inc(spread_done[half], 1)

                def chunk(j, n, step, part, shift, ahead, more):
                    if j == NCH and more:
                        pe.wait_ge(xT_ready[half], n * 2 + 2)
                    if ahead:
                        pe.wait_ge(silu_ready[half], step)
                        columns(part, shift, [lhs], gate_bank)
                        part += 4
                    turn(half, step - 1, 0, tr_bank)
                    if ahead:
                        pe.wait_ge(hid_ready[half], step)
                        columns(part, shift, [lhs], up_bank)
                        part += 4
                    if j == ROWS_AT and more:
                        expert_rows(n + 1)
                    if j == GATES_AT:
                        pe.wait_ge(gsel_ready[half], n)
                        transposes(sel_bank, [gsel[:, t, :] for t in range(T)]).then_inc(gsel_turned[half], 1)
                    pe.wait_ge(hidT_ready[half], step)
                    for i in range(4):
                        part_ready(part, shift)
                        part_product(part, shift, 2 * (i % 2), hidT_parts[0], down_bank[i // 2],
                                     j == 1 and i % 2 == 0, j == NCH and i % 2 == 1) \
                            .then_inc(part_used, 1)
                        part += 1

                expert_rows(1)
                pe.wait_ge(xT_ready[half], 2)
                columns(part0, 0, [lhs], gate_bank)
                columns(part0 + 4, 0, [lhs], up_bank)
                for j, n, step, part, shift, ahead, more in opening(half):
                    chunk(j, n, step, part, shift, ahead, more)
                with pe.Fori(0, E - 1) as e:
                    for j, n, step, part, shift, ahead, more in places(half, e, False):
                        chunk(j, n, step, part, shift, ahead, more)
                        if j in (1, 2):
                            spread_result(n - 1, j - 1)
                for j, n, step, part, shift, ahead, more in places(half, E - 1, True):
                    chunk(j, n, step, part, shift, ahead, more)
                for t in range(T):
                    spread_result(E, t)

            pe.wait_ge(consts_ready, 1)
            attention(0)
            dense()
            attention(1)
            for i in range(2):
                transpose_rows(1, ("XF", 1, i))
            pe.wait_ge(loaded_router, 16)
            for t in range(T):
                b = begin(("RT", t))
                for i in range(2):
                    emptied(pe, (1, "XF", t, i))
                product(b, E, [hnT[:, k, tile(t)] for k in range(KT)], [router[:, k, :] for k in range(KT)]) \
                    .then_inc(job_done, 1)
            b = begin(("POS",))
            pe.wait_ge(consts_ready, 2)
            pe.wait_ge(chosen_ready, 1)
            pe.matmul(b[:, 0:E], before[:, :], chosen[:, 0, :], start=True, stop=True)
            pe.matmul(b[:, E:2 * E], ones[:, :], chosen[:, 0, :], start=True, stop=False)
            pe.matmul(b[:, E:2 * E], before[:, :], chosen[:, 1, :], start=False, stop=True)
            pe.matmul(b[:, 2 * E:3 * E], ones[:, :], chosen[:, 0, :], start=True, stop=False)
            pe.matmul(b[:, 2 * E:3 * E], ones[:, :], chosen[:, 1, :], start=False, stop=True) \
                .then_inc(job_done, 1)
            experts(0)
            more = pe.value_load(flag[0:1, 0:1])
            with pe.If(more > 0):
                experts(1)

        @block.scalar
        def _(act):
            def copy(o, i):
                return act.activation(o, i, ACT.Copy)

            def row(v, n):
                return v.rearrange("(a n) -> a n", a=1).to_broadcast([P, n])

            def load_gain(v):
                act.dma_start(gain[:, :], row(v, D)).then_inc(loaded_gain, 16)

            def load_layer_gains(layer):
                act.dma_start(cgain[:, 0:CQ], row(a["mla_q_norm"][layer], CQ)).then_inc(loaded_cgain, 16)
                act.dma_start(cgain[:, CQ:], row(a["mla_kv_norm"][layer], CKV)).then_inc(loaded_cgain, 16)
                act.dma_start(sgain[:, :], row(a["diff_subln"][layer], 2 * DB)).then_inc(loaded_cgain, 16)

            def squares(which, t):
                if which == ("attn", 0):
                    act.wait_ge(loaded_x[t], 16)
                else:
                    act.wait_ge(residual_ready, norm_count(which, t) - T)
                act.activation(hn[:, t, :], h[:, t, :], ACT.Square,
                               accum_out=stat[:, norm_count(which, t) - 1, 0:1]).then_inc(squares_ready, 1)

            def split_hi(part, shift, half, final=False, rounds=0):
                n, kind, use = part_source(part, half, final)
                if n == 0:
                    arrived(act, use, rounds)
                if isinstance(shift, int) and part < PARTS:
                    pass
                else:
                    act.wait_ge(part_used, shift + (part - PARTS + 1))
                copy(part_buffers(part)[0], part_view(n, kind, use)).then_inc(hi_done, 1)

            def turn_evac(key, item):
                b = job(act, key)
                _, t, i = item
                if key[0:2] == (0, "XF"):
                    copy(hnT_hi[:, 4 * i:4 * i + 4, t * P:(t + 1) * P], b[:, :].rearrange("p (k s) -> p k s", k=4)) \
                        .then_inc(hnT_hi_ready, 1)
                    return
                copy(hnT[:, 4 * i:4 * i + 4, t * P:(t + 1) * P], b[:, :].rearrange("p (k s) -> p k s", k=4)) \
                    .then_inc(out_of(key), 1)

            load_gain(a["attn_norm"][0])
            with nc.allow_non_contiguous_dma(reason="the positions, one to a partition"):
                act.dma_start(pos_i, positions.rearrange("a (t p) -> p (a t)", p=P)).then_inc(loaded_small, 16)
            act.dma_start(freq[:, :], row(a["rope_freq"], NF)).then_inc(loaded_small, 16)
            for i, name in enumerate(("q1", "k1", "q2", "k2")):
                v = a[f"diff_lambda_{name}"]
                act.dma_start(lamv[:, :, i, :], v.unsqueeze(0).to_broadcast([P, DEPTH, DB])).then_inc(loaded_small, 16)
            load_layer_gains(0)
            act.wait_ge(angles_ready, 1)
            act.activation(sin[:, :, :], ang, ACT.Sin).then_inc(trig_ready, 1)
            act.activation(cos[:, :, :], angc, ACT.Sin).then_inc(trig_ready, 1)
            act.wait_ge(lam_sums, 1)
            act.activation(lame, lams, ACT.Exp).then_inc(lam_exp, 1)

            def attention(layer):
                for item in ORDER:
                    name, key = item[0], (layer, *item)
                    if name == "N1":
                        squares(("attn", layer), item[1])
                    elif name == "NF1":
                        squares(("ffn", layer), item[1])
                    elif name in ("X", "OT", "XF"):
                        if item[2] == 0 or name == "XF" and layer == 0:
                            turn_evac(key, item)
                    elif item == ("WO", 0, 0):
                        for i in range(4):
                            split_hi((0, first_part(0))[layer] + i, 0, (None, 0)[layer])
                    elif name == "PC":
                        t = item[1]
                        b = job(act, key)
                        copy(pc[:, t, :], b[:, 0:416])
                        act.activation(qcT[:, 0, 0:CQ], b[:, 0:CQ], ACT.Square, accum_out=cstat[:, t, 0, 0:1])
                        act.activation(qcT[:, 1, 0:CKV], b[:, CQ:CQ + CKV], ACT.Square,
                                       accum_out=cstat[:, t, 0, 1:2]).then_inc(out_of(key), 1)
                        if t == T - 1:
                            act.wait_ge(normed, norm_count(("attn", layer), t))
                            load_gain(a["ffn_norm"][layer])
                    elif name == "PI":
                        b = job(act, key)
                        copy(pqi[:, item[1], 0:HI * DI], b[:, :]).then_inc(out_of(key), 1)
                    elif name == "PA":
                        b = job(act, key)
                        n = (HA + 1) * DA
                        copy(pa[:, item[1], 0:n], b[:, 0:n])
                        copy(pa[:, item[1], n + DA:n + 2 * DA], b[:, n:n + DA]).then_inc(out_of(key), 1)
                    elif name == "IT":
                        b = job(act, key)
                        t = item[1]
                        copy(qiT[:, :, t * P:(t + 1) * P], b[:, :].rearrange("p (k s) -> p k s", k=4)) \
                            .then_inc(out_of(key), 1)
                    elif name in ("BT", "AT"):
                        t = item[1]
                        b = job(act, key)
                        dst, n, scale = (bT, 4, DB ** -0.5) if name == "BT" else (aT, 3, DA ** -0.5)
                        v = b[:, 0:n * P].rearrange("p (k s) -> p k s", k=n)
                        act.mul(dst[:, 0:2, t * P:(t + 1) * P], v[:, 0:2, :], scale)
                        copy(dst[:, 2:n, t * P:(t + 1) * P], v[:, 2:n, :]).then_inc(out_of(key), 1)
                    elif name == "QC":
                        i = item[2]
                        b = job(act, key)
                        act.mul(qc[:, 4 * i:4 * i + 4, :], b[:, 0:4 * DC].rearrange("p (h d) -> p h d", h=4),
                                DC ** -0.5).then_inc(out_of(key), 1)
                    elif name == "MQ":
                        _, t, i = item
                        b = job(act, key)
                        copy(qcT[0:DC, 4 * i:4 * i + 4, t * P:(t + 1) * P],
                             b[0:DC, :].rearrange("p (k s) -> p k s", k=4)).then_inc(out_of(key), 1)
                    elif name == "U":
                        n = item[1]
                        kind, t, p = UNITS[n]
                        nk = keys(t)
                        if kind == "idx":
                            act.wait_ge(logits_ready, layer * NU + n + 1)
                            if n >= 2:
                                act.wait_ge(index_added, layer * NI + n - 1)
                            act.activation(prob[:, n % 2, :, 0:nk], pair[n % 2][:, :, 0:nk], ACT.Relu) \
                                .then_inc(relu_done, 1)
                        else:
                            act.wait_ge(max_ready, layer * NE + EXPS[n])
                            for m in range(2):
                                src = prob[:, n % 2, m, 0:nk] if kind == "dsa" else pair[n % 2][:, m, 0:nk]
                                last = act.activation(prob[:, n % 2, m, 0:nk], src, ACT.Exp,
                                                      bias=nmax[:, n, m:m + 1], accum_out=lsum[:, n, m:m + 1])
                            last.then_inc(exp_done, 1)
                    elif name == "TP" and UNITS[item[1]][0] != "mla":
                        n = item[1]
                        blocks = (UNITS[n][1] + 1) * (1 if UNITS[n][0] == "diff" else 2)
                        b = job(act, key)
                        copy(pt[:, n % 2, 0:blocks, :], b[:, 0:blocks * P].rearrange("p (k s) -> p k s", k=blocks)) \
                            .then_inc(out_of(key), 1)

            def silu(half, step, t, used):
                act.wait_ge(part_used, used)
                before = T if half == 0 and isinstance(step, int) and step < DENSE_STEPS else 1
                if not (isinstance(step, int) and step < before):
                    act.wait_ge(hid_ready[half], step - (before - 1))
                act.activation(sg[:, t, :], gate_bank[t], ACT.Silu).then_inc(silu_ready[half], 1)

            def hidden_turned(half, step, t, b):
                act.wait_ge(tr_done[half], step + 1)
                copy(hidT_hi[:, t, :, :], b.rearrange("p (k s) -> p k s", k=4)).then_inc(hidT_hi_ready[half], 1)

            def dense():
                for i in range(2):
                    turn_evac((0, "XF", 1, i), ("XF", 1, i))
                for n in range(4, PARTS):
                    split_hi(n, 0, None)
                base = -4
                for j in range(NCH + 1):
                    at = base + 4 if j == 0 else base

                    def parts(first, last):
                        for n in range(first, last + 1):
                            if at + n < FFN_PARTS:
                                split_hi(at + n, 0, None)

                    if j < NCH:
                        parts(7, 9)
                        for t in range(T):
                            silu(0, T * j + t, t, at + 4)
                    parts(10, 10) if j < NCH else None
                    if j:
                        for t in range(T):
                            hidden_turned(0, T * (j - 1) + t, t, dense_turn[t])
                    if j < NCH:
                        parts(11, 18 if j else 14)
                    if j == 0:
                        act.wait_ge(normed, norm_count(("ffn", 0), 1))
                        load_gain(a["attn_norm"][1])
                        act.wait_ge(d_normed, T)
                        load_layer_gains(1)
                    base += 12

            def experts(half):
                s0, part0 = first_step(half), first_part(half)

                def rows_taken(n):
                    act.wait_ge(xt_done[half], n)
                    for i in range(2):
                        copy(xT_hi[:, 4 * i:4 * i + 4, :], x_bank[i].rearrange("p (k s) -> p k s", k=4)) \
                            .then_inc(xT_hi_ready[half], 1)

                def chunk(j, n, step, part, shift, ahead, more, rounds):
                    def parts(first, final):
                        for i in range(first, final + 1):
                            if more or part + i < part0 + E * FFN_PARTS:
                                split_hi(part + i, shift, half, not more, rounds)

                    if ahead:
                        parts(7, 9)
                        silu(half, step, 0, shift + (part + 4))
                        parts(10, 10)
                    hidden_turned(half, step - 1, 0, tr_bank)
                    if ahead:
                        parts(11, 14)
                    if j == GATES_AT:
                        act.wait_ge(gsel_turned[half], n)
                        copy(gselT, sel_bank[:, 0:T * P].rearrange("p (t n) -> p t n", t=T)) \
                            .then_inc(gselT_ready[half], 1)
                    if j == NCH - 1 and more:
                        act.wait_ge(part_used, shift + (part + 8))
                        rows_taken(n + 1)
                    if ahead:
                        parts(15, 17)
                    if j == NCH:
                        act.wait_ge(part_used, shift + (part + (12 if ahead else 4)))
                        for c in range(2):
                            copy(yrow[:, 512 * c:512 * c + 512], down_bank[c]).then_inc(y_ready[half], 1)
                    if ahead:
                        parts(18, 18)

                def start(first, final):
                    for n in range(first, final + 1):
                        split_hi(part0 + n, 0, half)

                start(4 if half == 0 else 0, 6)
                rows_taken(1)
                start(7, 9)
                silu(half, s0, 0, part0 + 4)
                start(10, 14)
                for place in opening(half):
                    chunk(*place, 0)
                with act.Fori(0, E - 1) as e:
                    for place in places(half, e, False):
                        chunk(*place, 16 * (PER_EXPERT // RING) * e)
                for place in places(half, E - 1, True):
                    chunk(*place, 0)

            attention(0)
            dense()
            attention(1)
            act.wait_ge(normed, norm_count(("ffn", 1), 1))
            load_gain(a["final_norm"])
            act.dma_start(router, a["moe_router"][0].rearrange("(k p) e -> p k e", p=P)).then_inc(loaded_router, 16)
            turn_evac((1, "XF", 1, 0), ("XF", 1, 0))
            act.wait_ge(gates_in, 1)
            act.activation(gate[:, 1, :], gate[:, 0, :], ACT.Exp).then_inc(gates_exp, 1)
            experts(0)
            more = act.value_load(flag[0:1, 0:1])
            with act.If(more > 0):
                experts(1)
            for t in range(T):
                squares(("final", 1), t)

        @block.vector
        def _(dve):
            chained = [0]

            def link(ins):
                chained[0] += 1
                ins.then_inc(dve_chain, 1)
                dve.wait_ge(dve_chain, chained[0])

            def scalar2(o, i, s1, s2, op0, op1):
                return dve.tensor_scalar(o, i, s1, s2, op0, op1)

            def mean(which, t):
                i = norm_count(which, t)
                dve.wait_ge(squares_ready, i)
                scalar2(stat[:, i - 1, 1:2], stat[:, i - 1, 0:1], 1.0 / D, EPS, ALU.mult, ALU.add) \
                    .then_inc(mean_ready, 1)

            def norm(which, t):
                i = norm_count(which, t)
                dve.wait_ge(rms_ready, i)
                if t == 0:
                    dve.wait_ge(loaded_gain, 16 * (NORMS.index(which) + 1))
                return dve.scalar_tensor_tensor(out=hn[:, t, :], in0=h[:, t, :], scalar=stat[:, i - 1, 0:1],
                                                in1=gain[:, :], op0=ALU.mult, op1=ALU.mult)

            def split_lo(part, shift, half, final=False):
                n, kind, use = part_source(part, half, final)
                hi, lo = part_buffers(part)
                dve.wait_ge(hi_done, shift + (part + 1))
                dve.tensor_tensor(lo, part_view(n, kind, use), hi.bitcast(F32), ALU.subtract) \
                    .then_inc(lo_done, 1)

            def turn_evac(key, item):
                b = job(dve, key)
                _, t, i = item
                if key[0:2] == (0, "XF"):
                    dve.wait_ge(hnT_hi_ready, 2 * t + i + 1)
                    part = (slice(None), slice(4 * i, 4 * i + 4), slice(t * P, (t + 1) * P))
                    dve.tensor_tensor(hnT_lo[part], b[:, :].rearrange("p (k s) -> p k s", k=4),
                                      hnT_hi[part].bitcast(F32), ALU.subtract).then_inc(out_of(key), 1)
                    return
                dve.tensor_copy(hnT[:, 4 * i:4 * i + 4, t * P:(t + 1) * P],
                                b[:, :].rearrange("p (k s) -> p k s", k=4)).then_inc(out_of(key), 1)

            dve.wait_ge(loaded_small, 16 * 6)
            link(dve.tensor_copy(pos_f, pos_i))
            for t in range(T):
                last = dve.tensor_scalar(ang[:, t, :], freq[:, :], pos_f[:, t:t + 1], None, ALU.mult)
            link(last)
            link(scalar2(turns, ang, 1.0 / TWO_PI, ROUND, ALU.mult, ALU.add))
            link(dve.tensor_scalar(turns, turns, ROUND, None, ALU.subtract))
            for part in PI_PARTS:
                link(dve.scalar_tensor_tensor(out=ang, in0=turns, scalar=-part, in1=ang,
                                              op0=ALU.mult, op1=ALU.add))
            link(dve.tensor_scalar(angc, ang, math.pi / 2, None, ALU.add))
            link(scalar2(turns, angc, math.pi, -TWO_PI, ALU.is_gt, ALU.mult))
            link(dve.tensor_tensor(angc, angc, turns, ALU.add))
            link(scalar2(angc, angc, 3.1415925, -3.1415925, ALU.min, ALU.max))
            scalar2(ang, ang, 3.1415925, -3.1415925, ALU.min, ALU.max).then_inc(angles_ready, 1)
            link(dve.tensor_tensor(lamp, lamv[:, :, 0:4:2, :], lamv[:, :, 1:4:2, :], ALU.mult))
            dve.tensor_reduce(lams, lamp, AX.X, ALU.add).then_inc(lam_sums, 1)
            dve.wait_ge(lam_exp, 1)
            for layer in range(DEPTH):
                link(dve.tensor_tensor(lam[:, layer:layer + 1], lame[:, layer, 0:1], lame[:, layer, 1:2],
                                       ALU.subtract))
                link(dve.tensor_scalar(lam[:, layer:layer + 1], lam[:, layer:layer + 1],
                                       LAM_INIT[layer], None, ALU.add))

            def index_unit(layer, n):
                _, t, p = UNITS[n]
                nk = keys(t)
                dve.wait_ge(relu_done, layer * NI + n + 1)
                acc = score[:, t, 0:nk]
                for m in range(2):
                    i = 2 * p + m
                    rel = prob[:, n % 2, m, 0:nk]
                    if i == 0:
                        ins = dve.tensor_scalar(acc, rel, wi[:, t, 0:1], None, ALU.mult)
                    else:
                        ins = dve.scalar_tensor_tensor(out=acc, in0=rel, scalar=wi[:, t, i:i + 1], in1=acc,
                                                       op0=ALU.mult, op1=ALU.add)
                    if m == 0:
                        link(ins)
                ins.then_inc(index_added, 1)
                dve.wait_ge(index_added, layer * NI + n + 1)
                if p == IDXP - 1:
                    dve.tensor_scalar(score[:, t, 0:nk - CHUNK], score[:, t, 0:nk - CHUNK], IDX_SCALE, None,
                                      ALU.mult)
                    link(dve.scalar_tensor_tensor(out=score[:, t, nk - CHUNK:nk], in0=score[:, t, nk - CHUNK:nk],
                                                  scalar=IDX_SCALE, in1=neg_chunk[:, :], op0=ALU.mult,
                                                  op1=ALU.add))

            def select_round(t, r):
                v = score[:, t, 0:keys(t)]
                link(dve.max(top8[:, :], v))
                link(dve.match_replace(out=v, in_to_replace=top8[:, :], in_values=v, imm_value=TAKEN))
                if r == TOPK // 8 - 1:
                    link(scalar2(v, v, 0.5 * TAKEN, MASKED, ALU.is_gt, ALU.mult))

            def unit_max(layer, n):
                kind, t, p = UNITS[n]
                nk = keys(t)
                dve.wait_ge(logits_ready, layer * NU + n + 1)
                src = pair[n % 2][:, :, 0:nk]
                if kind == "dsa":
                    dst = prob[:, n % 2, :, 0:nk]
                    link(dve.tensor_tensor(dst, src, bc(score[:, t, 0:nk], [P, 2, nk]), ALU.add))
                    src = dst
                dve.tensor_reduce(nmax[:, n, :], src, AX.X, ALU.max, negate=True).then_inc(max_ready, 1)

            def attention(layer):
                rounds = []
                for item in ORDER:
                    name, key = item[0], (layer, *item)
                    if name == "N1":
                        mean(("attn", layer), item[1])
                    elif name == "N2":
                        norm(("attn", layer), item[1]).then_inc(normed, 1)
                    elif name == "NF1":
                        mean(("ffn", layer), item[1])
                    elif name == "NF2":
                        norm(("ffn", layer), item[1]).then_inc(normed, 1)
                    elif name in ("X", "OT", "XF"):
                        if item[2] == 1 or name == "XF" and layer == 0:
                            turn_evac(key, item)
                    elif name == "PI":
                        t = item[1]
                        emptied(dve, (layer, "PC", t))
                        scalar2(cstat[:, t, 1, 0:1], cstat[:, t, 0, 0:1], 1.0 / CQ, EPS, ALU.mult, ALU.add)
                        scalar2(cstat[:, t, 1, 1:2], cstat[:, t, 0, 1:2], 1.0 / CKV, EPS, ALU.mult, ALU.add) \
                            .then_inc(c_mean, 1)
                    elif name == "PK":
                        t = item[1]
                        b = job(dve, key)
                        dve.tensor_copy(pqi[:, t, HI * DI:(HI + 1) * DI], b[:, 0:DI])
                        dve.tensor_copy(wi[:, t, :], b[:, DI:DI + HI])
                        dve.tensor_copy(pb[:, t, 0:256], b[:, DI + HI:DI + HI + 256]).then_inc(out_of(key), 1)
                    elif name == "C2":
                        t = item[1]
                        dve.wait_ge(c_rms, layer * T + t + 1)
                        dve.wait_ge(loaded_cgain, 48 * (layer + 1))
                        for i, (c0, c1) in enumerate(((0, CQ), (CQ, CQ + CKV))):
                            last = dve.scalar_tensor_tensor(out=pc[:, t, c0:c1], in0=pc[:, t, c0:c1],
                                                            scalar=cstat[:, t, 0, i:i + 1], in1=cgain[:, c0:c1],
                                                            op0=ALU.mult, op1=ALU.mult)
                        last.then_inc(c_normed, 1)
                        if t == 0:
                            link(dve.tensor_scalar(sgain[:, :], sgain[:, :], 1.0 - LAM_INIT[layer], None, ALU.mult))
                    elif name == "CT":
                        b = job(dve, key)
                        t = item[1]
                        dve.tensor_copy(cT[:, :, t * P:(t + 1) * P], b[:, 0:3 * P].rearrange("p (k s) -> p k s", k=3)) \
                            .then_inc(out_of(key), 1)
                    elif name == "KIT":
                        b = job(dve, key)
                        t = item[1]
                        dve.tensor_copy(kiT[:, t * P:(t + 1) * P], b[:, 0:P]).then_inc(out_of(key), 1)
                    elif name == "PB":
                        b = job(dve, key)
                        dve.tensor_copy(pb[:, item[1], 256:768], b[:, :]).then_inc(out_of(key), 1)
                    elif name == "KV":
                        _, t, i = item
                        b = job(dve, key)
                        v = b[:, :].rearrange("p (h d) -> p h d", h=4)
                        dve.tensor_copy(kc[:, 4 * i:4 * i + 4, 0:DN], v[:, :, 0:DN])
                        dve.tensor_copy(vc[:, t, 4 * i * DV:4 * (i + 1) * DV].rearrange("p (h d) -> p h d", h=4),
                                        v[:, :, DN:]).then_inc(out_of(key), 1)
                    elif name == "MK":
                        _, t, i = item
                        b = job(dve, key)
                        dve.tensor_copy(kcT[0:DC, 4 * i:4 * i + 4, t * P:(t + 1) * P],
                                        b[0:DC, :].rearrange("p (k s) -> p k s", k=4)).then_inc(out_of(key), 1)
                    elif name == "U":
                        n = item[1]
                        if UNITS[n][0] == "idx":
                            index_unit(layer, n)
                            if UNITS[n][2] == IDXP - 1:
                                rounds += [(UNITS[n][1], r) for r in range(TOPK // 8)]
                        else:
                            unit_max(layer, n)
                    elif name == "TP":
                        n = item[1]
                        kind, t, p = UNITS[n]
                        nk = keys(t)
                        dve.wait_ge(exp_done, layer * NE + EXPS[n])
                        link(dve.reciprocal(rsum[:, n, :], lsum[:, n, :]))
                        if kind == "diff":
                            p0, p1 = prob[:, n % 2, 0, 0:nk], prob[:, n % 2, 1, 0:nk]
                            link(scalar2(p1, p1, rsum[:, n, 1:2], lam[:, layer:layer + 1], ALU.mult, ALU.mult))
                            dve.scalar_tensor_tensor(out=p0, in0=p0, scalar=rsum[:, n, 0:1], in1=p1,
                                                     op0=ALU.mult, op1=ALU.subtract).then_inc(combined, 1)
                        elif kind == "mla":
                            b = job(dve, key)
                            blocks = 2 * (t + 1)
                            dve.tensor_copy(pt[:, n % 2, 0:blocks, :],
                                            b[:, 0:blocks * P].rearrange("p (k s) -> p k s", k=blocks)) \
                                .then_inc(out_of(key), 1)
                    elif name == "O":
                        n = item[1]
                        kind, t, p = UNITS[n]
                        b = job(dve, key)
                        if kind == "diff":
                            dve.tensor_copy(hn[:, t, 256 + 64 * p:320 + 64 * p], b[:, 0:64]).then_inc(out_of(key), 1)
                        else:
                            at = (512 if kind == "mla" else 0) + 128 * p
                            dve.tensor_tensor(hn[:, t, at:at + 128].rearrange("p (m d) -> p m d", m=2),
                                              b[:, 0:128].rearrange("p (m d) -> p m d", m=2),
                                              rsum[:, n, :].unsqueeze(2).to_broadcast([P, 2, 64]), ALU.mult) \
                                .then_inc(out_of(key), 1)
                    elif name == "D1":
                        t = item[1]
                        o = hn[:, t, 256:512]
                        last_o = max(n for n in DIFFS if UNITS[n][1] == t)
                        emptied(dve, (layer, "O", last_o))
                        link(dve.tensor_tensor(kiT, o, o, ALU.mult))
                        link(dve.tensor_reduce(dstat[:, t, 0, :], kiT.rearrange("p (h d) -> p h d", h=HB), AX.X, ALU.add))
                        scalar2(dstat[:, t, 1, :], dstat[:, t, 0, :], 1.0 / (2 * DB), EPS, ALU.mult, ALU.add) \
                            .then_inc(d_mean, 1)
                    elif name == "D2":
                        t = item[1]
                        o = hn[:, t, 256:512].rearrange("p (h d) -> p h d", h=HB)
                        dve.wait_ge(d_rms, layer * T + t + 1)
                        link(dve.tensor_tensor(o, o, dstat[:, t, 0, :].unsqueeze(2).to_broadcast([P, HB, 2 * DB]),
                                               ALU.mult))
                        dve.tensor_tensor(o, o, bc(sgain[:, :], [P, HB, 2 * DB]), ALU.mult).then_inc(d_normed, 1)
                    elif name == "WO":
                        _, t, half = item
                        if (t, half) == (0, 0):
                            for i in range(4):
                                split_lo((0, first_part(0))[layer] + i, 0, (None, 0)[layer])
                        b = job(dve, key)
                        v = h[:, t, 512 * half:512 * half + 512]
                        dve.tensor_tensor(v, v, b[:, :], ALU.add).then_inc(out_of(key), 1)
                        if half == 1:
                            emptied(dve, key)
                            dve.sem_inc(residual_ready, 1)
                    if rounds and name in ("U", "TP", "O", "QC", "KV", "BT"):
                        select_round(*rounds.pop(0))
                assert not rounds

            def hidden(half, step, t, used):
                dve.wait_ge(part_used, used)
                dve.wait_ge(silu_ready[half], step + 1)
                dve.tensor_tensor(hid[:, t, :], up_bank[t], sg[:, t, :], ALU.mult).then_inc(hid_ready[half], 1)

            def hidden_turned(half, step, t, b):
                dve.wait_ge(hidT_hi_ready[half], step + 1)
                dve.tensor_tensor(hidT_lo[:, t, :, :], b.rearrange("p (k s) -> p k s", k=4),
                                  hidT_hi[:, t, :, :].bitcast(F32), ALU.subtract).then_inc(hidT_ready[half], 1)

            def dense():
                for i in range(2):
                    turn_evac((0, "XF", 1, i), ("XF", 1, i))
                for n in range(4, PARTS):
                    split_lo(n, 0, None)
                base = -4
                for j in range(NCH + 1):
                    at = base + 4 if j == 0 else base

                    def parts(first, last):
                        for n in range(first, last + 1):
                            if j < NCH and at + n < FFN_PARTS:
                                split_lo(at + n, 0, None)

                    def add_down(c, used):
                        dve.wait_ge(part_used, used)
                        for t in range(T):
                            v = h[:, t, 512 * c:512 * c + 512]
                            dve.tensor_tensor(v, v, dense_down[c][t], ALU.add).then_inc(dense_added, 1)

                    down_at = at + (8 if j < NCH else 0)
                    parts(7, 10)
                    if j:
                        for t in range(T):
                            hidden_turned(0, T * (j - 1) + t, t, dense_turn[t])
                    parts(11, 13)
                    if j < NCH:
                        for t in range(T):
                            hidden(0, T * j + t, t, at + 8)
                    parts(14, 16 if j else 14)
                    if j:
                        add_down(0, down_at + 2)
                        parts(17, 18)
                        add_down(1, down_at + 4)
                    base += 12
                for t in range(T):
                    dve.wait_ge(dense_added, 4 * NCH - 1 + t)
                    dve.sem_inc(residual_ready, 1)

            def experts(half):
                s0, part0 = first_step(half), first_part(half)

                def rows_taken(n):
                    for i in range(2):
                        dve.wait_ge(xT_hi_ready[half], 2 * n + (i - 1))
                        dve.tensor_tensor(xT_lo[:, 4 * i:4 * i + 4, :], x_bank[i].rearrange("p (k s) -> p k s", k=4),
                                          xT_hi[:, 4 * i:4 * i + 4, :].bitcast(F32), ALU.subtract) \
                            .then_inc(xT_ready[half], 1)

                def of_expert(table, e):
                    v = table[:, e, :] if isinstance(e, int) else table[:, bass.ds(e, 1), :].rearrange("p a t -> p (a t)")
                    return v.unsqueeze(2).to_broadcast([P, T, P])

                def find_rows(e):
                    return dve.tensor_tensor(sel, of_expert(place, e), bc(slots[:, half, :], [P, T, P]), ALU.is_equal)

                def find_gates(e):
                    link_loop(dve.tensor_tensor(gsel, of_expert(place, e), bc(slots[:, half, :], [P, T, P]), ALU.is_equal),
                              e)
                    dve.tensor_tensor(gsel, gsel, of_expert(share, e), ALU.mult).then_inc(gsel_ready[half], 1)

                def link_loop(ins, e):
                    ins.then_inc(gsel_found[half], 1)
                    dve.wait_ge(gsel_found[half], e + 1)

                def add_result(n, t):
                    for c in range(2):
                        dve.wait_ge(spread_done[half], n * 4 + (2 * t + c - 3))
                        v = h[:, t, 512 * c:512 * c + 512]
                        dve.tensor_tensor(v, v, x_bank[c], ALU.add).then_inc(added[half], 1)

                def chunk(j, n, step, part, shift, ahead, more, e=None):
                    def parts(first, final):
                        for i in range(first, final + 1):
                            if more or part + i < part0 + E * FFN_PARTS:
                                split_lo(part + i, shift, half, not more)

                    if j == ROWS_AT and more:
                        find_rows(e + 1).then_inc(sel_ready[half], 1)
                    if j == GATES_AT:
                        find_gates(e)
                    if ahead:
                        parts(7, 10)
                    hidden_turned(half, step - 1, 0, tr_bank)
                    if ahead:
                        parts(11, 13)
                        hidden(half, step, 0, shift + (part + 8))
                        parts(14, 14)
                    if j == NCH - 1 and more:
                        rows_taken(n + 1)
                    if ahead:
                        parts(15, 18)

                def start(first, final):
                    for n in range(first, final + 1):
                        split_lo(part0 + n, 0, half)

                find_rows(0).then_inc(sel_ready[half], 1)
                start(4 if half == 0 else 0, 6)
                rows_taken(1)
                start(7, 13)
                hidden(half, s0, 0, part0 + 8)
                start(14, 14)
                for place_ in opening(half):
                    chunk(*place_)
                with dve.Fori(0, E - 1) as e:
                    for place_ in places(half, e, False):
                        chunk(*place_, e)
                        if place_[0] in (1, 2):
                            add_result(place_[1] - 1, place_[0] - 1)
                for place_ in places(half, E - 1, True):
                    chunk(*place_, E - 1)
                for t in range(T):
                    add_result(E, t)
                dve.wait_ge(added[half], 4 * E)

            def route():
                for t in range(T):
                    b = job(dve, ("RT", t))
                    dve.tensor_copy(lg[:, t, :], b[:, 0:E]).then_inc(out_of(("RT", t)), 1)
                emptied(dve, ("RT", 0))
                emptied(dve, ("RT", 1))
                dve.wait_ge(consts_ready, 2)
                shape = [P, T, E]
                left = lg
                for k in range(2):
                    link(dve.tensor_reduce(best[:, k, :], left, AX.X, ALU.max))
                    link(dve.tensor_tensor(eq, left, best[:, k, :].unsqueeze(2).to_broadcast(shape), ALU.is_equal))
                    link(dve.tensor_tensor(eq, eq, bc(falling, shape), ALU.mult))
                    link(dve.tensor_reduce(first[:, k, :], eq, AX.X, ALU.max))
                    link(dve.tensor_tensor(pick[k], bc(falling, shape),
                                           first[:, k, :].unsqueeze(2).to_broadcast(shape), ALU.is_equal))
                    if k == 0:
                        link(dve.scalar_tensor_tensor(out=lg2, in0=pick[0], scalar=TAKEN, in1=lg,
                                                      op0=ALU.mult, op1=ALU.add))
                        left = lg2
                link(dve.tensor_tensor(chosen, pick[0], pick[1], ALU.add))
                dve.tensor_tensor(gate[:, 0, :], best[:, 1, :], best[:, 0, :], ALU.subtract).then_inc(gates_in, 1)
                dve.sem_inc(chosen_ready, 1)
                dve.wait_ge(gates_exp, 1)
                link(dve.tensor_scalar(gate[:, 0, :], gate[:, 1, :], 1.0, None, ALU.add))
                link(dve.reciprocal(gate[:, 0, :], gate[:, 0, :]))
                link(dve.tensor_tensor(gate[:, 1, :], gate[:, 1, :], gate[:, 0, :], ALU.mult))
                b = job(dve, ("POS",))
                dve.tensor_copy(rank, b[:, 0:3 * E].rearrange("p (t e) -> p t e", t=3)).then_inc(out_of(("POS",)), 1)
                emptied(dve, ("POS",))
                link(dve.tensor_reduce(most, rank[:, 2, :], AX.X, ALU.max))
                link(dve.tensor_scalar(flag, most, P + 0.5, None, ALU.is_gt))
                dve.sem_inc(routed, 1)
                by_token = place.rearrange("p e t -> p t e")
                link(dve.scalar_tensor_tensor(out=eq, in0=rank[:, 0:T, :], scalar=1.0, in1=chosen,
                                              op0=ALU.add, op1=ALU.mult))
                link(dve.tensor_scalar(by_token, eq, -1.0, None, ALU.add))
                link(dve.tensor_tensor(spread, pick[0], gate[:, 0, :].unsqueeze(2).to_broadcast(shape), ALU.mult))
                link(dve.tensor_tensor(eq, pick[1], gate[:, 1, :].unsqueeze(2).to_broadcast(shape), ALU.mult))
                link(dve.tensor_tensor(share.rearrange("p e t -> p t e"), spread, eq, ALU.add))

            attention(0)
            dense()
            attention(1)
            turn_evac((1, "XF", 1, 1), ("XF", 1, 1))
            route()
            experts(0)
            more = dve.value_load(flag[0:1, 0:1])
            with dve.If(more > 0):
                experts(1)
            for t in range(T):
                dve.sem_inc(residual_ready, 1)
            for t in range(T):
                mean(("final", 1), t)
            for t in range(T):
                norm(("final", 1), t).then_inc(out_ready, 1)


_INS = ("x", "positions", "attn_norm", "w_in", "mla_q_norm", "w_uq", "mla_kv_norm", "w_ukv",
        "diff_lambda_q1", "diff_lambda_k1", "diff_lambda_q2", "diff_lambda_k2", "diff_subln", "w_out",
        "ffn_norm", "dense_w_gate", "dense_w_up", "dense_w_down", "moe_router", "moe_w_gate",
        "moe_w_up", "moe_w_down", "final_norm")


def kernel(**inputs):
    import numpy as np
    import concourse.bacc as bacc
    from concourse.bass_utils import run_bass_kernel_spmd

    nc = bacc.Bacc("TRN2", target_bir_lowering=False, num_devices=1)
    arrays = {n: np.ascontiguousarray(inputs[n]) for n in _INS}
    arrays["rope_freq"] = (THETA ** (-np.arange(16) / 16.0)).astype(np.float32)
    args = {n: nc.dram_tensor(f"in_{n}", v.shape, mybir.dt.from_np(v.dtype), kind="ExternalInput").ap()
            for n, v in arrays.items()}
    out = nc.dram_tensor("out_0", arrays["x"].shape, F32, kind="ExternalOutput").ap()
    hybrid_block(nc, args, out)
    r = run_bass_kernel_spmd(nc, [{f"in_{n}": v for n, v in arrays.items()}], core_ids=[0])
    return r.results[0]["out_0"]
```

```python
import math
from contextlib import ExitStack

import concourse.bass as bass
from concourse import mybir
from concourse.alu_op_type import AluOpType as ALU

F32 = mybir.dt.float32
F32R = mybir.dt.float32r
BF16 = mybir.dt.bfloat16
I32 = mybir.dt.int32
ACT = mybir.ActivationFunctionType
AX = mybir.AxisListType

P = 128
CHUNK = 64
THETA = 500000.0
EPS = 1e-6
TWO_PI = 2.0 * math.pi
PI_PARTS = (6.28125, 1.9340515136718750e-03, 1.2554228305816650e-06)
PI_PARTS = PI_PARTS + (TWO_PI - sum(PI_PARTS),)
ROUND = 1.5 * 2.0 ** 23
MASKED = -(2.0 ** 100)
TAKEN = -3.0e38

RING = 3
SLOT = 4096
ARENA = 15808
FFN_ARENA = 7168
PARTS = 7
WBANKS = 4


def attention_order(layer, n_tiles, idx_units, units):
    T = range(n_tiles)
    if layer == 0:
        order = [(name, t) for name in ("N1", "N2") for t in T]
        order += [("X", t, i) for t in T for i in range(2)] + [("PC", t) for t in T]
    else:
        order = [("N1", 0), ("N2", 0), ("X", 0, 0), ("X", 0, 1), ("N1", 1), ("N2", 1), ("PC", 0),
                 ("X", 1, 0), ("X", 1, 1), ("PC", 1)]
    order += [(name, t) for name in ("PI", "C2", "PK") for t in T]
    order += [("CT", t) for t in T] + [("PA", t) for t in T]
    order += [(name, t) for t in T for name in ("IT", "KIT")]
    order += [("PB", 0), ("U", 0), ("U", 1), ("U", 2), ("PB", 1), ("U", 3), ("U", 4), ("U", 5)]
    order += [("QC", 0, 0), ("QC", 0, 1), ("U", 6), ("U", 7), ("KV", 0, 0), ("KV", 0, 1)]
    order += [("BT", t) for t in T]
    n0, n1 = idx_units, idx_units + units
    fills = {
        n0 + 3: [(name, 0, i) for name in ("MQ", "MK") for i in range(2)],
        n0 + 4: [(name, 1, i) for name in ("QC", "KV") for i in range(2)],
        n0 + 7: [(name, 1, i) for name in ("MQ", "MK") for i in range(2)],
        n0 + 8: [("D1", 0)], n0 + 10: [("D2", 0), ("AT", 0)], n0 + 11: [("AT", 1)],
        n0 + 12: [("D1", 1)], n0 + 14: [("D2", 1)],
    }
    for n in range(n0, n1 + 3):
        order += fills.get(n, [])
        if n0 <= n - 2 < n1:
            order.append(("CB", n - 2))
        if n < n1:
            order.append(("U", n))
        if n0 <= n - 2 < n1:
            order.append(("TP", n - 2))
        if n0 <= n - 3:
            order.append(("O", n - 3))
        if n == n1 + 1:
            order += [("OT", 0, 0), ("OT", 0, 1)]
    order += [("OT", 1, 0), ("OT", 1, 1), ("WO", 0, 0), ("WO", 1, 0),
              ("WO", 0, 1), ("NF1", 0), ("NF2", 0), ("WO", 1, 1), ("XF", 0, 0), ("XF", 0, 1),
              ("NF1", 1), ("NF2", 1)]
    return order


def hybrid_block(nc, a, out):
    x, positions = a["x"], a["positions"]
    S, D = x.shape[1], x.shape[2]
    DEPTH, _, NIN = a["w_in"].shape
    T, KT = S // P, D // P
    HA, DA = 4, 64
    HI, DI = 8, 64
    TOPK = min(256, S // 4)
    LAM_INIT = [0.8 - 0.6 * math.exp(-0.3 * layer) for layer in range(DEPTH)]
    IDX_SCALE = (HI * DI) ** -0.5
    HB, DB = 4, 32
    HC, DN, DR, DV = 8, 64, 32, 64
    DC = DN + DR
    CQ, CKV = a["w_uq"].shape[1], a["w_ukv"].shape[1]
    NF = DR // 2
    FF = a["dense_w_gate"].shape[2]
    NCH = FF // 512
    E = a["moe_w_gate"].shape[1]
    assert T == 2 and D == 1024 and FF % 512 == 0 and DEPTH == 2
    assert 3 * NCH % RING == 0 and 12 * NCH % PARTS == 0

    widths = (HA * DA, DA, DA, HI * DI, DI, HI, HB * 2 * DB, HB * 2 * DB, HB * 2 * DB, CQ, CKV, DR)
    starts = [sum(widths[:i]) for i in range(len(widths) + 1)]
    q_a, k_a, v_a, q_i, k_i, w_i, q_b, k_b, v_b, c_q, c_kv, k_r, end = starts
    assert end == NIN
    PROJ = {"PC": (c_q, end), "PI": (q_i, k_i), "PK": (k_i, k_b), "PA": (q_a, q_i), "PB": (k_b, c_q)}

    IDXP = HI // 2
    index_units = [("idx", t, p) for t in (1, 0) for p in range(IDXP)]
    attention_units = [(kind, t, p) for kind, n in (("diff", HB), ("mla", HC // 2), ("dsa", HA // 2))
                       for t in range(T) for p in range(n)]
    UNITS = index_units + attention_units
    NU, NI = len(UNITS), len(index_units)
    ORDER = [attention_order(layer, T, NI, NU - NI) for layer in range(DEPTH)]

    NOT_JOBS = ("U", "CB", "N1", "N2", "C2", "D1", "D2", "NF1", "NF2")
    JOB = {}
    for layer in range(DEPTH):
        for item in ORDER[layer]:
            if item[0] not in NOT_JOBS:
                JOB[(layer, *item)] = len(JOB)
        if layer == DEPTH - 1:
            JOB[("RT", 0)] = len(JOB)
        for half in range(2):
            JOB[(layer, "XF", 1, half)] = len(JOB)
    JOB[("RT", 1)] = len(JOB)
    JOB[("POS",)] = len(JOB)

    DENSE_STEPS = NCH * T
    USE = {}
    for layer in range(DEPTH):
        for c in PROJ:
            USE[(layer, c)] = len(USE)
        for name in ("UP", "WO0", "WO1"):
            USE[(layer, name)] = len(USE)
        if layer == 0:
            for j in range(NCH + 1):
                for kind, jj in (("g", j), ("u", j), ("d", j - 1)):
                    if 0 <= jj < NCH:
                        USE[("dense", kind, jj)] = len(USE)
    MOE_USE = len(USE)
    PER_EXPERT = 3 * NCH
    SPLIT_SLOTS = [*PROJ, "WO0", "WO1"]
    LAYER_PARTS = 4 * len(SPLIT_SLOTS)
    FFN_PARTS = 4 * PER_EXPERT
    DENSE_PART = LAYER_PARTS
    LAYER_PART = (0, DENSE_PART + FFN_PARTS)
    MOE_PART = LAYER_PART[1] + LAYER_PARTS

    ctx = ExitStack()
    with ctx:
        def sb(name, shape, dt=F32):
            return ctx.enter_context(nc.sbuf_tensor(name, shape, dt))

        with nc.sbuf_tensor("arena", [P, ARENA], F32) as arena:
            pass
        with nc.sbuf_tensor("ffn_arena", [P, FFN_ARENA], F32) as ffn_arena:
            split = [nc.sbuf_tensor(name, [P, T, 4, P], F32R) for name in ("hidT_hi", "hidT_lo")]
            with split[0] as hidT_hi, split[1] as hidT_lo:
                pass
        arena_room = sb("arena_room", [P, ARENA])

        def sem(name):
            return ctx.enter_context(nc.semaphore(name))

        ring = sb("ring", [P, RING, SLOT])
        h = sb("h", [P, T, D])
        hn = sb("hn", [P, T, D])
        hnT_hi = sb("hnT_hi", [P, KT, S], F32R)
        hnT_lo = sb("hnT_lo", [P, KT, S], F32R)
        gain = sb("gain", [P, D])
        ident = sb("ident", [P, P])
        neg_chunk = sb("neg_chunk", [P, CHUNK])
        mask_q = sb("mask_q", [P, P], BF16)
        mask_k = sb("mask_k", [P, CHUNK], BF16)
        freq = sb("freq", [P, NF])
        cos = sb("cos", [P, T, NF])
        sin = sb("sin", [P, T, NF])
        cgain = sb("cgain", [P, CQ + CKV])
        sgain = sb("sgain", [P, 2 * DB])
        stat = sb("stat", [P, 2 * (2 * DEPTH + 1), 2])
        mhalf = sb("mhalf", [P, 4])
        cstat = sb("cstat", [P, T, 2, 2])
        dstat = sb("dstat", [P, T, 2, HB])
        lam = sb("lam", [P, DEPTH])
        nmax = sb("nmax", [P, NU, 2])
        lsum = sb("lsum", [P, NU, 2])
        top8 = sb("top8", [P, 8])
        wi = sb("wi", [P, T, HI])
        rope_c = sb("rope_c", [P, HC * DR])
        rope_s = sb("rope_s", [P, HC * DR])

        w_hi = sb("w_hi", [P, PARTS, 1024], F32R)
        w_lo = sb("w_lo", [P, PARTS, 1024], F32R)
        used = [0]

        def carve(n):
            at = used[0]
            used[0] += n
            assert used[0] <= ARENA, used[0]
            return arena[:, at:at + n]

        pa = carve(T * 448).rearrange("p (t n) -> p t n", t=T)
        both = carve(2 * HC * DC)
        pqi = both[:, 0:T * 640].rearrange("p (t n) -> p t n", t=T)
        qc = both[:, 0:HC * DC].rearrange("p (h d) -> p h d", h=HC)
        kc = both[:, HC * DC:2 * HC * DC].rearrange("p (h d) -> p h d", h=HC)
        pb = carve(T * 768).rearrange("p (t n) -> p t n", t=T)
        pc = carve(T * 416).rearrange("p (t n) -> p t n", t=T)
        vc = carve(T * HC * DV).rearrange("p (t n) -> p t n", t=T)
        cT = carve(3 * S).rearrange("p (k s) -> p k s", k=3)
        bT = carve(4 * S).rearrange("p (k s) -> p k s", k=4)
        aT = carve(3 * S).rearrange("p (k s) -> p k s", k=3)
        kiT = carve(S)
        qiT_or_pt = carve(4 * S)
        qiT = qiT_or_pt.rearrange("p (k s) -> p k s", k=4)
        pt = qiT_or_pt.rearrange("p (b k s) -> p b k s", b=2, k=4)
        qcT = carve(HC * S).rearrange("p (k s) -> p k s", k=HC)
        kcT = carve(HC * S).rearrange("p (k s) -> p k s", k=HC)
        prob = carve(3 * 2 * S).rearrange("p (b m s) -> p b m s", b=3, m=2)
        score = carve(T * S).rearrange("p (t s) -> p t s", t=T)
        lamv = qcT[:, 0, :].rearrange("p (l v d) -> p l v d", l=DEPTH, v=4)
        lamp = qcT[:, 1, 0:DEPTH * 2 * DB].rearrange("p (l v d) -> p l v d", l=DEPTH, v=2)
        lams = qcT[:, 2, 0:2 * DEPTH].rearrange("p (l v) -> p l v", l=DEPTH)
        lame = qcT[:, 2, 64:64 + 2 * DEPTH].rearrange("p (l v) -> p l v", l=DEPTH)
        pos_i = qcT[:, 3, 0:T].bitcast(I32)
        pos_f = qcT[:, 3, 64:64 + T]
        ang = qcT[:, 4, 0:T * NF].rearrange("p (t f) -> p t f", t=T)
        turns = qcT[:, 5, 0:T * NF].rearrange("p (t f) -> p t f", t=T)
        angc = qcT[:, 6, 0:T * NF].rearrange("p (t f) -> p t f", t=T)
        used[0] = 0
        sg = carve(T * 512).rearrange("p (t n) -> p t n", t=T)
        hid = carve(T * 512).rearrange("p (t n) -> p t n", t=T)
        yrow = carve(D)
        hnT = carve(KT * S).rearrange("p (k s) -> p k s", k=KT)
        router = carve(KT * E).rearrange("p (k e) -> p k e", k=KT)
        before = carve(P)
        ones = carve(P)
        lg = carve(T * E).rearrange("p (t e) -> p t e", t=T)
        lg2 = carve(T * E).rearrange("p (t e) -> p t e", t=T)
        top = carve(T * 8).rearrange("p (t n) -> p t n", t=T)
        total = carve(T)
        chosen = carve(T * E).rearrange("p (t e) -> p t e", t=T)
        rank = carve(3 * E).rearrange("p (t e) -> p t e", t=3)
        slots = carve(2 * P).rearrange("p (s n) -> p s n", s=2)
        place = carve(T * E).rearrange("p (e t) -> p e t", e=E)
        share = carve(T * E).rearrange("p (e t) -> p e t", e=E)
        sel = carve(T * P).rearrange("p (t n) -> p t n", t=T)
        gsel = carve(T * P).rearrange("p (t n) -> p t n", t=T)
        gselT = carve(T * P).rearrange("p (t n) -> p t n", t=T)
        most = carve(1)
        flag = carve(1).bitcast(I32)
        assert used[0] <= FFN_ARENA and FFN_ARENA + 2 * T * 4 * P <= ARENA
        xT_hi, xT_lo = hnT_hi[:, :, 0:P], hnT_lo[:, :, 0:P]

        pair = [ctx.enter_context(nc.psum_tensor(f"pair{i}", [P, 2, 512], F32)) for i in range(2)]
        work = [ctx.enter_context(nc.psum_tensor(f"work{i}", [P, 512], F32)) for i in range(WBANKS)]
        logit_bank = [pair[i // 2][:, i % 2, :].rearrange("p (m s) -> p m s", m=2) for i in range(4)]
        gate_bank = [pair[0][:, t, :] for t in range(T)]
        up_bank = [pair[1][:, t, :] for t in range(T)]
        early = JOB[(1, "X", 0, 0)] % WBANKS
        dense_down = [[work[(early + 2 * t + c) % WBANKS][:, :] for t in range(T)] for c in range(2)]
        last_down = [[dense_down[c][0], up_bank[c]] for c in range(2)]
        x_bank, down_bank = [work[0][:, :], work[1][:, :]], [work[2][:, :], work[3][:, :]]
        tr_bank, sel_bank = gate_bank[1], up_bank[1]
        spread_bank = [x_bank, x_bank]
        last_spread_bank = [x_bank, [gate_bank[0], up_bank[0]]]

        loaded_x = [sem(f"loaded_x{t}") for t in range(T)]
        loaded_ukv = sem("loaded_ukv")
        loaded_small = sem("loaded_small")
        loaded_gain = sem("loaded_gain")
        loaded_cgain = sem("loaded_cgain")
        loaded_router = sem("loaded_router")
        slot_full = [sem(f"slot_full{i}") for i in range(RING)]
        consts_ready = sem("consts_ready")
        pool_chain = sem("pool_chain")
        dve_chain = sem("dve_chain")
        angles_ready = sem("angles_ready")
        trig_ready = sem("trig_ready")
        lam_sums = sem("lam_sums")
        lam_exp = sem("lam_exp")
        residual_ready = sem("residual_ready")
        squares_ready = sem("squares_ready")
        mean_ready = sem("mean_ready")
        rms_ready = sem("rms_ready")
        normed = sem("normed")
        job_done = sem("job_done")
        evacuated = [sem(f"evacuated{i}") for i in range(WBANKS)]
        c_mean = sem("c_mean")
        c_rms = sem("c_rms")
        c_normed = sem("c_normed")
        roped = sem("roped")
        logits_ready = sem("logits_ready")
        relu_done = sem("relu_done")
        index_added = sem("index_added")
        max_ready = sem("max_ready")
        exp_done = sem("exp_done")
        combined = sem("combined")
        d_mean = sem("d_mean")
        d_rms = sem("d_rms")
        d_normed = sem("d_normed")
        tr_done, silu_ready, hid_ready, hidT_hi_ready, hidT_ready, sel_ready, xt_done, xT_hi_ready, \
            xT_ready, gsel_ready, gsel_turned, gselT_ready, y_ready, spread_done, added = (
                [sem(f"{n}{half}") for half in range(2)] for n in (
                    "tr_done", "silu_ready", "hid_ready", "hidT_hi_ready", "hidT_ready",
                    "sel_ready", "xt_done", "xT_hi_ready", "xT_ready", "gsel_ready", "gsel_turned",
                    "gselT_ready", "y_ready", "spread_done", "added"))
        hi_done = sem("hi_done")
        lo_done = sem("lo_done")
        part_used = sem("part_used")
        first_tile_down = sem("first_tile_down")
        gsel_found = [sem(f"gsel_found{half}") for half in range(2)]
        hnT_hi_ready = sem("hnT_hi_ready")
        dense_added = sem("dense_added")
        routed = sem("routed")
        chosen_ready = sem("chosen_ready")
        gates_in = sem("gates_in")
        gates_exp = sem("gates_exp")
        out_ready = sem("out_ready")
        stored = sem("stored")

        def job(eng, key):
            eng.wait_ge(job_done, JOB[key] + 1)
            return work[JOB[key] % WBANKS]

        def emptied(eng, key):
            eng.wait_ge(evacuated[JOB[key] % WBANKS], JOB[key] // WBANKS + 1)

        def out_of(key):
            return evacuated[JOB[key] % WBANKS]

        def slot(use):
            return ring[:, use % RING, :]

        def arrived(eng, use, rounds=0):
            eng.wait_ge(slot_full[use % RING], rounds + 16 * (use // RING + 1))

        def first_part(half):
            return MOE_PART + FFN_PARTS * E * half

        def used_up(part):
            return part + 1 - LAYER_PARTS * (1 if part < LAYER_PART[1] else 2)

        def part_view(n, kind, use):
            if kind < 2:
                return slot(use).rearrange("p (k n) -> p k n", k=KT)[:, 2 * n:2 * n + 2, :]
            c, k = n // 2, 2 * (n % 2)
            return slot(use).rearrange("p (k n) -> p k n", k=4)[:, k:k + 2, 512 * c:512 * c + 512]

        def part_buffers(part, n=512):
            return [w[:, part % PARTS, 0:2 * n].rearrange("p (k n) -> p k n", k=2) for w in (w_hi, w_lo)]

        def part_source(part):
            for layer in range(DEPTH):
                i, n = divmod(part - LAYER_PART[layer], 4)
                if 0 <= i < len(SPLIT_SLOTS):
                    use = USE[(layer, SPLIT_SLOTS[i])]
                    return n, use, proj_weights(use, SPLIT_SLOTS[i])[:, 2 * n:2 * n + 2, :]
            if part < MOE_PART:
                first, use0, slots_in_all = DENSE_PART, USE[("dense", "g", 0)], PER_EXPERT
            else:
                half, slots_in_all = (part - MOE_PART) // (E * FFN_PARTS), E * PER_EXPERT
                first, use0 = first_part(half), MOE_USE + half * slots_in_all
            i, n = divmod(part - first, 4)
            kind = i if i < 2 else 2 if i == slots_in_all - 1 else (i - 2) % 3
            return n, use0 + i, part_view(n, kind, use0 + i)

        def width(name):
            return PROJ[name][1] - PROJ[name][0] if name in PROJ else 512

        def proj_weights(use, name):
            return slot(use)[:, 0:KT * width(name)].rearrange("p (k n) -> p k n", k=KT)

        def part_free(eng, part, shift=0):
            for layer in range(DEPTH):
                i = (part - LAYER_PART[layer]) // 4
                if 0 <= i < len(SPLIT_SLOTS):
                    name = SPLIT_SLOTS[i]
                    key = (layer, name, T - 1) if name in PROJ else (layer, "WO", T - 1, int(name[2]))
                    eng.wait_ge(job_done, JOB[key] + 1)
                    return
            eng.wait_ge(part_used, shift + used_up(part))

        SPLIT_AT = {
            ("X", 0, 1): (0, 3), ("PC", 1): (7, 10), ("PI", 1): (11, 14), ("PK", 1): (15, 18),
            ("PA", 1): (19, 19), **{("O", NI + 10 + i): (20 + i, 20 + i) for i in range(7)}, ("WO", 1, 0): (27, 30)}
        SPLIT_AT = [{**SPLIT_AT, ("PC", 0): (4, 6)}, {**SPLIT_AT, ("N2", 1): (4, 6), ("NF2", 1): (31, 31)}]
        TURNED = {key: i for i, key in enumerate(key for key in JOB if len(key) > 1 and (
            key[1] in ("X", "OT") or key[0:2] == (0, "XF")))}

        ROWS_AT, GATES_AT = 3, 5

        def opening(half):
            return [(j, 1, first_step(half) + j, first_part(half) + 12 * j - 4, 0, True, True) for j in (1, 2)]

        def places(half, e, last):
            found = []
            for i, j in enumerate([*range(3, NCH + 1), 1, 2]):
                if last and j < 3:
                    break
                step = e * NCH + (first_step(half) + 3 + i)
                part = first_part(half) + 32 + 12 * i + (FFN_PARTS * e if last else 0)
                found.append((j, e + (1 if j > 2 else 2), step, part, 0 if last else e * FFN_PARTS,
                              not (last and j == NCH), not last))
            return found

        def dense_turn(j):
            return dense_down[1] if j < NCH else gate_bank

        def first_step(half):
            return DENSE_STEPS if half == 0 else 0

        def bc(ap, shape):
            for _ in range(len(shape) - len(ap.shape)):
                ap = ap.unsqueeze(1)
            return ap.to_broadcast(shape)

        def keys(t):
            return P * (t + 1)

        EXPS = {n: i + 1 for i, n in enumerate(range(NI, NU))}
        NE = NU - NI
        DIFFS = [n for n in range(NU) if UNITS[n][0] == "diff"]
        ROPES = [("kr", 0), ("kr", 1), ("i", 0), ("i", 1), ("a", 0), ("a", 1), ("b", 0), ("b", 1),
                 ("c", 0), ("c", 1)]

        def roped_by(eng, layer, key):
            eng.wait_ge(roped, layer * len(ROPES) + ROPES.index(key) + 1)

        NORMS = [("attn", 0), ("ffn", 0), ("attn", 1), ("ffn", 1), ("final", 1)]

        def norm_count(which, t):
            return NORMS.index(which) * T + t + 1

        FREE = {}
        for layer in range(DEPTH):
            for i, c in enumerate(SPLIT_SLOTS):
                FREE[USE[(layer, c)]] = (lo_done, LAYER_PART[layer] + 4 * i + 4)
            FREE[USE[(layer, "UP")]] = (job_done, JOB[(layer, "KV", 1, 1)] + 1)
        for n in range(PER_EXPERT):
            FREE[USE[("dense", "g", 0)] + n] = (lo_done, DENSE_PART + 4 * n + 4)

        block = ctx.enter_context(nc.Block())

        @block.sync
        def _(sp):
            wg, wu, wd = a["moe_w_gate"], a["moe_w_up"], a["moe_w_down"]

            def column_chunk(w, c0, c1):
                return w[:, c0:c1].rearrange("(k p) n -> p k n", p=P)

            def load(use, view, src, rounds=0):
                sp.dma_start(view, src).then_inc(slot_full[use % RING], 16)

            def freed(use):
                if use in FREE:
                    sp.wait_ge(*FREE[use])

            def wide(use, n, k=KT):
                return slot(use)[:, 0:k * n].rearrange("p (k n) -> p k n", k=k)

            for t in range(T):
                sp.dma_start(h[:, t, :], x[0, t * P:(t + 1) * P, :]).then_inc(loaded_x[t], 16)
            for layer in range(DEPTH):
                for c, (c0, c1) in PROJ.items():
                    use = USE[(layer, c)]
                    freed(use - RING)
                    if (layer, c) == (0, "PI"):
                        sp.wait_ge(loaded_small, 16 * 6)
                    load(use, wide(use, c1 - c0), column_chunk(a["w_in"][layer], c0, c1))
                use = USE[(layer, "UP")]
                freed(use - RING)
                nq, nkv = HC * DC, HC * (DN + DV)
                sp.dma_start(slot(use)[:, 0:2 * nq].rearrange("p (k n) -> p k n", k=2),
                             a["w_uq"][layer].rearrange("(k p) n -> p k n", p=P)) \
                    .then_inc(slot_full[use % RING], 16)
                sp.dma_start(slot(use)[:, 2 * nq:2 * nq + nkv], a["w_ukv"][layer]) \
                    .then_inc(loaded_ukv, 16)
                for half in range(2):
                    use = USE[(layer, f"WO{half}")]
                    freed(use - RING)
                    load(use, wide(use, 512), column_chunk(a["w_out"][layer], 512 * half, 512 * half + 512))
                if layer == 0:
                    for j in range(NCH + 1):
                        for kind, w in (("g", a["dense_w_gate"][0]), ("u", a["dense_w_up"][0])):
                            if j < NCH:
                                use = USE[("dense", kind, j)]
                                freed(use - RING)
                                load(use, wide(use, 512), column_chunk(w, 512 * j, 512 * j + 512))
                        if j:
                            use = USE[("dense", "d", j - 1)]
                            freed(use - RING)
                            load(use, wide(use, D, 4),
                                 a["dense_w_down"][0][512 * (j - 1):512 * j, :]
                                 .rearrange("(k p) n -> p k n", p=P))

            def chunk_at(e, k):
                e, k = e + k // PER_EXPERT, k % PER_EXPERT
                j, kind = k // 3 + 1, k % 3
                if kind == 2:
                    return e, j - 1, 2
                return (e, j, kind) if j < NCH else (e + 1, 0, kind)

            def load_chunk(use, e, j, kind):
                w = (wg, wu, wd)[kind]
                w = w[0, e] if isinstance(e, int) else w[0][bass.ds(e, 1)].rearrange("a k n -> (a k) n")
                if kind < 2:
                    load(use, wide(use, 512), column_chunk(w, 512 * j, 512 * j + 512))
                else:
                    load(use, wide(use, D, 4),
                         w[512 * j:512 * j + 512, :].rearrange("(k p) n -> p k n", p=P))

            def chunk_split(half, n):
                sp.wait_ge(lo_done, n * 4 + (first_part(half) + 4))

            def expert_weights(half):
                first = MOE_USE + half * E * PER_EXPERT
                for i in range(RING + 2):
                    if i >= RING:
                        chunk_split(half, i - RING)
                    elif half == 0:
                        freed(first + i - RING)
                    load_chunk(first + i, *((0, 0, i) if i < 2 else chunk_at(0, i - 2)))
                with sp.Fori(0, E - 1) as e:
                    for k in range(PER_EXPERT):
                        chunk_split(half, e * PER_EXPERT + (2 + k))
                        load_chunk(first + 2 + k + RING, *chunk_at(e, k + RING))
                last = (E - 1) * PER_EXPERT
                for k in range(last + RING, last + PER_EXPERT - 2):
                    chunk_split(half, 2 + k - RING)
                    load_chunk(first + 2 + k, *((E - 1, NCH - 1, 2) if k % PER_EXPERT == 3 * NCH - 3
                                                else chunk_at(0, k)))

            expert_weights(0)
            sp.wait_ge(routed, 1)
            more = sp.value_load(flag[0:1, 0:1])
            with sp.If(more > 0):
                sp.wait_ge(lo_done, first_part(1))
                expert_weights(1)
            for t in range(T):
                sp.wait_ge(out_ready, t + 1)
                sp.dma_start(out[0, t * P:(t + 1) * P, :], hn[:, t, :]).then_inc(stored, 16)
            sp.wait_ge(stored, 16 * T)

        @block.gpsimd
        def _(pool):
            chained = [0]

            def link(ins):
                chained[0] += 1
                ins.then_inc(pool_chain, 1)
                pool.wait_ge(pool_chain, chained[0])

            link(pool.memset(ident[:, :], 0.0))
            link(pool.affine_select(out=ident[:, :], in_=ident[:, :], compare_op=ALU.not_equal, fill=1.0,
                                    base=0, pattern=[[-1, P]], channel_multiplier=1))
            pool.memset(mhalf[:, :], -0.5)
            pool.memset(mask_q[:, 0:CHUNK], 1.0)
            pool.memset(mask_q[:, CHUNK:P], 0.0)
            pool.memset(mask_k[:, :], MASKED)
            link(pool.memset(neg_chunk[:, :], 0.0))
            pool.memset(neg_chunk[0:CHUNK, :], MASKED).then_inc(consts_ready, 1)
            pool.wait_ge(consts_ready, 1)

            def inverse_root(outp, inp, n):
                return pool.tensor_tensor(outp, inp, mhalf[:, 0:n], ALU.pow)

            def norm_root(which, t):
                i = norm_count(which, t)
                pool.wait_ge(mean_ready, i)
                inverse_root(stat[:, i - 1, 0:1], stat[:, i - 1, 1:2], 1).then_inc(rms_ready, 1)

            def rope(v, t, n, half):
                shape = [P, n, 2, half]
                step = NF // half
                c, s = (bc(z[:, t, :].rearrange("p (f s) -> p f s", s=step)[:, :, 0], shape) for z in (cos, sin))
                rc = rope_c[:, 0:2 * n * half].rearrange("p (n a f) -> p n a f", n=n, a=2)
                rs = rope_s[:, 0:2 * n * half].rearrange("p (n a f) -> p n a f", n=n, a=2)
                link(pool.tensor_tensor(rc, v, c, ALU.mult))
                link(pool.tensor_tensor(rs, v, s, ALU.mult))
                link(pool.tensor_tensor(v[:, :, 0, :], rc[:, :, 0, :], rs[:, :, 1, :], ALU.subtract))
                return pool.tensor_tensor(v[:, :, 1, :], rc[:, :, 1, :], rs[:, :, 0, :], ALU.add)

            def halves(v, n, d, half):
                return v.rearrange("p (n d) -> p n d", n=n)[:, :, 0:2 * half] \
                        .rearrange("p n (a f) -> p n a f", a=2)

            rotations = [0]

            def rotated(ins):
                rotations[0] += 1
                ins.then_inc(roped, 1)
                pool.wait_ge(roped, rotations[0])

            for layer in range(DEPTH):
                for t in range(T):
                    norm_root(("attn", layer), t)
                for t in range(T):
                    pool.wait_ge(c_mean, layer * T + t + 1)
                    inverse_root(cstat[:, t, 0, :], cstat[:, t, 1, :], 2).then_inc(c_rms, 1)
                if layer == 0:
                    pool.wait_ge(trig_ready, 2)
                for t in range(T):
                    emptied(pool, (layer, "PC", t))
                    rotated(rope(halves(pc[:, t, CQ + CKV:], 1, DR, DR // 2), t, 1, DR // 2))
                for t in range(T):
                    emptied(pool, (layer, "PI", t))
                    emptied(pool, (layer, "PK", t))
                    link(rope(halves(pqi[:, t, 0:(HI + 1) * DI], HI + 1, DI, DI // 8), t, HI + 1, DI // 8))
                    rotated(pool.tensor_copy(pqi[:, t, (HI + 1) * DI:], pqi[:, t, HI * DI:(HI + 1) * DI]))
                for t in range(T):
                    emptied(pool, (layer, "PA", t))
                    link(rope(halves(pa[:, t, 0:(HA + 1) * DA], HA + 1, DA, DA // 8), t, HA + 1, DA // 8))
                    rotated(pool.tensor_copy(pa[:, t, (HA + 1) * DA:(HA + 2) * DA],
                                             pa[:, t, HA * DA:(HA + 1) * DA]))
                for t in range(T):
                    emptied(pool, (layer, "PK", t))
                    emptied(pool, (layer, "PB", t))
                    rotated(rope(halves(pb[:, t, 0:4 * HB * DB], 4 * HB, DB, DB // 8), t, 4 * HB, DB // 8))
                for t in range(T):
                    for i in range(2):
                        emptied(pool, (layer, "QC", t, i))
                    link(rope(qc[:, :, DN:].rearrange("p n (a f) -> p n a f", a=2), t, HC, DR // 2))
                    for i in range(2):
                        emptied(pool, (layer, "KV", t, i))
                    rotated(pool.tensor_copy(kc[:, :, DN:], bc(pc[:, t, CQ + CKV:], [P, HC, DR])))
                for t in range(T):
                    pool.wait_ge(d_mean, layer * T + t + 1)
                    inverse_root(dstat[:, t, 0, :], dstat[:, t, 1, :], HB).then_inc(d_rms, 1)
                for t in range(T):
                    norm_root(("ffn", layer), t)

            pool.wait_ge(normed, norm_count(("ffn", 1), 0))
            link(pool.memset(before[:, :], 1.0))
            link(pool.affine_select(out=before[:, :], in_=before[:, :], compare_op=ALU.is_gt, fill=0.0,
                               base=0, pattern=[[1, P]], channel_multiplier=-1))
            pool.memset(ones[:, :], 1.0)
            pool.iota(slots, [[P, 2], [1, P]], base=0, channel_multiplier=0,
                      allow_small_or_imprecise_dtypes=True).then_inc(consts_ready, 1)
            for t in range(T):
                norm_root(("final", 1), t)

        @block.tensor
        def _(pe):
            def begin(key):
                n = JOB[key]
                if n >= WBANKS:
                    pe.wait_ge(evacuated[n % WBANKS], n // WBANKS)
                early_job = n - JOB[(1, "X", 0, 0)]
                if 0 <= early_job < WBANKS:
                    pe.wait_ge(dense_added, 4 * (NCH - 1) + (early_job + 1 if early_job < 2 else 0))
                return work[n % WBANKS]

            def transposes(b, blocks, n=P):
                for i, src in enumerate(blocks):
                    last = pe.transpose(b[0:n, i * P:(i + 1) * P], src, ident[:, :])
                return last

            def tile(t):
                return slice(t * P, (t + 1) * P)

            def cols(src, t, i0, n):
                return [src[:, t, (i0 + i) * P:(i0 + i + 1) * P] for i in range(n)]

            def product(b, n, lhs, rhs):
                for k in range(len(rhs)):
                    last = pe.matmul(b[:, 0:n], lhs[k], rhs[k], start=(k == 0), stop=(k == len(rhs) - 1))
                return last

            def wide(use, n):
                v = slot(use)[:, 0:KT * n].rearrange("p (k n) -> p k n", k=KT)
                return [v[:, k, :] for k in range(KT)]

            def part_product(part, k, lhs, b, first, last, n=512):
                w = part_buffers(part, n)
                for kk in range(2):
                    for i, (x_part, w_part) in enumerate(((0, 0), (0, 1), (1, 0))):
                        mm = pe.matmul(b, lhs[x_part][k + kk], w[w_part][:, kk, :],
                                       start=(first and kk == 0 and i == 0), stop=(last and kk == 1 and i == 2))
                return mm

            def part_ready(part, shift=0):
                pe.wait_ge(lo_done, shift + (part + 1))

            hnT_parts = [[[v[:, k, tile(t)] for k in range(KT)] for v in (hnT_hi, hnT_lo)] for t in range(T)]

            def split_product(part, t, b, n):
                for i in range(4):
                    part_ready(part + i)
                    last = part_product(part + i, 2 * i, hnT_parts[t], b[:, 0:n], i == 0, i == 3, n)
                return last

            def transpose_rows(layer, item):
                name, t, i = item
                b = begin((layer, *item))
                if name == "OT":
                    last_o = max(n for n in range(NI, NU) if UNITS[n][1] == t)
                    emptied(pe, (layer, "O", last_o))
                    pe.wait_ge(d_normed, layer * T + t + 1)
                else:
                    pe.wait_ge(normed, norm_count(("attn" if name == "X" else "ffn", layer), t))
                transposes(b, cols(hn, t, 4 * i, 4)).then_inc(job_done, 1)

            def logits(layer, n):
                kind, t, p = UNITS[n]
                S2 = logit_bank[n % 4]
                nk = keys(t)
                if n >= 4:
                    if n - 4 < NI:
                        pe.wait_ge(relu_done, layer * NI + n - 3)
                    else:
                        pe.wait_ge(exp_done, layer * NE + EXPS[n - 4])
                if (kind, p) in (("idx", 0), ("diff", 0), ("mla", 0), ("dsa", 0)):
                    for name in {"idx": ("IT", "KIT"), "diff": ("BT",), "dsa": ("AT",), "mla": ("MQ", "MK")}[kind]:
                        for tt in range(t + 1):
                            for i in (range(2) if kind == "mla" else (None,)):
                                emptied(pe, (layer, name, tt) if i is None else (layer, name, tt, i))
                for m in range(2):
                    if kind == "idx":
                        r = 64 * (p % 2)
                        q, k = qiT[r:r + 64, 2 * (p // 2) + m, tile(t)], kiT[r:r + 64, 0:nk]
                    elif kind == "diff":
                        r = 32 * p
                        q, k = bT[r:r + DB, m, tile(t)], bT[r:r + DB, 2 + m, 0:nk]
                    elif kind == "mla":
                        q, k, r = qcT[0:DC, 2 * p + m, tile(t)], kcT[0:DC, 2 * p + m, 0:nk], 0
                    else:
                        r = 64 * p
                        q, k = aT[r:r + 64, m, tile(t)], aT[r:r + 64, 2, 0:nk]
                    plain = kind in ("idx", "dsa")
                    last = pe.matmul(S2[:, m, 0:nk], q, k, start=True, stop=plain)
                    if not plain:
                        last = pe.matmul(S2[:, m, nk - CHUNK:nk], mask_q[r:r + 1, :], mask_k[r:r + 1, :],
                                         start=False, stop=True)
                last.then_inc(logits_ready, 1)

            def attention(layer):
                for item in ORDER[layer]:
                    name, key = item[0], (layer, *item)
                    if name in ("X", "XF", "OT"):
                        transpose_rows(layer, item)
                    elif name in PROJ:
                        t, n = item[1], width(name)
                        b = begin(key)
                        for i in range(2):
                            emptied(pe, (layer, "X", t, i))
                        split_product(LAYER_PART[layer] + 4 * SPLIT_SLOTS.index(name), t, b, n).then_inc(job_done, 1)
                    elif name == "CT":
                        b = begin(key)
                        pe.wait_ge(c_normed, layer * T + item[1] + 1)
                        transposes(b, cols(pc, item[1], 0, 3)).then_inc(job_done, 1)
                    elif name in ("IT", "KIT", "AT", "BT"):
                        t = item[1]
                        b = begin(key)
                        roped_by(pe, layer, ({"IT": "i", "KIT": "i", "AT": "a", "BT": "b"}[name], t))
                        src, i0, n = {"IT": (pqi, 0, 4), "KIT": (pqi, 4, 1), "AT": (pa, 0, 3), "BT": (pb, 0, 4)}[name]
                        transposes(b, cols(src, t, i0, n)).then_inc(job_done, 1)
                    elif name == "QC":
                        _, t, i = item
                        b, use, n = begin(key), USE[(layer, "UP")], HC * DC // 2
                        arrived(pe, use)
                        emptied(pe, (layer, "CT", t))
                        product(b, n, [cT[:, k, tile(t)] for k in range(2)],
                                [slot(use)[:, k * 2 * n + i * n:k * 2 * n + i * n + n] for k in range(2)]) \
                            .then_inc(job_done, 1)
                    elif name == "KV":
                        _, t, i = item
                        b, at = begin(key), 2 * HC * DC + 512 * i
                        pe.wait_ge(loaded_ukv, 16 * (layer + 1))
                        product(b, 512, [cT[:, 2, tile(t)]], [slot(USE[(layer, "UP")])[:, at:at + 512]]) \
                            .then_inc(job_done, 1)
                    elif name in ("MQ", "MK"):
                        _, t, i = item
                        b = begin(key)
                        roped_by(pe, layer, ("c", t))
                        src = qc if name == "MQ" else kc
                        transposes(b, [src[:, 4 * i + j, :] for j in range(4)], DC).then_inc(job_done, 1)
                    elif name == "U":
                        logits(layer, item[1])
                    elif name == "TP":
                        n = item[1]
                        kind, t, p = UNITS[n]
                        b = begin(key)
                        if kind == "diff":
                            pe.wait_ge(combined, layer * len(DIFFS) + DIFFS.index(n) + 1)
                        else:
                            pe.wait_ge(exp_done, layer * NE + EXPS[n])
                        transposes(b, [prob[:, n % 3, m, tile(kb)] for m in range(1 if kind == "diff" else 2)
                                       for kb in range(t + 1)]).then_inc(job_done, 1)
                    elif name == "O":
                        n = item[1]
                        kind, t, p = UNITS[n]
                        b = begin(key)
                        emptied(pe, (layer, "TP", n))
                        for m in range(1 if kind == "diff" else 2):
                            for kb in range(t + 1):
                                v = {"diff": pb[:, kb, 512 + 64 * p:576 + 64 * p],
                                     "mla": vc[:, kb, DV * (2 * p + m):DV * (2 * p + m + 1)],
                                     "dsa": pa[:, kb, 384:448]}[kind]
                                last = pe.matmul(b[:, 64 * m:64 * m + 64], pt[:, n % 2, m * (t + 1) + kb, :],
                                                 v, start=(kb == 0), stop=(kb == t))
                        last.then_inc(job_done, 1)
                    elif name == "WO":
                        _, t, half = item
                        b = begin(key)
                        for i in range(2):
                            emptied(pe, (layer, "OT", t, i))
                        split_product(LAYER_PART[layer] + 4 * (len(PROJ) + half), t, b, 512).then_inc(job_done, 1)

            def columns(part, shift, operands, banks):
                for i in range(4):
                    part_ready(part + i, shift)
                    for lhs, b in zip(operands, banks):
                        mm = part_product(part + i, 2 * i, lhs, b, i == 0, i == 3)
                    mm.then_inc(part_used, 1)

            def turn(half, step, t, b):
                pe.wait_ge(hid_ready[half], step + 1)
                transposes(b, [hid[:, t, k * P:(k + 1) * P] for k in range(4)]).then_inc(tr_done[half], 1)

            hidT_parts = [[[v[:, t, k, :] for k in range(4)] for v in (hidT_hi, hidT_lo)] for t in range(T)]

            def dense():
                part = DENSE_PART
                for j in range(NCH + 1):
                    if j == 0:
                        for t in range(T):
                            for i in range(2):
                                emptied(pe, (0, "XF", t, i))
                            for i in range(4):
                                part_ready(part + i)
                                mm = part_product(part + i, 2 * i, hnT_parts[t], gate_bank[t], i == 0, i == 3)
                                if t == T - 1:
                                    mm.then_inc(part_used, 1)
                                if (t, i) == (0, 2):
                                    for half in range(2):
                                        transpose_rows(0, ("XF", 1, half))
                        part += 4
                    elif j < NCH:
                        pe.wait_ge(silu_ready[0], T * j)
                        columns(part, 0, hnT_parts, gate_bank)
                        part += 4
                    if j:
                        if 1 < j < NCH:
                            pe.wait_ge(dense_added, 4 * (j - 1))
                        for t in range(T):
                            turn(0, T * (j - 1) + t, t, dense_turn(j)[t])
                    if j < NCH:
                        if j:
                            pe.wait_ge(hid_ready[0], T * j)
                        columns(part, 0, hnT_parts, up_bank)
                        part += 4
                    if j == NCH:
                        pe.wait_ge(dense_added, 4 * (j - 1))
                        for t in range(T):
                            pe.wait_ge(hidT_ready[0], T * (j - 1) + t + 1)
                            for i in range(4):
                                part_ready(part + i)
                                mm = part_product(part + i, 2 * (i % 2), hidT_parts[t], last_down[i // 2][t],
                                                  i % 2 == 0, i % 2 == 1)
                                if t == T - 1:
                                    mm.then_inc(part_used, 1)
                                elif i % 2 == 1:
                                    mm.then_inc(first_tile_down, 1)
                    elif j:
                        pe.wait_ge(hidT_ready[0], T * j)
                        for i in range(4):
                            part_ready(part)
                            for t in range(T):
                                mm = part_product(part, 2 * (i % 2), hidT_parts[t], dense_down[i // 2][t],
                                                  i % 2 == 0, i % 2 == 1)
                            mm.then_inc(part_used, 1)
                            part += 1

            def experts(half):
                s0, part0 = first_step(half), first_part(half)
                lhs = [[v[:, k, :] for k in range(KT)] for v in (xT_hi, xT_lo)]

                def expert_rows(n):
                    pe.wait_ge(sel_ready[half], n)
                    for i in range(2):
                        for k in range(4):
                            for t in range(T):
                                c = (4 * i + k) * P
                                last = pe.matmul(x_bank[i][:, k * P:(k + 1) * P], hn[:, t, c:c + P], sel[:, t, :],
                                                 start=(t == 0), stop=(t == T - 1))
                    last.then_inc(xt_done[half], 1)

                def spread_result(n, t, banks=spread_bank):
                    if t == 0:
                        pe.wait_ge(y_ready[half], n * 2)
                        pe.wait_ge(gselT_ready[half], n)
                    elif banks is spread_bank:
                        pe.wait_ge(added[half], n * 4 - 2)
                    for c in range(2):
                        pe.matmul(banks[t][c], gselT[:, t, :], yrow[:, 512 * c:512 * c + 512], start=True,
                                  stop=True).then_inc(spread_done[half], 1)

                def chunk(j, n, step, part, shift, ahead, more):
                    if j == NCH and more:
                        pe.wait_ge(xT_ready[half], n * 2 + 2)
                    if ahead:
                        pe.wait_ge(silu_ready[half], step)
                        columns(part, shift, [lhs], gate_bank)
                        part += 4
                    turn(half, step - 1, 0, tr_bank)
                    if ahead:
                        pe.wait_ge(hid_ready[half], step)
                        columns(part, shift, [lhs], up_bank)
                        part += 4
                    if j == ROWS_AT and more:
                        expert_rows(n + 1)
                    if j == GATES_AT:
                        pe.wait_ge(gsel_ready[half], n)
                        transposes(sel_bank, [gsel[:, t, :] for t in range(T)]).then_inc(gsel_turned[half], 1)
                    pe.wait_ge(hidT_ready[half], step)
                    for i in range(4):
                        part_ready(part, shift)
                        part_product(part, 2 * (i % 2), hidT_parts[0], down_bank[i // 2],
                                     j == 1 and i % 2 == 0, j == NCH and i % 2 == 1) \
                            .then_inc(part_used, 1)
                        part += 1

                expert_rows(1)
                pe.wait_ge(xT_ready[half], 2)
                columns(part0, 0, [lhs], gate_bank)
                columns(part0 + 4, 0, [lhs], up_bank)
                for j, n, step, part, shift, ahead, more in opening(half):
                    chunk(j, n, step, part, shift, ahead, more)
                with pe.Fori(0, E - 1) as e:
                    for j, n, step, part, shift, ahead, more in places(half, e, False):
                        chunk(j, n, step, part, shift, ahead, more)
                        if j in (1, 2):
                            spread_result(n - 1, j - 1)
                for j, n, step, part, shift, ahead, more in places(half, E - 1, True):
                    chunk(j, n, step, part, shift, ahead, more)
                for t in range(T):
                    spread_result(E, t, last_spread_bank)

            pe.wait_ge(consts_ready, 1)
            attention(0)
            dense()
            attention(1)
            pe.wait_ge(loaded_router, 16)
            for t in range(T):
                if t == 1:
                    for i in range(2):
                        transpose_rows(1, ("XF", 1, i))
                b = begin(("RT", t))
                for i in range(2):
                    emptied(pe, (1, "XF", t, i))
                product(b, E, [hnT[:, k, tile(t)] for k in range(KT)], [router[:, k, :] for k in range(KT)]) \
                    .then_inc(job_done, 1)
            b = begin(("POS",))
            pe.wait_ge(consts_ready, 2)
            pe.wait_ge(chosen_ready, 1)
            pe.matmul(b[:, 0:E], before[:, :], chosen[:, 0, :], start=True, stop=True)
            pe.matmul(b[:, E:2 * E], ones[:, :], chosen[:, 0, :], start=True, stop=False)
            pe.matmul(b[:, E:2 * E], before[:, :], chosen[:, 1, :], start=False, stop=True)
            pe.matmul(b[:, 2 * E:3 * E], ones[:, :], chosen[:, 0, :], start=True, stop=False)
            pe.matmul(b[:, 2 * E:3 * E], ones[:, :], chosen[:, 1, :], start=False, stop=True) \
                .then_inc(job_done, 1)
            experts(0)
            more = pe.value_load(flag[0:1, 0:1])
            with pe.If(more > 0):
                experts(1)

        @block.scalar
        def _(act):
            def copy(o, i):
                return act.activation(o, i, ACT.Copy)

            def row(v, n):
                return v.rearrange("(a n) -> a n", a=1).to_broadcast([P, n])

            def load_gain(v):
                act.dma_start(gain[:, :], row(v, D)).then_inc(loaded_gain, 16)

            def load_layer_gains(layer):
                act.dma_start(cgain[:, 0:CQ], row(a["mla_q_norm"][layer], CQ)).then_inc(loaded_cgain, 16)
                act.dma_start(cgain[:, CQ:], row(a["mla_kv_norm"][layer], CKV)).then_inc(loaded_cgain, 16)
                act.dma_start(sgain[:, :], row(a["diff_subln"][layer], 2 * DB)).then_inc(loaded_cgain, 16)

            def squares(which, t):
                if which == ("attn", 0):
                    act.wait_ge(loaded_x[t], 16)
                else:
                    act.wait_ge(residual_ready, norm_count(which, t) - T)
                act.activation(hn[:, t, :], h[:, t, :], ACT.Square,
                               accum_out=stat[:, norm_count(which, t) - 1, 0:1]).then_inc(squares_ready, 1)

            def split_hi(part, shift=0, rounds=0):
                n, use, raw = part_source(part)
                if n == 0:
                    arrived(act, use, rounds)
                if part >= PARTS:
                    part_free(act, part - PARTS, shift)
                copy(part_buffers(part, raw.shape[2])[0], raw).then_inc(hi_done, 1)

            def turn_evac(key, item):
                b = job(act, key)
                _, t, i = item
                if key in TURNED:
                    copy(hnT_hi[:, 4 * i:4 * i + 4, t * P:(t + 1) * P], b[:, :].rearrange("p (k s) -> p k s", k=4)) \
                        .then_inc(hnT_hi_ready, 1)
                    return
                copy(hnT[:, 4 * i:4 * i + 4, t * P:(t + 1) * P], b[:, :].rearrange("p (k s) -> p k s", k=4)) \
                    .then_inc(out_of(key), 1)

            with nc.allow_non_contiguous_dma(reason="the positions, one to a partition"):
                act.dma_start(pos_i, positions.rearrange("a (t p) -> p (a t)", p=P)).then_inc(loaded_small, 16)
            load_gain(a["attn_norm"][0])
            act.dma_start(freq[:, :], row(a["rope_freq"], NF)).then_inc(loaded_small, 16)
            for i, name in enumerate(("q1", "k1", "q2", "k2")):
                v = a[f"diff_lambda_{name}"]
                act.dma_start(lamv[:, :, i, :], v.unsqueeze(0).to_broadcast([P, DEPTH, DB])).then_inc(loaded_small, 16)
            load_layer_gains(0)

            def attention(layer):
                for item in ORDER[layer]:
                    name, key = item[0], (layer, *item)
                    if name == "N1":
                        squares(("attn", layer), item[1])
                    elif name == "NF1":
                        squares(("ffn", layer), item[1])
                    elif name in ("X", "OT", "XF"):
                        if item[2] == 0 or key in TURNED:
                            turn_evac(key, item)
                        if key == (1, "OT", 1, 1):
                            act.dma_start(router, a["moe_router"][0].rearrange("(k p) e -> p k e", p=P)) \
                                .then_inc(loaded_router, 16)
                    elif name == "PC":
                        t = item[1]
                        b = job(act, key)
                        copy(pc[:, t, :], b[:, 0:416])
                        act.activation(kcT[:, 2 * t, 0:CQ], b[:, 0:CQ], ACT.Square, accum_out=cstat[:, t, 0, 0:1])
                        act.activation(kcT[:, 2 * t + 1, 0:CKV], b[:, CQ:CQ + CKV], ACT.Square,
                                       accum_out=cstat[:, t, 0, 1:2]).then_inc(out_of(key), 1)
                        if (layer, t) == (0, 0):
                            act.wait_ge(angles_ready, 1)
                            act.activation(sin[:, :, :], ang, ACT.Sin).then_inc(trig_ready, 1)
                            act.activation(cos[:, :, :], angc, ACT.Sin).then_inc(trig_ready, 1)
                            act.wait_ge(lam_sums, 1)
                            act.activation(lame, lams, ACT.Exp).then_inc(lam_exp, 1)
                        if t == T - 1:
                            act.wait_ge(normed, norm_count(("attn", layer), t))
                            load_gain(a["ffn_norm"][layer])
                    elif name == "PI":
                        b = job(act, key)
                        copy(pqi[:, item[1], 0:HI * DI], b[:, :]).then_inc(out_of(key), 1)
                    elif name == "PA":
                        b = job(act, key)
                        n = (HA + 1) * DA
                        copy(pa[:, item[1], 0:n], b[:, 0:n])
                        copy(pa[:, item[1], n + DA:n + 2 * DA], b[:, n:n + DA]).then_inc(out_of(key), 1)
                    elif name == "IT":
                        b = job(act, key)
                        t = item[1]
                        copy(qiT[:, :, t * P:(t + 1) * P], b[:, :].rearrange("p (k s) -> p k s", k=4)) \
                            .then_inc(out_of(key), 1)
                    elif name in ("BT", "AT"):
                        t = item[1]
                        b = job(act, key)
                        dst, n, scale = (bT, 4, DB ** -0.5) if name == "BT" else (aT, 3, DA ** -0.5)
                        v = b[:, 0:n * P].rearrange("p (k s) -> p k s", k=n)
                        act.mul(dst[:, 0:2, t * P:(t + 1) * P], v[:, 0:2, :], scale)
                        copy(dst[:, 2:n, t * P:(t + 1) * P], v[:, 2:n, :]).then_inc(out_of(key), 1)
                    elif name == "QC":
                        i = item[2]
                        b = job(act, key)
                        act.mul(qc[:, 4 * i:4 * i + 4, :], b[:, 0:4 * DC].rearrange("p (h d) -> p h d", h=4),
                                DC ** -0.5).then_inc(out_of(key), 1)
                    elif name == "MQ":
                        _, t, i = item
                        b = job(act, key)
                        copy(qcT[0:DC, 4 * i:4 * i + 4, t * P:(t + 1) * P],
                             b[0:DC, :].rearrange("p (k s) -> p k s", k=4)).then_inc(out_of(key), 1)
                    elif name == "U":
                        n = item[1]
                        kind, t, p = UNITS[n]
                        nk = keys(t)
                        if kind == "idx":
                            act.wait_ge(logits_ready, layer * NU + n + 1)
                            if n >= 3:
                                act.wait_ge(index_added, layer * NI + n - 2)
                            act.activation(prob[:, n % 3, :, 0:nk], logit_bank[n % 4][:, :, 0:nk], ACT.Relu) \
                                .then_inc(relu_done, 1)
                        else:
                            act.wait_ge(max_ready, layer * NE + EXPS[n])
                            for m in range(2):
                                src = prob[:, n % 3, m, 0:nk] if kind == "dsa" else logit_bank[n % 4][:, m, 0:nk]
                                last = act.activation(prob[:, n % 3, m, 0:nk], src, ACT.Exp,
                                                      bias=nmax[:, n, m:m + 1], accum_out=lsum[:, n, m:m + 1])
                            last.then_inc(exp_done, 1)
                    elif name == "TP" and UNITS[item[1]][0] != "mla":
                        n = item[1]
                        blocks = (UNITS[n][1] + 1) * (1 if UNITS[n][0] == "diff" else 2)
                        b = job(act, key)
                        copy(pt[:, n % 2, 0:blocks, :], b[:, 0:blocks * P].rearrange("p (k s) -> p k s", k=blocks)) \
                            .then_inc(out_of(key), 1)
                    if item in SPLIT_AT[layer]:
                        first, final = SPLIT_AT[layer][item]
                        for n in range(first, final + 1):
                            split_hi(LAYER_PART[layer] + n)

            def silu(half, step, t, used):
                act.wait_ge(part_used, used)
                before = T if half == 0 and isinstance(step, int) and step < DENSE_STEPS else 1
                if not (isinstance(step, int) and step < before):
                    act.wait_ge(hid_ready[half], step - (before - 1))
                act.activation(sg[:, t, :], gate_bank[t], ACT.Silu).then_inc(silu_ready[half], 1)

            def hidden_turned(half, step, t, b):
                act.wait_ge(tr_done[half], step + 1)
                copy(hidT_hi[:, t, :, :], b.rearrange("p (k s) -> p k s", k=4)).then_inc(hidT_hi_ready[half], 1)

            def dense():
                for n in range(3, PARTS):
                    split_hi(DENSE_PART + n)
                for i in range(2):
                    turn_evac((0, "XF", 1, i), ("XF", 1, i))
                base = DENSE_PART - 4
                for j in range(NCH + 1):
                    at = base + 4 if j == 0 else base

                    def parts(first, last):
                        for n in range(first, last + 1):
                            if at + n < DENSE_PART + FFN_PARTS:
                                split_hi(at + n)

                    if j < NCH:
                        parts(7, 9)
                        for t in range(T):
                            silu(0, T * j + t, t, used_up(at + 3))
                    parts(10, 10) if j < NCH else None
                    if j:
                        for t in range(T):
                            hidden_turned(0, T * (j - 1) + t, t, dense_turn(j)[t])
                    if j < NCH:
                        parts(11, 18 if j else 14)
                    if j == 0:
                        act.wait_ge(normed, norm_count(("ffn", 0), 1))
                        load_gain(a["attn_norm"][1])
                        act.wait_ge(d_normed, T)
                        load_layer_gains(1)
                    base += 12

            def experts(half):
                s0, part0 = first_step(half), first_part(half)

                def rows_taken(n):
                    act.wait_ge(xt_done[half], n)
                    for i in range(2):
                        copy(xT_hi[:, 4 * i:4 * i + 4, :], x_bank[i].rearrange("p (k s) -> p k s", k=4)) \
                            .then_inc(xT_hi_ready[half], 1)

                def chunk(j, n, step, part, shift, ahead, more, rounds):
                    def parts(first, final):
                        for i in range(first, final + 1):
                            if more or part + i < part0 + E * FFN_PARTS:
                                split_hi(part + i, shift, rounds)

                    if ahead:
                        parts(7, 9)
                        silu(half, step, 0, shift + used_up(part + 3))
                        parts(10, 10)
                    hidden_turned(half, step - 1, 0, tr_bank)
                    if ahead:
                        parts(11, 14)
                    if j == GATES_AT:
                        act.wait_ge(gsel_turned[half], n)
                        copy(gselT, sel_bank[:, 0:T * P].rearrange("p (t n) -> p t n", t=T)) \
                            .then_inc(gselT_ready[half], 1)
                    if j == NCH - 1 and more:
                        act.wait_ge(part_used, shift + used_up(part + 7))
                        rows_taken(n + 1)
                    if ahead:
                        parts(15, 17)
                    if j == NCH:
                        act.wait_ge(part_used, shift + used_up(part + (11 if ahead else 3)))
                        for c in range(2 if more else 1):
                            copy(yrow[:, 512 * c:512 * c + 512], down_bank[c]).then_inc(y_ready[half], 1)
                    if ahead:
                        parts(18, 18)

                def start(first, final):
                    for n in range(first, final + 1):
                        split_hi(part0 + n)

                if half == 1:
                    start(0, 6)
                rows_taken(1)
                start(7, 9)
                silu(half, s0, 0, used_up(part0 + 3))
                start(10, 14)
                for place in opening(half):
                    chunk(*place, 0)
                with act.Fori(0, E - 1) as e:
                    for place in places(half, e, False):
                        chunk(*place, 16 * (PER_EXPERT // RING) * e)
                for place in places(half, E - 1, True):
                    chunk(*place, 0)

            attention(0)
            dense()
            attention(1)
            act.wait_ge(normed, norm_count(("ffn", 1), 1))
            load_gain(a["final_norm"])
            turn_evac((1, "XF", 1, 0), ("XF", 1, 0))
            for n in range(4, PARTS):
                split_hi(MOE_PART + n)
            act.wait_ge(gates_in, 1)
            act.activation(lg2, lg, ACT.Exp).then_inc(gates_exp, 1)
            experts(0)
            more = act.value_load(flag[0:1, 0:1])
            with act.If(more > 0):
                experts(1)
            for t in range(T):
                squares(("final", 1), t)

        @block.vector
        def _(dve):
            chained = [0]

            def link(ins):
                chained[0] += 1
                ins.then_inc(dve_chain, 1)
                dve.wait_ge(dve_chain, chained[0])

            def scalar2(o, i, s1, s2, op0, op1):
                return dve.tensor_scalar(o, i, s1, s2, op0, op1)

            def mean(which, t):
                i = norm_count(which, t)
                dve.wait_ge(squares_ready, i)
                scalar2(stat[:, i - 1, 1:2], stat[:, i - 1, 0:1], 1.0 / D, EPS, ALU.mult, ALU.add) \
                    .then_inc(mean_ready, 1)

            def norm(which, t):
                i = norm_count(which, t)
                dve.wait_ge(rms_ready, i)
                if t == 0:
                    dve.wait_ge(loaded_gain, 16 * (NORMS.index(which) + 1))
                return dve.scalar_tensor_tensor(out=hn[:, t, :], in0=h[:, t, :], scalar=stat[:, i - 1, 0:1],
                                                in1=gain[:, :], op0=ALU.mult, op1=ALU.mult)

            def split_lo(part, shift=0):
                _, _, raw = part_source(part)
                hi, lo = part_buffers(part, raw.shape[2])
                dve.wait_ge(hi_done, shift + (part + 1))
                dve.tensor_tensor(lo, raw, hi.bitcast(F32), ALU.subtract).then_inc(lo_done, 1)

            def turn_evac(key, item):
                b = job(dve, key)
                _, t, i = item
                if key in TURNED:
                    dve.wait_ge(hnT_hi_ready, TURNED[key] + 1)
                    half = (slice(None), slice(4 * i, 4 * i + 4), slice(t * P, (t + 1) * P))
                    dve.tensor_tensor(hnT_lo[half], b[:, :].rearrange("p (k s) -> p k s", k=4),
                                      hnT_hi[half].bitcast(F32), ALU.subtract).then_inc(out_of(key), 1)
                    return
                dve.tensor_copy(hnT[:, 4 * i:4 * i + 4, t * P:(t + 1) * P],
                                b[:, :].rearrange("p (k s) -> p k s", k=4)).then_inc(out_of(key), 1)

            def angles():
                dve.wait_ge(loaded_small, 16 * 6)
                link(dve.tensor_copy(pos_f, pos_i))
                for t in range(T):
                    last = dve.tensor_scalar(ang[:, t, :], freq[:, :], pos_f[:, t:t + 1], None, ALU.mult)
                link(last)
                link(scalar2(turns, ang, 1.0 / TWO_PI, ROUND, ALU.mult, ALU.add))
                link(dve.tensor_scalar(turns, turns, ROUND, None, ALU.subtract))
                for part in PI_PARTS:
                    link(dve.scalar_tensor_tensor(out=ang, in0=turns, scalar=-part, in1=ang,
                                                  op0=ALU.mult, op1=ALU.add))
                link(dve.tensor_scalar(angc, ang, math.pi / 2, None, ALU.add))
                link(scalar2(turns, angc, math.pi, -TWO_PI, ALU.is_gt, ALU.mult))
                link(dve.tensor_tensor(angc, angc, turns, ALU.add))
                link(scalar2(angc, angc, 3.1415925, -3.1415925, ALU.min, ALU.max))
                scalar2(ang, ang, 3.1415925, -3.1415925, ALU.min, ALU.max).then_inc(angles_ready, 1)
                link(dve.tensor_tensor(lamp, lamv[:, :, 0:4:2, :], lamv[:, :, 1:4:2, :], ALU.mult))
                dve.tensor_reduce(lams, lamp, AX.X, ALU.add).then_inc(lam_sums, 1)

            def lambdas():
                dve.wait_ge(lam_exp, 1)
                for layer in range(DEPTH):
                    link(dve.tensor_tensor(lam[:, layer:layer + 1], lame[:, layer, 0:1], lame[:, layer, 1:2],
                                           ALU.subtract))
                    link(dve.tensor_scalar(lam[:, layer:layer + 1], lam[:, layer:layer + 1],
                                           LAM_INIT[layer], None, ALU.add))

            def index_unit(layer, n):
                _, t, p = UNITS[n]
                nk = keys(t)
                dve.wait_ge(relu_done, layer * NI + n + 1)
                acc = score[:, t, 0:nk]
                for m in range(2):
                    i = 4 * (p // 2) + 2 * m + p % 2
                    rel = prob[:, n % 3, m, 0:nk]
                    if i == 0:
                        ins = dve.tensor_scalar(acc, rel, wi[:, t, 0:1], None, ALU.mult)
                    else:
                        ins = dve.scalar_tensor_tensor(out=acc, in0=rel, scalar=wi[:, t, i:i + 1], in1=acc,
                                                       op0=ALU.mult, op1=ALU.add)
                    if m == 0:
                        link(ins)
                ins.then_inc(index_added, 1)
                dve.wait_ge(index_added, layer * NI + n + 1)
                if p == IDXP - 1:
                    dve.tensor_scalar(score[:, t, 0:nk - CHUNK], score[:, t, 0:nk - CHUNK], IDX_SCALE, None,
                                      ALU.mult)
                    link(dve.scalar_tensor_tensor(out=score[:, t, nk - CHUNK:nk], in0=score[:, t, nk - CHUNK:nk],
                                                  scalar=IDX_SCALE, in1=neg_chunk[:, :], op0=ALU.mult,
                                                  op1=ALU.add))

            def select_round(t, r):
                v = score[:, t, 0:keys(t)]
                link(dve.max(top8[:, :], v))
                link(dve.match_replace(out=v, in_to_replace=top8[:, :], in_values=v, imm_value=TAKEN))
                if r == TOPK // 8 - 1:
                    link(scalar2(v, v, 0.5 * TAKEN, MASKED, ALU.is_gt, ALU.mult))

            def unit_max(layer, n):
                kind, t, p = UNITS[n]
                nk = keys(t)
                dve.wait_ge(logits_ready, layer * NU + n + 1)
                src = logit_bank[n % 4][:, :, 0:nk]
                if kind == "dsa":
                    dst = prob[:, n % 3, :, 0:nk]
                    link(dve.tensor_tensor(dst, src, bc(score[:, t, 0:nk], [P, 2, nk]), ALU.add))
                    src = dst
                dve.tensor_reduce(nmax[:, n, :], src, AX.X, ALU.max, negate=True).then_inc(max_ready, 1)

            def map_major(o, i):
                return dve.tensor_copy(o.rearrange("p (m h d) -> p h m d", m=2, h=HB),
                                       i.rearrange("p (h m d) -> p h m d", h=HB, m=2))

            def attention(layer):
                rounds = []
                for item in ORDER[layer]:
                    name, key = item[0], (layer, *item)
                    if name == "N1":
                        mean(("attn", layer), item[1])
                    elif name == "N2":
                        norm(("attn", layer), item[1]).then_inc(normed, 1)
                    elif name == "NF1":
                        mean(("ffn", layer), item[1])
                    elif name == "NF2":
                        norm(("ffn", layer), item[1]).then_inc(normed, 1)
                    elif name in ("X", "OT", "XF"):
                        if item[2] == 1 or key in TURNED:
                            turn_evac(key, item)
                    elif name == "PI":
                        t = item[1]
                        emptied(dve, (layer, "PC", t))
                        scalar2(cstat[:, t, 1, 0:1], cstat[:, t, 0, 0:1], 1.0 / CQ, EPS, ALU.mult, ALU.add)
                        scalar2(cstat[:, t, 1, 1:2], cstat[:, t, 0, 1:2], 1.0 / CKV, EPS, ALU.mult, ALU.add) \
                            .then_inc(c_mean, 1)
                    elif name == "PK":
                        t = item[1]
                        b = job(dve, key)
                        dve.tensor_copy(pqi[:, t, HI * DI:(HI + 1) * DI], b[:, 0:DI])
                        dve.tensor_copy(wi[:, t, :], b[:, DI:DI + HI])
                        map_major(pb[:, t, 0:256], b[:, DI + HI:DI + HI + 256]).then_inc(out_of(key), 1)
                    elif name == "C2":
                        t = item[1]
                        if (layer, t) == (0, 0):
                            lambdas()
                        dve.wait_ge(c_rms, layer * T + t + 1)
                        dve.wait_ge(loaded_cgain, 48 * (layer + 1))
                        for i, (c0, c1) in enumerate(((0, CQ), (CQ, CQ + CKV))):
                            last = dve.scalar_tensor_tensor(out=pc[:, t, c0:c1], in0=pc[:, t, c0:c1],
                                                            scalar=cstat[:, t, 0, i:i + 1], in1=cgain[:, c0:c1],
                                                            op0=ALU.mult, op1=ALU.mult)
                        last.then_inc(c_normed, 1)
                        if t == 0:
                            link(dve.tensor_scalar(sgain[:, :], sgain[:, :], 1.0 - LAM_INIT[layer], None, ALU.mult))
                    elif name == "CT":
                        b = job(dve, key)
                        t = item[1]
                        dve.tensor_copy(cT[:, :, t * P:(t + 1) * P], b[:, 0:3 * P].rearrange("p (k s) -> p k s", k=3)) \
                            .then_inc(out_of(key), 1)
                    elif name == "KIT":
                        b = job(dve, key)
                        t = item[1]
                        dve.tensor_copy(kiT[:, t * P:(t + 1) * P], b[:, 0:P]).then_inc(out_of(key), 1)
                    elif name == "PB":
                        b = job(dve, key)
                        map_major(pb[:, item[1], 256:512], b[:, 0:256])
                        dve.tensor_copy(pb[:, item[1], 512:768], b[:, 256:512]).then_inc(out_of(key), 1)
                    elif name == "KV":
                        _, t, i = item
                        b = job(dve, key)
                        v = b[:, :].rearrange("p (h d) -> p h d", h=4)
                        dve.tensor_copy(kc[:, 4 * i:4 * i + 4, 0:DN], v[:, :, 0:DN])
                        dve.tensor_copy(vc[:, t, 4 * i * DV:4 * (i + 1) * DV].rearrange("p (h d) -> p h d", h=4),
                                        v[:, :, DN:]).then_inc(out_of(key), 1)
                    elif name == "MK":
                        _, t, i = item
                        b = job(dve, key)
                        dve.tensor_copy(kcT[0:DC, 4 * i:4 * i + 4, t * P:(t + 1) * P],
                                        b[0:DC, :].rearrange("p (k s) -> p k s", k=4)).then_inc(out_of(key), 1)
                    elif name == "U":
                        n = item[1]
                        if UNITS[n][0] == "idx":
                            index_unit(layer, n)
                            if UNITS[n][2] == IDXP - 1:
                                rounds += [(UNITS[n][1], r) for r in range(TOPK // 8)]
                        else:
                            unit_max(layer, n)
                    elif name == "CB":
                        n = item[1]
                        kind, t, p = UNITS[n]
                        nk = keys(t)
                        dve.wait_ge(exp_done, layer * NE + EXPS[n])
                        link(dve.reciprocal(lsum[:, n, :], lsum[:, n, :]))
                        if kind == "diff":
                            p0, p1 = prob[:, n % 3, 0, 0:nk], prob[:, n % 3, 1, 0:nk]
                            link(scalar2(p1, p1, lsum[:, n, 1:2], lam[:, layer:layer + 1], ALU.mult, ALU.mult))
                            dve.scalar_tensor_tensor(out=p0, in0=p0, scalar=lsum[:, n, 0:1], in1=p1,
                                                     op0=ALU.mult, op1=ALU.subtract).then_inc(combined, 1)
                    elif name == "TP":
                        n = item[1]
                        kind, t, p = UNITS[n]
                        if kind == "mla":
                            b = job(dve, key)
                            blocks = 2 * (t + 1)
                            dve.tensor_copy(pt[:, n % 2, 0:blocks, :],
                                            b[:, 0:blocks * P].rearrange("p (k s) -> p k s", k=blocks)) \
                                .then_inc(out_of(key), 1)
                    elif name == "O":
                        n = item[1]
                        kind, t, p = UNITS[n]
                        b = job(dve, key)
                        if kind == "diff":
                            dve.tensor_copy(hn[:, t, 256 + 64 * p:320 + 64 * p], b[:, 0:64]).then_inc(out_of(key), 1)
                        else:
                            dst = hn[:, t, 512 + 128 * p:640 + 128 * p].rearrange("p (m d) -> p m d", m=2) \
                                if kind == "mla" else \
                                hn[:, t, 0:256].rearrange("p (m q d) -> p m q d", m=2, q=2)[:, :, p, :]
                            dve.tensor_tensor(dst,
                                              b[:, 0:128].rearrange("p (m d) -> p m d", m=2),
                                              lsum[:, n, :].unsqueeze(2).to_broadcast([P, 2, 64]), ALU.mult) \
                                .then_inc(out_of(key), 1)
                    elif name == "D1":
                        t = item[1]
                        o = hn[:, t, 256:512]
                        last_o = max(n for n in DIFFS if UNITS[n][1] == t)
                        emptied(dve, (layer, "O", last_o))
                        link(dve.tensor_tensor(kiT, o, o, ALU.mult))
                        link(dve.tensor_reduce(dstat[:, t, 0, :], kiT.rearrange("p (h d) -> p h d", h=HB), AX.X, ALU.add))
                        scalar2(dstat[:, t, 1, :], dstat[:, t, 0, :], 1.0 / (2 * DB), EPS, ALU.mult, ALU.add) \
                            .then_inc(d_mean, 1)
                    elif name == "D2":
                        t = item[1]
                        o = hn[:, t, 256:512].rearrange("p (h d) -> p h d", h=HB)
                        dve.wait_ge(d_rms, layer * T + t + 1)
                        link(dve.tensor_tensor(o, o, dstat[:, t, 0, :].unsqueeze(2).to_broadcast([P, HB, 2 * DB]),
                                               ALU.mult))
                        dve.tensor_tensor(o, o, bc(sgain[:, :], [P, HB, 2 * DB]), ALU.mult).then_inc(d_normed, 1)
                    elif name == "WO":
                        _, t, half = item
                        b = job(dve, key)
                        v = h[:, t, 512 * half:512 * half + 512]
                        dve.tensor_tensor(v, v, b[:, :], ALU.add).then_inc(out_of(key), 1)
                        if half == 1:
                            emptied(dve, key)
                            dve.sem_inc(residual_ready, 1)
                    elif item == ("PC", 0) and layer == 0:
                        angles()
                    if item in SPLIT_AT[layer]:
                        first, final = SPLIT_AT[layer][item]
                        for n in range(first, final + 1):
                            split_lo(LAYER_PART[layer] + n)
                    if rounds and name in ("TP", "O"):
                        select_round(*rounds.pop(0))
                assert not rounds

            def hidden(half, step, t, used):
                dve.wait_ge(part_used, used)
                dve.wait_ge(silu_ready[half], step + 1)
                dve.tensor_tensor(hid[:, t, :], up_bank[t], sg[:, t, :], ALU.mult).then_inc(hid_ready[half], 1)

            def hidden_turned(half, step, t, b):
                dve.wait_ge(hidT_hi_ready[half], step + 1)
                dve.tensor_tensor(hidT_lo[:, t, :, :], b.rearrange("p (k s) -> p k s", k=4),
                                  hidT_hi[:, t, :, :].bitcast(F32), ALU.subtract).then_inc(hidT_ready[half], 1)

            def dense():
                for n in range(3, PARTS):
                    split_lo(DENSE_PART + n)
                for i in range(2):
                    turn_evac((0, "XF", 1, i), ("XF", 1, i))
                base = DENSE_PART - 4
                for j in range(NCH + 1):
                    at = base + 4 if j == 0 else base

                    def parts(first, last):
                        for n in range(first, last + 1):
                            if j < NCH and at + n < DENSE_PART + FFN_PARTS:
                                split_lo(at + n)

                    def add_down(c, used):
                        dve.wait_ge(part_used, used)
                        for t in range(T):
                            v = h[:, t, 512 * c:512 * c + 512]
                            dve.tensor_tensor(v, v, dense_down[c][t], ALU.add).then_inc(dense_added, 1)

                    down_at = at + (8 if j < NCH else 0)
                    parts(7, 10)
                    if j:
                        for t in range(T):
                            hidden_turned(0, T * (j - 1) + t, t, dense_turn(j)[t])
                    parts(11, 13)
                    if j < NCH:
                        for t in range(T):
                            hidden(0, T * j + t, t, used_up(at + 7))
                    parts(14, 16 if j else 14)
                    if j == NCH:
                        for t in range(T):
                            for c in range(2):
                                if t == 0:
                                    dve.wait_ge(first_tile_down, c + 1)
                                else:
                                    dve.wait_ge(part_used, used_up(down_at + 2 * c + 1))
                                v = h[:, t, 512 * c:512 * c + 512]
                                dve.tensor_tensor(v, v, last_down[c][t], ALU.add).then_inc(dense_added, 1)
                            dve.wait_ge(dense_added, 4 * (NCH - 1) + 2 * (t + 1))
                            dve.sem_inc(residual_ready, 1)
                    elif j:
                        add_down(0, used_up(down_at + 1))
                        parts(17, 18)
                        add_down(1, used_up(down_at + 3))
                    base += 12

            def experts(half):
                s0, part0 = first_step(half), first_part(half)

                def rows_taken(n):
                    for i in range(2):
                        dve.wait_ge(xT_hi_ready[half], 2 * n + (i - 1))
                        dve.tensor_tensor(xT_lo[:, 4 * i:4 * i + 4, :], x_bank[i].rearrange("p (k s) -> p k s", k=4),
                                          xT_hi[:, 4 * i:4 * i + 4, :].bitcast(F32), ALU.subtract) \
                            .then_inc(xT_ready[half], 1)

                def of_expert(table, e):
                    v = table[:, e, :] if isinstance(e, int) else table[:, bass.ds(e, 1), :].rearrange("p a t -> p (a t)")
                    return v.unsqueeze(2).to_broadcast([P, T, P])

                def find_rows(e):
                    return dve.tensor_tensor(sel, of_expert(place, e), bc(slots[:, half, :], [P, T, P]), ALU.is_equal)

                def find_gates(e):
                    link_loop(dve.tensor_tensor(gsel, of_expert(place, e), bc(slots[:, half, :], [P, T, P]), ALU.is_equal),
                              e)
                    dve.tensor_tensor(gsel, gsel, of_expert(share, e), ALU.mult).then_inc(gsel_ready[half], 1)

                def link_loop(ins, e):
                    ins.then_inc(gsel_found[half], 1)
                    dve.wait_ge(gsel_found[half], e + 1)

                def add_result(n, t, banks=spread_bank):
                    for c in range(2):
                        dve.wait_ge(spread_done[half], n * 4 + (2 * t + c - 3))
                        v = h[:, t, 512 * c:512 * c + 512]
                        dve.tensor_tensor(v, v, banks[t][c], ALU.add).then_inc(added[half], 1)

                def chunk(j, n, step, part, shift, ahead, more, e=None):
                    def parts(first, final):
                        for i in range(first, final + 1):
                            if more or part + i < part0 + E * FFN_PARTS:
                                split_lo(part + i, shift)

                    if j == ROWS_AT and more:
                        find_rows(e + 1).then_inc(sel_ready[half], 1)
                    if j == GATES_AT:
                        find_gates(e)
                    if ahead:
                        parts(7, 10)
                    hidden_turned(half, step - 1, 0, tr_bank)
                    if ahead:
                        parts(11, 13)
                        hidden(half, step, 0, shift + used_up(part + 7))
                        parts(14, 14)
                    if j == NCH - 1 and more:
                        rows_taken(n + 1)
                    if ahead:
                        parts(15, 18)
                    if not more and j == NCH:
                        dve.wait_ge(part_used, used_up(part + 3))
                        dve.tensor_copy(yrow[:, 512:], down_bank[1]).then_inc(y_ready[half], 1)

                def start(first, final):
                    for n in range(first, final + 1):
                        split_lo(part0 + n)

                find_rows(0).then_inc(sel_ready[half], 1)
                if half == 0:
                    gates()
                if half == 1:
                    start(0, 6)
                rows_taken(1)
                start(7, 13)
                hidden(half, s0, 0, used_up(part0 + 7))
                start(14, 14)
                for place_ in opening(half):
                    chunk(*place_)
                with dve.Fori(0, E - 1) as e:
                    for place_ in places(half, e, False):
                        chunk(*place_, e)
                        if place_[0] in (1, 2):
                            add_result(place_[1] - 1, place_[0] - 1)
                for place_ in places(half, E - 1, True):
                    chunk(*place_, E - 1)
                for t in range(T):
                    add_result(E, t, last_spread_bank)
                dve.wait_ge(added[half], 4 * E)

            def route():
                for t in range(T):
                    if t == 1:
                        turn_evac((1, "XF", 1, 1), ("XF", 1, 1))
                        for n in range(4, PARTS):
                            split_lo(MOE_PART + n)
                    b = job(dve, ("RT", t))
                    dve.tensor_copy(lg[:, t, :], b[:, 0:E]).then_inc(out_of(("RT", t)), 1)
                emptied(dve, ("RT", 0))
                emptied(dve, ("RT", 1))
                dve.wait_ge(consts_ready, 2)
                for t in range(T):
                    last = dve.max(top[:, t, :], lg[:, t, :])
                link(last)
                link(dve.memset(top[:, :, 2:8], TAKEN))
                for t in range(T):
                    last = dve.match_replace(out=lg2[:, t, :], in_to_replace=top[:, t, :], in_values=lg[:, t, :],
                                             imm_value=TAKEN)
                link(last)
                dve.tensor_scalar(chosen, lg2, 0.5 * TAKEN, None, ALU.is_lt).then_inc(chosen_ready, 1)
                dve.wait_ge(chosen_ready, 1)
                dve.tensor_tensor(lg, lg, top[:, :, 0:1].to_broadcast([P, T, E]), ALU.subtract).then_inc(gates_in, 1)
                b = job(dve, ("POS",))
                link(dve.scalar_tensor_tensor(out=rank[:, 0:T, :], in0=b[:, 0:T * E].rearrange("p (t e) -> p t e", t=T),
                                              scalar=1.0, in1=chosen, op0=ALU.add, op1=ALU.mult))
                link(dve.tensor_scalar(place.rearrange("p e t -> p t e"), rank[:, 0:T, :], -1.0, None, ALU.add))

            def gates():
                b = work[JOB[("POS",)] % WBANKS]
                dve.tensor_copy(rank[:, T, :], b[:, T * E:(T + 1) * E]).then_inc(out_of(("POS",)), 1)
                emptied(dve, ("POS",))
                link(dve.tensor_reduce(most, rank[:, T, :], AX.X, ALU.max))
                link(dve.tensor_scalar(flag, most, P + 0.5, None, ALU.is_gt))
                dve.sem_inc(routed, 1)
                dve.wait_ge(gates_exp, 1)
                link(dve.tensor_tensor(lg2, lg2, chosen, ALU.mult))
                link(dve.tensor_reduce(total, lg2, AX.X, ALU.add))
                link(dve.reciprocal(total, total))
                link(dve.tensor_tensor(share.rearrange("p e t -> p t e"), lg2,
                                       total.unsqueeze(2).to_broadcast([P, T, E]), ALU.mult))

            attention(0)
            dense()
            attention(1)
            route()
            experts(0)
            more = dve.value_load(flag[0:1, 0:1])
            with dve.If(more > 0):
                experts(1)
            for t in range(T):
                dve.sem_inc(residual_ready, 1)
            for t in range(T):
                mean(("final", 1), t)
            for t in range(T):
                norm(("final", 1), t).then_inc(out_ready, 1)


_INS = ("x", "positions", "attn_norm", "w_in", "mla_q_norm", "w_uq", "mla_kv_norm", "w_ukv",
        "diff_lambda_q1", "diff_lambda_k1", "diff_lambda_q2", "diff_lambda_k2", "diff_subln", "w_out",
        "ffn_norm", "dense_w_gate", "dense_w_up", "dense_w_down", "moe_router", "moe_w_gate",
        "moe_w_up", "moe_w_down", "final_norm")


def kernel(**inputs):
    import numpy as np
    import concourse.bacc as bacc
    from concourse.bass_utils import run_bass_kernel_spmd

    nc = bacc.Bacc("TRN2", target_bir_lowering=False, num_devices=1)
    arrays = {n: np.ascontiguousarray(inputs[n]) for n in _INS}
    arrays["rope_freq"] = (THETA ** (-np.arange(16) / 16.0)).astype(np.float32)
    args = {n: nc.dram_tensor(f"in_{n}", v.shape, mybir.dt.from_np(v.dtype), kind="ExternalInput").ap()
            for n, v in arrays.items()}
    out = nc.dram_tensor("out_0", arrays["x"].shape, F32, kind="ExternalOutput").ap()
    hybrid_block(nc, args, out)
    r = run_bass_kernel_spmd(nc, [{f"in_{n}": v for n, v in arrays.items()}], core_ids=[0])
    return r.results[0]["out_0"]
```
